# Optimizing a Trainium2 kernel written in Bass

```python
import jax
import jax.numpy as jnp
from jax import lax
import numpy as np
import math
import jax, jax.numpy as jnp

D_MODEL = 1024
BATCH = 1
SEQ = 256
DEPTH = 2

RMS_EPS = 1e-6
MIX_W = D_MODEL
A_HEADS = 4
A_HEAD_K = 128
A_HEAD_V = MIX_W // 2 // A_HEADS
A_KW = A_HEADS * A_HEAD_K
A_W = A_HEADS * A_HEAD_V
HGRN_CHUNK = 64
B_GROUPS = 4
B_W = MIX_W // 2
B_GROUP_DIM = B_W // B_GROUPS
GMLP_CHUNK = 128
EVEN_IN = 2 * A_KW + 2 * A_W + 2 * B_W
C_HEADS = 4
Q_LORA = 256
KV_LORA = 128
C_NOPE = 128
C_ROPE = 64
C_QK = C_NOPE + C_ROPE
C_V = MIX_W // 2 // C_HEADS
C_W = C_HEADS * C_V
ROPE_THETA = 10000.0
ATTN_Q_BLOCK = 128
D_HEADS = 4
D_HEAD_DIM = MIX_W // 2 // D_HEADS
D_W = D_HEADS * D_HEAD_DIM
MOBA_BLOCK = 256
MOBA_TOPK = 3
MOBA_Q_CHUNK = 64
ODD_IN = Q_LORA + KV_LORA + C_ROPE + 3 * D_W
PEER_HEADS = 8
PEER_N_KEYS = 128
PEER_N_EXPERTS = PEER_N_KEYS * PEER_N_KEYS
PEER_TOPK = 16
PEER_HALF = 128
PEER_QDIM = 2 * PEER_HALF
PEER_CHUNK = 128


def rmsnorm(x, g):
    xf = x.astype(jnp.float32)
    y = xf * lax.rsqrt(jnp.mean(xf * xf, axis=-1, keepdims=True) + RMS_EPS)
    return y.astype(x.dtype) * g

def split_cols(z, sizes):
    cuts = [int(c) for c in np.cumsum(sizes)[:-1]]
    return jnp.split(z, cuts, axis=-1)

def rope(x, positions):
    half = x.shape[-1] // 2
    inv_freq = ROPE_THETA ** (-jnp.arange(half, dtype=jnp.float32) / half)
    ang = positions.astype(jnp.float32)[..., None] * inv_freq
    cos = jnp.cos(ang)[:, :, None, :]
    sin = jnp.sin(ang)[:, :, None, :]
    x1 = x[..., :half].astype(jnp.float32)
    x2 = x[..., half:].astype(jnp.float32)
    return jnp.concatenate([x1 * cos - x2 * sin, x2 * cos + x1 * sin], axis=-1).astype(x.dtype)

def hgrn_lower_bounds(lb_logits):
    p = jax.nn.softmax(lb_logits.astype(jnp.float32), axis=0)
    return jnp.cumsum(p, axis=0)[:DEPTH]

def hgrn2_recurrence(q, k, v, log_f):
    B, S, H, dk = q.shape
    dv = v.shape[-1]
    nc = S // HGRN_CHUNK

    def chunks(t):
        return t.reshape(B, nc, HGRN_CHUNK, H, t.shape[-1]).transpose(1, 0, 3, 2, 4)

    causal = jnp.tril(jnp.ones((HGRN_CHUNK, HGRN_CHUNK), dtype=bool))[:, :, None]

    def step(state, inp):
        qi, ki, vi, gi = inp
        b = jnp.cumsum(gi.astype(jnp.float32), axis=2)
        o_inter = jnp.einsum('bhtk,bhkv->bhtv', qi * jnp.exp(b), state)
        diff = b[:, :, :, None, :] - b[:, :, None, :, :]
        decay = jnp.exp(jnp.where(causal, diff, -jnp.inf))
        scores = jnp.einsum('bhtk,bhsk,bhtsk->bhts', qi, ki, decay)
        o = o_inter + jnp.einsum('bhts,bhsv->bhtv', scores, vi)
        b_last = b[:, :, -1:, :]
        k_dec = ki * jnp.exp(b_last - b)
        state = jnp.exp(b_last[:, :, 0, :])[..., None] * state + jnp.einsum('bhsk,bhsv->bhkv', k_dec, vi)
        return state, o

    state0 = jnp.zeros((B, H, dk, dv), jnp.float32)
    _, o = lax.scan(step, state0, (chunks(q), chunks(k), chunks(v), chunks(log_f)))
    return o.transpose(1, 0, 3, 2, 4).reshape(B, S, H, dv)

def causal_attention(q, k, v, scale):
    B, H, S, dqk = q.shape
    nq = S // ATTN_Q_BLOCK
    qb = q.reshape(B, H, nq, ATTN_Q_BLOCK, dqk).transpose(2, 0, 1, 3, 4)
    k_pos = jnp.arange(S)

    def block(args):
        i, qi = args
        s = jnp.einsum('bhqd,bhkd->bhqk', qi, k).astype(jnp.float32) * scale
        q_pos = i * ATTN_Q_BLOCK + jnp.arange(ATTN_Q_BLOCK)
        s = jnp.where(k_pos[None, :] <= q_pos[:, None], s, -jnp.inf)
        p = jax.nn.softmax(s, axis=-1).astype(v.dtype)
        return jnp.einsum('bhqk,bhkd->bhqd', p, v)

    o = lax.map(block, (jnp.arange(nq), qb))
    return o.transpose(1, 2, 0, 3, 4).reshape(B, H, S, v.shape[-1])

def moba_attention(q, k, v, scale):
    B, H, S, d = q.shape
    nb = -(-S // MOBA_BLOCK)
    sp = nb * MOBA_BLOCK
    pad = ((0, 0), (0, 0), (0, sp - S), (0, 0))
    q, k, v = jnp.pad(q, pad), jnp.pad(k, pad), jnp.pad(v, pad)
    kb = k.reshape(B, H, nb, MOBA_BLOCK, d)
    vb = v.reshape(B, H, nb, MOBA_BLOCK, d)
    k_mean = jnp.mean(kb.astype(jnp.float32), axis=3)
    gate = jnp.einsum('bhsd,bhnd->bhsn', q.astype(jnp.float32), k_mean)
    q_block = jnp.arange(sp) // MOBA_BLOCK
    past = jnp.arange(nb)[None, :] < q_block[:, None]
    gate = jnp.where(past, gate, -jnp.inf)
    topk = min(MOBA_TOPK, nb)
    _, sel = lax.top_k(gate, topk)
    valid = sel < q_block[:, None]
    nqc = sp // MOBA_Q_CHUNK

    def chunks(t):
        return t.reshape(B, H, nqc, MOBA_Q_CHUNK, t.shape[-1]).transpose(2, 0, 1, 3, 4)

    b_idx = jnp.arange(B)[:, None, None, None]
    h_idx = jnp.arange(H)[None, :, None, None]

    def chunk(args):
        i, qi, si, vi_ = args
        k_sel = kb[b_idx, h_idx, si]
        v_sel = vb[b_idx, h_idx, si]
        s_sel = jnp.einsum('bhqd,bhqnkd->bhqnk', qi, k_sel).astype(jnp.float32) * scale
        s_sel = jnp.where(vi_[..., None], s_sel, -jnp.inf).reshape(B, H, MOBA_Q_CHUNK, topk * MOBA_BLOCK)
        j = (i * MOBA_Q_CHUNK) // MOBA_BLOCK
        k_own = lax.dynamic_index_in_dim(kb, j, axis=2, keepdims=False)
        v_own = lax.dynamic_index_in_dim(vb, j, axis=2, keepdims=False)
        s_own = jnp.einsum('bhqd,bhkd->bhqk', qi, k_own).astype(jnp.float32) * scale
        q_pos = i * MOBA_Q_CHUNK + jnp.arange(MOBA_Q_CHUNK)
        k_pos = j * MOBA_BLOCK + jnp.arange(MOBA_BLOCK)
        s_own = jnp.where(k_pos[None, :] <= q_pos[:, None], s_own, -jnp.inf)
        p = jax.nn.softmax(jnp.concatenate([s_sel, s_own], axis=-1), axis=-1).astype(v.dtype)
        p_sel = p[..., :topk * MOBA_BLOCK].reshape(B, H, MOBA_Q_CHUNK, topk, MOBA_BLOCK)
        p_own = p[..., topk * MOBA_BLOCK:]
        return (jnp.einsum('bhqnk,bhqnkd->bhqd', p_sel, v_sel)
                + jnp.einsum('bhqk,bhkd->bhqd', p_own, v_own))

    o = lax.map(chunk, (jnp.arange(nqc), chunks(q), chunks(sel), chunks(valid)))
    return o.transpose(1, 2, 0, 3, 4).reshape(B, H, sp, d)[:, :, :S]

def hgrn_gmlp_mixer(x, lb, norm_mix, w_in, hgrn_out_norm, gmlp_v_norm, gmlp_w_s, gmlp_b_s, w_out):
    B, S, _ = x.shape
    xn = rmsnorm(x, norm_mix)
    q, fg, inp, og, u, v = split_cols(xn @ w_in, [A_KW, A_KW, A_W, A_W, B_W, B_W])
    f = lb + (1.0 - lb) * jax.nn.sigmoid(fg.astype(jnp.float32))
    o = hgrn2_recurrence(q.reshape(B, S, A_HEADS, A_HEAD_K),
                         (1.0 - f).reshape(B, S, A_HEADS, A_HEAD_K),
                         jax.nn.silu(inp).reshape(B, S, A_HEADS, A_HEAD_V),
                         jnp.log(f).reshape(B, S, A_HEADS, A_HEAD_K))
    o = rmsnorm(o.astype(x.dtype), hgrn_out_norm.reshape(A_HEADS, A_HEAD_V))
    out_a = o.reshape(B, S, A_W) * jax.nn.silu(og)
    u = jax.nn.gelu(u)
    v = rmsnorm(jax.nn.gelu(v).reshape(B, S, B_GROUPS, B_GROUP_DIM),
                gmlp_v_norm.reshape(B_GROUPS, B_GROUP_DIM))
    nc = S // GMLP_CHUNK
    w_causal = gmlp_w_s * jnp.tril(jnp.ones((GMLP_CHUNK, GMLP_CHUNK), gmlp_w_s.dtype))
    sv = jnp.einsum('gts,bnsgd->bntgd', w_causal, v.reshape(B, nc, GMLP_CHUNK, B_GROUPS, B_GROUP_DIM))
    sv = sv + gmlp_b_s.T[:, :, None]
    out_b = u * sv.reshape(B, S, B_W)
    return jnp.concatenate([out_a, out_b], axis=-1) @ w_out

def mla_moba_mixer(x, positions, norm_mix, w_in, cq_norm, ckv_norm, w_uq, w_ukv,
                   mla_q_norm, mla_k_norm, moba_q_norm, moba_k_norm, w_out):
    B, S, _ = x.shape
    xn = rmsnorm(x, norm_mix)
    c_q, c_kv, k_pe, q_d, k_d, v_d = split_cols(xn @ w_in, [Q_LORA, KV_LORA, C_ROPE, D_W, D_W, D_W])
    q_c = (rmsnorm(c_q, cq_norm) @ w_uq).reshape(B, S, C_HEADS, C_QK)
    kv_c = (rmsnorm(c_kv, ckv_norm) @ w_ukv).reshape(B, S, C_HEADS, C_NOPE + C_V)
    k_c = jnp.concatenate([kv_c[..., :C_NOPE],
                           jnp.broadcast_to(k_pe[:, :, None, :], (B, S, C_HEADS, C_ROPE))], axis=-1)
    v_c = kv_c[..., C_NOPE:]
    q_c = rmsnorm(q_c, mla_q_norm)
    k_c = rmsnorm(k_c, mla_k_norm)
    q_c = jnp.concatenate([q_c[..., :C_NOPE], rope(q_c[..., C_NOPE:], positions)], axis=-1)
    k_c = jnp.concatenate([k_c[..., :C_NOPE], rope(k_c[..., C_NOPE:], positions)], axis=-1)
    o_c = causal_attention(q_c.transpose(0, 2, 1, 3), k_c.transpose(0, 2, 1, 3),
                           v_c.transpose(0, 2, 1, 3), C_QK ** -0.5)
    out_c = o_c.transpose(0, 2, 1, 3).reshape(B, S, C_W)
    q_d = rmsnorm(q_d.reshape(B, S, D_HEADS, D_HEAD_DIM), moba_q_norm)
    k_d = rmsnorm(k_d.reshape(B, S, D_HEADS, D_HEAD_DIM), moba_k_norm)
    v_d = v_d.reshape(B, S, D_HEADS, D_HEAD_DIM)
    o_d = moba_attention(q_d.transpose(0, 2, 1, 3), k_d.transpose(0, 2, 1, 3),
                         v_d.transpose(0, 2, 1, 3), D_HEAD_DIM ** -0.5)
    out_d = o_d.transpose(0, 2, 1, 3).reshape(B, S, D_W)
    return jnp.concatenate([out_c, out_d], axis=-1) @ w_out

def peer_ffn(x, norm_ffn, w_query, sub_keys, expert_down, expert_up):
    B, S, D = x.shape
    xn = rmsnorm(x, norm_ffn)
    nt = S // PEER_CHUNK
    xc = xn.reshape(B, nt, PEER_CHUNK, D).transpose(1, 0, 2, 3)

    def chunk(xi):
        q = (xi @ w_query).reshape(B, PEER_CHUNK, PEER_HEADS, 2, PEER_HALF)
        s = jnp.einsum('bthpd,hpnd->bthpn', q, sub_keys)
        s1, i1 = lax.top_k(s[..., 0, :], PEER_TOPK)
        s2, i2 = lax.top_k(s[..., 1, :], PEER_TOPK)
        cand = (s1[..., :, None] + s2[..., None, :]).reshape(B, PEER_CHUNK, PEER_HEADS, PEER_TOPK * PEER_TOPK)
        top_s, top_c = lax.top_k(cand, PEER_TOPK)
        idx = (jnp.take_along_axis(i1, top_c // PEER_TOPK, axis=-1) * PEER_N_KEYS
               + jnp.take_along_axis(i2, top_c % PEER_TOPK, axis=-1))
        g = jax.nn.softmax(top_s.astype(jnp.float32), axis=-1)
        u = jnp.take(expert_down, idx, axis=0)
        act = jax.nn.gelu(jnp.einsum('btd,bthkd->bthk', xi, u).astype(jnp.float32))
        v_sel = jnp.take(expert_up, idx, axis=0)
        return jnp.einsum('bthk,bthkd->btd', (g * act).astype(xi.dtype), v_sel)

    out = lax.map(chunk, xc)
    return out.transpose(1, 0, 2, 3).reshape(B, S, D)

def first_inputs(seed: int = 0) -> dict:
    key = jax.random.key(seed)
    ks = iter(jax.random.split(key, 64))

    def nrm(shape, scale):
        return jax.random.normal(next(ks), shape, jnp.float32) * scale

    def gain(n):
        return 1.0 + 0.1 * jax.random.normal(next(ks), (n,), jnp.float32)

    d = D_MODEL
    inp = {}
    inp['x'] = nrm((BATCH, SEQ, d), 1.0)
    inp['positions'] = jnp.broadcast_to(jnp.arange(SEQ, dtype=jnp.int32), (BATCH, SEQ))
    inp['lb_logits'] = nrm((DEPTH + 1, A_KW), 0.5)
    inp['l0_norm_mix'] = gain(d)
    inp['l0_w_in'] = nrm((d, EVEN_IN), d ** -0.5)
    inp['l0_hgrn_out_norm'] = gain(A_W)
    inp['l0_gmlp_v_norm'] = gain(B_W)
    inp['l0_gmlp_w_s'] = nrm((B_GROUPS, GMLP_CHUNK, GMLP_CHUNK), GMLP_CHUNK ** -0.5)
    inp['l0_gmlp_b_s'] = 1.0 + nrm((B_GROUPS, GMLP_CHUNK), 0.1)
    inp['l0_w_out'] = nrm((A_W + B_W, d), (A_W + B_W) ** -0.5)
    inp['l0_norm_ffn'] = gain(d)
    inp['l0_peer_w_query'] = nrm((d, PEER_HEADS * PEER_QDIM), d ** -0.5)
    inp['l0_peer_sub_keys'] = nrm((PEER_HEADS, 2, PEER_N_KEYS, PEER_HALF), PEER_HALF ** -0.5)
    inp['l0_peer_expert_down'] = nrm((PEER_N_EXPERTS, d), d ** -0.5)
    inp['l0_peer_expert_up'] = nrm((PEER_N_EXPERTS, d), 0.25)
    inp['l1_norm_mix'] = gain(d)
    inp['l1_w_in'] = nrm((d, ODD_IN), d ** -0.5)
    inp['l1_mla_cq_norm'] = gain(Q_LORA)
    inp['l1_mla_ckv_norm'] = gain(KV_LORA)
    inp['l1_mla_w_uq'] = nrm((Q_LORA, C_HEADS * C_QK), Q_LORA ** -0.5)
    inp['l1_mla_w_ukv'] = nrm((KV_LORA, C_HEADS * (C_NOPE + C_V)), KV_LORA ** -0.5)
    inp['l1_mla_q_norm'] = gain(C_QK)
    inp['l1_mla_k_norm'] = gain(C_QK)
    inp['l1_moba_q_norm'] = gain(D_HEAD_DIM)
    inp['l1_moba_k_norm'] = gain(D_HEAD_DIM)
    inp['l1_w_out'] = nrm((C_W + D_W, d), (C_W + D_W) ** -0.5)
    inp['l1_norm_ffn'] = gain(d)
    inp['l1_peer_w_query'] = nrm((d, PEER_HEADS * PEER_QDIM), d ** -0.5)
    inp['l1_peer_sub_keys'] = nrm((PEER_HEADS, 2, PEER_N_KEYS, PEER_HALF), PEER_HALF ** -0.5)
    inp['l1_peer_expert_down'] = nrm((PEER_N_EXPERTS, d), d ** -0.5)
    inp['l1_peer_expert_up'] = nrm((PEER_N_EXPERTS, d), 0.25)
    return inp

def first_block(x, positions, lb_logits,
              l0_norm_mix, l0_w_in, l0_hgrn_out_norm, l0_gmlp_v_norm, l0_gmlp_w_s, l0_gmlp_b_s, l0_w_out,
              l0_norm_ffn, l0_peer_w_query, l0_peer_sub_keys, l0_peer_expert_down, l0_peer_expert_up,
              l1_norm_mix, l1_w_in, l1_mla_cq_norm, l1_mla_ckv_norm, l1_mla_w_uq, l1_mla_w_ukv,
              l1_mla_q_norm, l1_mla_k_norm, l1_moba_q_norm, l1_moba_k_norm, l1_w_out,
              l1_norm_ffn, l1_peer_w_query, l1_peer_sub_keys, l1_peer_expert_down, l1_peer_expert_up):
    lbs = hgrn_lower_bounds(lb_logits)
    mixer_params = [
        (lbs[0], l0_norm_mix, l0_w_in, l0_hgrn_out_norm, l0_gmlp_v_norm, l0_gmlp_w_s, l0_gmlp_b_s, l0_w_out),
        (positions, l1_norm_mix, l1_w_in, l1_mla_cq_norm, l1_mla_ckv_norm, l1_mla_w_uq, l1_mla_w_ukv,
         l1_mla_q_norm, l1_mla_k_norm, l1_moba_q_norm, l1_moba_k_norm, l1_w_out),
    ]
    ffn_params = [
        (l0_norm_ffn, l0_peer_w_query, l0_peer_sub_keys, l0_peer_expert_down, l0_peer_expert_up),
        (l1_norm_ffn, l1_peer_w_query, l1_peer_sub_keys, l1_peer_expert_down, l1_peer_expert_up),
    ]
    for layer in range(DEPTH):
        mixer = hgrn_gmlp_mixer if layer % 2 == 0 else mla_moba_mixer
        x = x + mixer(x, *mixer_params[layer])
        x = x + peer_ffn(x, *ffn_params[layer])
    return x


DEPTH_2 = 1

BRANCH_W = D_MODEL // 2
POOL_WINDOWS = (2, 4, 8, 16)
N_POOL_GROUPS = len(POOL_WINDOWS)
POOL_GROUP_W = BRANCH_W // N_POOL_GROUPS
DILATED_GROUPS = ((128, 1), (512, 4), (2048, 16))
N_ATT_GROUPS = len(DILATED_GROUPS)
HEAD_DIM = 64
HEADS_PER_GROUP = BRANCH_W // HEAD_DIM
N_ATT_HEADS = N_ATT_GROUPS * HEADS_PER_GROUP
QKV_W = N_ATT_HEADS * HEAD_DIM
Q_BLOCK = 128
NUM_BUCKETS = 32
MAX_DISTANCE = 1024
IN_W = 2 * BRANCH_W + 3 * QKV_W + BRANCH_W + 2 * D_MODEL
NEG_INF = -1e30


def _rmsnorm(x, g):
    xf = x.astype(jnp.float32)
    r = lax.rsqrt(jnp.mean(xf * xf, axis=-1, keepdims=True) + RMS_EPS)
    return (xf * r).astype(x.dtype) * g

def _t5_bucket(rel):
    nb = NUM_BUCKETS // 2
    ret = (rel > 0).astype(jnp.int32) * nb
    n = jnp.abs(rel)
    max_exact = nb // 2
    nf = jnp.maximum(n, 1).astype(jnp.float32)
    large = max_exact + (jnp.log(nf / max_exact) / math.log(MAX_DISTANCE / max_exact)
                         * (nb - max_exact)).astype(jnp.int32)
    large = jnp.minimum(large, nb - 1)
    return ret + jnp.where(n < max_exact, n, large)

def _multiscale_pool(u, w_pool, pool_scale):
    B, S, _ = u.shape
    ug = u.reshape(B, S, N_POOL_GROUPS, POOL_GROUP_W)
    cs = jnp.cumsum(ug.astype(jnp.float32), axis=1)
    cs = jnp.concatenate([jnp.zeros_like(cs[:, :1]), cs], axis=1)
    pos = jnp.arange(S, dtype=jnp.int32)[:, None]
    half = jnp.array([w // 2 for w in POOL_WINDOWS], dtype=jnp.int32)[None, :]
    lo = jnp.maximum(pos - half, 0)
    hi = jnp.minimum(pos + half - 1, S - 1)
    gidx = jnp.arange(N_POOL_GROUPS, dtype=jnp.int32)[None, :]
    win_sum = cs[:, hi + 1, gidx] - cs[:, lo, gidx]
    count = (hi - lo + 1).astype(jnp.float32)[None, :, :, None]
    pooled = (win_sum / count).astype(u.dtype) - ug
    mixed = jnp.einsum('bsgc,gcd->bsgd', pooled, w_pool)
    return mixed.reshape(B, S, BRANCH_W) * pool_scale

def _dilated_attention(q, k, v, rel_bias):
    B, S = q.shape[0], q.shape[1]
    n_blocks = S // Q_BLOCK
    scale = 1.0 / math.sqrt(HEAD_DIM)
    cfg = []
    for g, (window, dil) in enumerate(DILATED_GROUPS):
        n_side = window // (2 * dil)
        offs = jnp.arange(-n_side, n_side + 1, dtype=jnp.int32) * dil
        bias = rel_bias[_t5_bucket(offs)][:, g * HEADS_PER_GROUP:(g + 1) * HEADS_PER_GROUP]
        cfg.append((offs, bias.T.astype(jnp.float32), k[:, :, g], v[:, :, g]))

    def block(i):
        s0 = i * Q_BLOCK
        qpos = s0 + jnp.arange(Q_BLOCK, dtype=jnp.int32)
        qb = lax.dynamic_slice_in_dim(q, s0, Q_BLOCK, axis=1).astype(jnp.float32) * scale
        lses, outs = [], []
        for g, (offs, bias, kg_all, vg_all) in enumerate(cfg):
            nk = offs.shape[0]
            kpos = qpos[:, None] + offs[None, :]
            valid = (kpos >= 0) & (kpos < S)
            kidx = jnp.clip(kpos, 0, S - 1).reshape(-1)
            kg = jnp.take(kg_all, kidx, axis=1).reshape(B, Q_BLOCK, nk, HEADS_PER_GROUP, HEAD_DIM)
            vg = jnp.take(vg_all, kidx, axis=1).reshape(B, Q_BLOCK, nk, HEADS_PER_GROUP, HEAD_DIM)
            s = jnp.einsum('bqhd,bqkhd->bhqk', qb[:, :, g], kg.astype(jnp.float32))
            s = s + bias[None, :, None, :]
            s = jnp.where(valid[None, None], s, NEG_INF)
            lse = jax.nn.logsumexp(s, axis=-1)
            p = jnp.exp(s - lse[..., None])
            outs.append(jnp.einsum('bhqk,bqkhd->bqhd', p, vg.astype(jnp.float32)))
            lses.append(lse)
        wts = jax.nn.softmax(jnp.stack(lses, axis=0), axis=0)
        wts = jnp.transpose(wts, (0, 1, 3, 2))[..., None]
        out = jnp.sum(wts * jnp.stack(outs, axis=0), axis=0)
        return out.astype(q.dtype)

    o = lax.map(block, jnp.arange(n_blocks, dtype=jnp.int32))
    o = jnp.transpose(o, (1, 0, 2, 3, 4))
    return o.reshape(B, S, HEADS_PER_GROUP * HEAD_DIM)

def second_inputs(seed: int = 0) -> dict:
    key = jax.random.key(seed)
    ks = jax.random.split(key, 12)
    f32 = jnp.float32
    x = jax.random.normal(ks[0], (BATCH, SEQ, D_MODEL), f32)
    norm_gain = 1.0 + 0.05 * jax.random.normal(ks[1], (DEPTH_2, D_MODEL), f32)
    w_in = jax.random.normal(ks[2], (DEPTH_2, D_MODEL, IN_W), f32) * D_MODEL ** -0.5
    b_gate = 0.01 * jax.random.normal(ks[3], (DEPTH_2, 2, D_MODEL), f32)
    rel_bias = 0.5 * jax.random.normal(ks[4], (NUM_BUCKETS, N_ATT_HEADS), f32)
    w_pool = jax.random.normal(ks[5], (DEPTH_2, N_POOL_GROUPS, POOL_GROUP_W, POOL_GROUP_W), f32) * POOL_GROUP_W ** -0.5
    pool_scale = 1.0 + 0.1 * jax.random.normal(ks[6], (DEPTH_2, BRANCH_W), f32)
    w_proj_a = jax.random.normal(ks[7], (DEPTH_2, BRANCH_W, D_MODEL), f32) * BRANCH_W ** -0.5
    w_proj_b = jax.random.normal(ks[8], (DEPTH_2, BRANCH_W, D_MODEL), f32) * BRANCH_W ** -0.5
    w_out = jax.random.normal(ks[9], (DEPTH_2, D_MODEL, D_MODEL), f32) * D_MODEL ** -0.5
    final_gain = 1.0 + 0.05 * jax.random.normal(ks[10], (D_MODEL,), f32)
    return {"x": x, "norm_gain": norm_gain, "w_in": w_in, "b_gate": b_gate,
            "rel_bias": rel_bias, "w_pool": w_pool, "pool_scale": pool_scale,
            "w_proj_a": w_proj_a, "w_proj_b": w_proj_b, "w_out": w_out,
            "final_gain": final_gain}

def second_block(x, norm_gain, w_in, b_gate, rel_bias, w_pool, pool_scale,
              w_proj_a, w_proj_b, w_out, final_gain):
    B, S, D = x.shape
    splits = np.cumsum([BRANCH_W, BRANCH_W, QKV_W, QKV_W, QKV_W, BRANCH_W]).tolist()
    for l in range(DEPTH_2):
        h = _rmsnorm(x, norm_gain[l])
        z = h @ w_in[l]
        a_in, a_gate, q, k, v, b_gp, g_logits = jnp.split(z, splits, axis=-1)
        y_a = (_multiscale_pool(a_in, w_pool[l], pool_scale[l]) * jax.nn.silu(a_gate)) @ w_proj_a[l]
        shp = (B, S, N_ATT_GROUPS, HEADS_PER_GROUP, HEAD_DIM)
        att = _dilated_attention(q.reshape(shp), k.reshape(shp), v.reshape(shp), rel_bias)
        y_b = (att * jax.nn.silu(b_gp)) @ w_proj_b[l]
        gates = jax.nn.sigmoid(g_logits.reshape(B, S, 2, D) + b_gate[l])
        merged = gates[:, :, 0] * y_a + gates[:, :, 1] * y_b
        x = x + merged @ w_out[l]
    return _rmsnorm(x, final_gain)


def setup_inputs(seed=0):
    out = dict(first_inputs(seed))
    for name, value in second_inputs(seed + 1).items():
        if name != "x":
            out[name + "_2"] = value
    return out


def reference(
    x, positions, lb_logits, l0_norm_mix, l0_w_in, l0_hgrn_out_norm, l0_gmlp_v_norm,
    l0_gmlp_w_s, l0_gmlp_b_s, l0_w_out, l0_norm_ffn, l0_peer_w_query, l0_peer_sub_keys,
    l0_peer_expert_down, l0_peer_expert_up, l1_norm_mix, l1_w_in, l1_mla_cq_norm,
    l1_mla_ckv_norm, l1_mla_w_uq, l1_mla_w_ukv, l1_mla_q_norm, l1_mla_k_norm, l1_moba_q_norm,
    l1_moba_k_norm, l1_w_out, l1_norm_ffn, l1_peer_w_query, l1_peer_sub_keys,
    l1_peer_expert_down, l1_peer_expert_up, norm_gain_2, w_in_2, b_gate_2, rel_bias_2, w_pool_2,
    pool_scale_2, w_proj_a_2, w_proj_b_2, w_out_2, final_gain_2,
):
    x = first_block(
        x, positions, lb_logits, l0_norm_mix, l0_w_in, l0_hgrn_out_norm, l0_gmlp_v_norm,
        l0_gmlp_w_s, l0_gmlp_b_s, l0_w_out, l0_norm_ffn, l0_peer_w_query, l0_peer_sub_keys,
        l0_peer_expert_down, l0_peer_expert_up, l1_norm_mix, l1_w_in, l1_mla_cq_norm,
        l1_mla_ckv_norm, l1_mla_w_uq, l1_mla_w_ukv, l1_mla_q_norm, l1_mla_k_norm,
        l1_moba_q_norm, l1_moba_k_norm, l1_w_out, l1_norm_ffn, l1_peer_w_query,
        l1_peer_sub_keys, l1_peer_expert_down, l1_peer_expert_up,
    )
    return second_block(
        x, norm_gain_2, w_in_2, b_gate_2, rel_bias_2, w_pool_2, pool_scale_2, w_proj_a_2,
        w_proj_b_2, w_out_2, final_gain_2,
    )


_drawn_inputs = setup_inputs


def setup_inputs(seed=0):
    import zlib

    import numpy as np

    out = dict(_drawn_inputs(seed))
    spreads = {}
    factors = {'l1_mla_cq_norm': 3.582,
     'l1_mla_q_norm': 3.882,
     'l1_mla_k_norm': 3.532,
     'l1_moba_q_norm': 4.397,
     'l1_moba_k_norm': 3.738,
     'norm_gain_2': 3.429,
     'b_gate_2': 26.759,
     'rel_bias_2': 4.169,
     'pool_scale_2': 2.744}
    for name, (base, spread) in spreads.items():
        noise = np.random.default_rng([zlib.crc32(name.encode()), seed]).standard_normal(out[name].shape)
        drawn = base * np.exp(spread * noise) if base else spread * noise
        out[name] = jnp.asarray(drawn.astype(out[name].dtype))
    for name, factor in factors.items():
        out[name] = (out[name] * factor).astype(out[name].dtype)
    return out
```

```python
from contextlib import ExitStack

import numpy as np

import concourse.bass as bass
from concourse import mybir

ALU = mybir.AluOpType
ACT = mybir.ActivationFunctionType
AX = mybir.AxisListType.X
F32 = mybir.dt.float32
U32 = mybir.dt.uint32
I32 = mybir.dt.int32

NS = 4
SLOT = 2048
NBIG = -1.0e30
FILL = -3.0e38
SEL_AT = (10, 20)
EPS = 1e-6

PV_MIX0, PV_FFN0, PV_MIX1, PV_FFN1, PV_MIX2, PV_CQ, PV_CKV, PV_LB, PV_BS, PV_PS, PV_N = (
    0, 8, 16, 24, 32, 40, 42, 43, 55, 59, 63)
RW_HG, RW_GV, RW_MQ, RW_MK, RW_OQ, RW_OK, RW_BG, RW_FG, RW_N = (
    0, 512, 1024, 1216, 1408, 1536, 1664, 3712, 4736)
C_ID, C_IOTA, C_ONE, C_N0 = 0, 128, 256, 384
CA_LV, CA_TRI, CA_N = 0, 1024, 1152
CB_M, CB_INV, CB_N = 0, 384, 416
CC_PG, CC_N = 0, 2048
CD_OH, CD_NG, CD_N = 0, 512, 1024


class Program:

    def __init__(self, nc, ctx):
        self.nc, self.ctx = nc, ctx
        self.q = {k: [] for k in "VAGTS"}
        self.sem = {k: ctx.enter_context(nc.semaphore(f"done_{n}")) for k, n in
                    zip("VAGT", ("vector", "scalar", "gpsimd", "tensor"))}
        self.count = dict.fromkeys("VAGT", 0)
        self.ndma = 0

    def last(self, k):
        return (self.sem[k], self.count[k])

    def op(self, k, fn, *waits):
        own = [self.last(k)] if self.count[k] else []
        self.count[k] += 1
        self.q[k].append((own + [w for w in waits if w], fn, self.sem[k], 1))
        return self.last(k)

    def mm(self, fn, *waits, mark=False):
        if mark:
            self.count["T"] += 1
        self.q["T"].append(([w for w in waits if w], fn, self.sem["T"] if mark else None, 1))
        return self.last("T")

    def dma(self, out, in_, *waits, sem=None, value=16, k="S"):
        if sem is None:
            sem = self.ctx.enter_context(self.nc.semaphore(f"dma{self.ndma}"))
            self.ndma += 1
        self.q[k].append(([w for w in waits if w], lambda e: e.dma_start(out, in_), sem, 16))
        return (sem, value)

    def wait(self, k, *waits):
        self.q[k].append(([w for w in waits if w], None, None, 0))

    def emit(self, k, eng):
        seen = {}
        for waits, fn, sem, inc in self.q[k]:
            for s, v in waits:
                if v and seen.get(s.name, 0) < v:
                    eng.wait_ge(s, v)
                    seen[s.name] = v
            if fn is not None:
                ins = fn(eng)
                if sem is not None:
                    ins.then_inc(sem, inc)


def build(nc, d, out, upto=9):
    ctx = ExitStack()
    with ctx:
        def sb(name, shape, dt=F32):
            return ctx.enter_context(nc.sbuf_tensor(name, shape, dt))

        P = Program(nc, ctx)
        op, mm, dma = P.op, P.mm, P.dma

        X = sb("X", [128, 2, 1024])
        XNT = sb("XNT", [128, 8, 256])
        ring = sb("ring", [128, NS, SLOT])
        AR = sb("arena", [128, 32768])
        CST = sb("cst", [128, C_N0])
        PVT = sb("pvt", [128, PV_N])
        IT = sb("it", [128, 3, 256])
        SM = sb("sm", [128, 128])
        PS = ctx.enter_context(nc.psum_tensor("ps", [128, 8, 512], F32))
        scr = nc.dram_tensor("scr_rel", [24, 512], F32, kind="Internal")
        ident = CST[:, C_ID:C_ID + 128]
        iota = CST[:, C_IOTA:C_IOTA + 128]
        ones = CST[:, C_ONE:C_ONE + 128]

        def ar(off, *shape):
            n = int(np.prod(shape))
            assert off + n <= 32768
            v = AR[:, off:off + n]
            if len(shape) == 2:
                v = v.rearrange("p (a b) -> p a b", b=shape[1])
            if len(shape) == 3:
                v = v.rearrange("p (a b c) -> p a b c", b=shape[1], c=shape[2])
            return v

        free = [[] for _ in range(8)]
        turn = [0]
        allowed = [list(range(8))]

        def bank():
            b = allowed[0][turn[0] % len(allowed[0])]
            turn[0] += 1
            return b, free[b]

        ring_sem = [ctx.enter_context(nc.semaphore(f"ring{i}")) for i in range(NS)]
        ring_n = [0]
        ring_free = [None] * NS

        def load(src):
            s = ring_n[0] % NS
            ring_n[0] += 1
            n = src.shape[-1]
            tok = dma(ring[:, s, 0:n], src, ring_free[s], sem=ring_sem[s], value=16 * ((ring_n[0] - 1) // NS + 1))
            return s, ring[:, s, 0:n], tok

        def everything():
            return [P.last(k) for k in "VAGT"]

        parity = [0]

        def turn_engine():
            parity[0] ^= 1
            return "VA"[parity[0]]

        def evac(out_, in_, *waits, scale=None, eng=None):
            k = eng or turn_engine()
            if k == "V":
                if scale is None:
                    return op("V", lambda e: e.tensor_copy(out_, in_), *waits)
                return op("V", lambda e: e.tensor_scalar(out_, in_, scale, None, ALU.mult), *waits)
            if scale is None:
                return op("A", lambda e: e.activation(out_, in_, ACT.Copy), *waits)
            return op("A", lambda e: e.activation(out_, in_, ACT.Copy, scale=scale), *waits)

        def tt(out_, a, b, o, *waits, k="V"):
            return op(k, lambda e: e.tensor_tensor(out_, a, b, o), *waits)

        def ts(out_, a, s1, s2, o1, o2=None, *waits, k="V"):
            if o2 is None:
                return op(k, lambda e: e.tensor_scalar(out_, a, s1, None, o1), *waits)
            return op(k, lambda e: e.tensor_scalar(out_, a, s1, s2, o1, o2), *waits)

        def stt(out_, a, s, b, o1, o2, *waits):
            return op("V", lambda e: e.scalar_tensor_tensor(out=out_, in0=a, scalar=s, in1=b, op0=o1, op1=o2), *waits)

        def act(out_, in_, f, *waits, **kw):
            return op("A", lambda e: e.activation(out_, in_, f, **kw), *waits)

        def cp(out_, in_, *waits, k="V"):
            return op(k, lambda e: e.tensor_copy(out_, in_), *waits)

        def rstd(v, n, *waits):
            ts(v, v, 1.0 / n, EPS, ALU.mult, ALU.add, *waits)
            ta = act(v, v, ACT.Sqrt, P.last("V"))
            return op("V", lambda e: e.reciprocal(v, v), ta)

        def transposed(dst, src, src_tok, gain=None, nk=8):
            toks = []
            for kp in range(0, nk, 2):
                b, w = bank()
                n = min(2, nk - kp)
                for j in range(n):
                    for t in range(2):
                        last = j == n - 1 and t == 1
                        tok = mm(lambda e, b=b, j=j, t=t, kp=kp: e.transpose(
                            PS[:, b, j * 256 + t * 128:j * 256 + t * 128 + 128], src(t, kp + j), ident),
                            *w, *src_tok, mark=last)
                who = turn_engine()
                for j in range(n):
                    r = evac(dst(kp + j), PS[:, b, j * 256:j * 256 + 256], tok,
                             scale=gain(kp + j) if gain else None, eng=who)
                free[b] = [r]
                toks.append(r)
            return toks

        SCR = 30720

        def norm_T(gcol, arena_free):
            xs = ar(SCR, 2, 1024)
            for t in range(2):
                act(xs[:, t, :], X[:, t, :], ACT.Square, *arena_free, accum_out=SM[:, t:t + 1])
            r = rstd(SM[:, 0:2], 1024, P.last("A"), *arena_free)
            for t in range(2):
                x_tok = ts(xs[:, t, :], X[:, t, :], SM[:, t:t + 1], None, ALU.mult, None, r)
            return transposed(lambda k: XNT[:, k, :], lambda t, k: xs[:, t, k * 128:k * 128 + 128], [x_tok],
                              gain=lambda k: PVT[:, gcol + k:gcol + k + 1])

        def proj_nat(w, src, src_tok, nk, chunks, use):
            for c in chunks:
                s, wv, wt = load(w[c])
                n = SLOT // nk if w.shape[2] == SLOT else w.shape[2] // nk
                halves = [bank()] if n <= 256 else [bank(), bank()]
                for t in range(2):
                    b, wb = halves[t % len(halves)]
                    o = PS[:, b, (t * n if n <= 256 else 0):(t * n if n <= 256 else 0) + n]
                    for k in range(nk):
                        tok = mm(lambda e, o=o, t=t, k=k, n=n, wv=wv: e.matmul(
                            o, src(k)[:, t * 128:t * 128 + 128], wv[:, k * n:k * n + n],
                            start=(k == 0), stop=(k == nk - 1)), wt, *wb, *src_tok, mark=(k == nk - 1))
                ring_free[s] = tok
                if n <= 256:
                    b = halves[0][0]
                    free[b] = [use(c, PS[:, b, 0:2 * n].rearrange("p (t n) -> p t n", t=2), tok)]
                else:
                    for t in range(2):
                        b = halves[t][0]
                        free[b] = [use(c, t, PS[:, b, 0:n], tok)]

        def proj_T(w, src, src_tok, nk, chunks, use):
            for c in chunks:
                s, wv, wt = load(w[c])
                n = w.shape[2] // nk
                for nb in range(0, n // 128, 2):
                    b, wb = bank()
                    for j in range(2):
                        for k in range(nk):
                            tok = mm(lambda e, b=b, j=j, k=k, nb=nb, wv=wv: e.matmul(
                                PS[:, b, j * 256:j * 256 + 256],
                                wv[:, k * n + (nb + j) * 128:k * n + (nb + j) * 128 + 128], src(k),
                                start=(k == 0), stop=(k == nk - 1)), wt, *wb, *src_tok,
                                mark=(k == nk - 1 and j == 1))
                    free[b] = [use(c * (n // 128) + nb, PS[:, b, :].rearrange("p (j t) -> p j t", j=2), tok)]
                ring_free[s] = tok

        def xnt(k):
            return XNT[:, k, :]

        def add_x(c, ps, tok):
            n = ps.shape[2]
            return tt(X[:, :, c * n:c * n + n], X[:, :, c * n:c * n + n], ps, ALU.add, tok)

        def out_proj(w, mt, mt_tok):
            proj_nat(w, lambda k: mt[:, k, :], mt_tok, 8, range(4), add_x)

        c_tok = dma(CST[:, :], d["cst"])
        p_tok = dma(PVT[:, :], d["pv"])
        x_tok = dma(X[:, :, :], d["x"].rearrange("(t p) c -> p t c", p=128))
        P.wait("V", c_tok, p_tok, x_tok)
        P.wait("A", c_tok, p_tok, x_tok)
        P.wait("G", c_tok, p_tok, x_tok)
        P.wait("T", c_tok)

        def mixer0():
            Q, F, K, B = ar(0, 4, 256), ar(1024, 4, 256), ar(2048, 4, 256), ar(3072, 4, 256)
            E = [ar(4096, 8, 128), ar(5120, 8, 128)]
            SC, SC2 = ar(6144, 8, 128), ar(7168, 4, 128)
            CA = ar(7680, CA_N)
            VN, OG, U, VG = ar(8832, 2, 512), ar(9856, 2, 512), ar(10880, 2, 512), ar(11904, 2, 512)
            HG, GV = ar(12928, 512), ar(13440, 512)
            GW = ar(13952, 4, 128)
            OC = ar(14464, 2, 1024)
            MT = ar(16512, 8, 256)
            TMP = ar(18560, 2, 512)
            LB = ar(19584, 8, 4)

            ca_tok = dma(CA, d["ca"])
            hg_tok = dma(HG, d["rows"][0:1, RW_HG:RW_HG + 512].to_broadcast([128, 512]))
            gv_tok = dma(GV, d["rows"][0:1, RW_GV:RW_GV + 512].to_broadcast([128, 512]))
            gw_tok = dma(GW, d["gw"].rearrange("p (g t) -> p g t", g=4))
            xn = norm_T(PV_MIX0, [])

            L = PVT[:, PV_LB:PV_LB + 12].rearrange("p (r h) -> p r h", r=3)
            m = LB[:, 0, :]
            tt(m, L[:, 0, :], L[:, 1, :], ALU.max)
            tt(m, m, L[:, 2, :], ALU.max)
            tt(LB[:, 1:4, :], L, m.unsqueeze(1).to_broadcast([128, 3, 4]), ALU.subtract)
            ea = act(LB[:, 1:4, :], LB[:, 1:4, :], ACT.Exp, P.last("V"))
            tt(m, LB[:, 1, :], LB[:, 2, :], ALU.add, ea)
            tt(m, m, LB[:, 3, :], ALU.add)
            op("V", lambda e: e.reciprocal(m, m))
            lb, oml = LB[:, 4, :], LB[:, 5, :]
            tt(lb, LB[:, 1, :], m, ALU.mult)
            ts(oml, lb, -1.0, 1.0, ALU.mult, ALU.add)

            def use_qf(blk, ps, tok):
                if blk < 4:
                    return evac(Q[:, blk:blk + 2, :], ps, tok)
                return act(F[:, blk - 4:blk - 2, :], ps, ACT.Sigmoid, tok)
            proj_T(d["l0_win"], xnt, xn, 8, range(4), use_qf)
            sig = P.last("A")
            for h in range(4):
                f_tok = ts(F[:, h, :], F[:, h, :], oml[:, h:h + 1], lb[:, h:h + 1], ALU.mult, ALU.add, sig)
            k_tok = ts(K, F, -1.0, 1.0, ALU.mult, ALU.add)
            g_tok = act(F, F, ACT.Ln, k_tok)
            F8, B8, Q8, K8 = (v.rearrange("p h (t s) -> p (h t) s", t=2) for v in (F, B, Q, K))
            for i in range(8):
                op("V", lambda e, i=i: e.tensor_tensor_scan(B8[:, i, :], ones, F8[:, i, :], 0.0,
                                                            ALU.mult, ALU.add), g_tok)

            op("V", lambda e: e.memset(SC, 0.0))
            masks = CA[:, CA_LV:CA_LV + 1024].bitcast(U32)
            e_read = [None, None]
            for lv in range(8):
                Eb = E[lv % 2]
                if lv == 0:
                    lhs, rhs, e_tok = K8, Q8, P.last("V")
                    q_tok = P.last("A")
                else:
                    size, half = 1 << lv, 1 << (lv - 1)
                    Bv, Ev, Qv, Kv = (v.rearrange("p s (b w i) -> p (s b) w i", w=2, i=half)
                                      for v in (B8, Eb, Q8, K8))
                    mid = Bv[:, :, 0, half - 1:half]
                    n = 1024 // size
                    mid = mid.to_broadcast([128, n, half])
                    tt(Ev[:, :, 1, :], Bv[:, :, 1, :], mid, ALU.subtract, e_read[lv % 2])
                    tt(Ev[:, :, 0, :], mid, Bv[:, :, 0, :], ALU.subtract)
                    x_ = act(Eb, Eb, ACT.Exp, P.last("V"))
                    tt(Ev[:, :, 1, :], Ev[:, :, 1, :], Qv[:, :, 1, :], ALU.mult, x_)
                    e_tok = tt(Ev[:, :, 0, :], Ev[:, :, 0, :], Kv[:, :, 0, :], ALU.mult)
                    lhs = rhs = Eb
                    q_tok = None
                for half8 in range(2):
                    b, wb = bank()
                    for i in range(4):
                        s_tok = mm(lambda e, b=b, i=i, lhs=lhs, rhs=rhs, half8=half8: e.matmul(
                            PS[:, b, i * 128:i * 128 + 128], lhs[:, half8 * 4 + i, :], rhs[:, half8 * 4 + i, :],
                            start=True, stop=True), e_tok, q_tok, *wb, mark=(i == 3))
                    mk = masks[:, lv * 128:lv * 128 + 128].unsqueeze(1).to_broadcast([128, 4, 128])
                    free[b] = [op("V", lambda e, b=b, mk=mk, half8=half8: e.copy_predicated(
                        SC[:, half8 * 4:half8 * 4 + 4, :], mk,
                        PS[:, b, :].rearrange("p (i t) -> p i t", i=4)), s_tok, ca_tok)]
                e_read[lv % 2] = s_tok
            Eb = E[0].rearrange("p (h t) s -> p h t s", t=2)
            Bh, Qh, Kh = (v.rearrange("p h (t s) -> p h t s", t=2) for v in (B, Q, K))
            cp(Eb[:, :, 1, :], Bh[:, :, 1, :], e_read[0])
            tt(Eb[:, :, 0, :], Bh[:, :, 0, 127:128].to_broadcast([128, 4, 128]), Bh[:, :, 0, :], ALU.subtract)
            x_ = act(E[0], E[0], ACT.Exp, P.last("V"))
            tt(Eb[:, :, 1, :], Eb[:, :, 1, :], Qh[:, :, 1, :], ALU.mult, x_)
            e_tok = tt(Eb[:, :, 0, :], Eb[:, :, 0, :], Kh[:, :, 0, :], ALU.mult)
            b, wb = bank()
            for h in range(4):
                s_tok = mm(lambda e, h=h, b=b: e.matmul(PS[:, b, h * 128:h * 128 + 128], Eb[:, h, 0, :], Eb[:, h, 1, :],
                                                        start=True, stop=True), e_tok, *wb, mark=(h == 3))
            sc_tok = cp(SC2, PS[:, b, :].rearrange("p (h t) -> p h t", h=4), s_tok)
            free[b] = [sc_tok]

            def use_rest(c, ps, tok):
                dst, f, o = ((VN, ACT.Silu, 4), (OG, ACT.Silu, 6), (U, ACT.Gelu_apprx_tanh, 8),
                             (VG, ACT.Gelu_apprx_tanh, 10))[(c - 4) // 2]
                return act(dst[:, :, (c - o) * 256:(c - o) * 256 + 256], ps, f, tok)
            proj_nat(d["l0_win"], xnt, xn, 8, range(4, 12), use_rest)
            rest = P.last("A")

            for t in range(2):
                b, wb = bank()
                for h in range(4):
                    o = PS[:, b, h * 128:h * 128 + 128]
                    tok = mm(lambda e, h=h, t=t, o=o: e.matmul(
                        o, SC[:, 2 * h + t, :], VN[:, t, h * 128:h * 128 + 128], start=True, stop=(t == 0)),
                        sc_tok, rest, *wb, mark=True)
                    if t == 1:
                        tok = mm(lambda e, h=h, o=o: e.matmul(
                            o, SC2[:, h, :], VN[:, 0, h * 128:h * 128 + 128], start=False, stop=True), mark=True)
                free[b] = [cp(OC[:, t, 0:512], PS[:, b, :], tok)]
            o4 = OC[:, :, 0:512].rearrange("p t (h v) -> p t h v", h=4)
            tmp4 = TMP.rearrange("p t (h v) -> p t h v", h=4)

            def group_norm(dst, src, gain, *waits):
                ss = SM[:, 8:16].rearrange("p (t h) -> p t h", t=2)
                tt(tmp4, src, src, ALU.mult, *waits)
                op("V", lambda e: e.tensor_reduce(ss, tmp4, AX, ALU.add))
                rstd(SM[:, 8:16], 128)
                tt(dst, src, ss.unsqueeze(3).to_broadcast([128, 2, 4, 128]), ALU.mult)
                g = gain.rearrange("p (h v) -> p h v", h=4)
                for t in range(2):
                    r = tt(dst[:, t], dst[:, t], g, ALU.mult, hg_tok, gv_tok)
                return r
            group_norm(o4, o4, HG)
            tt(OC[:, :, 0:512], OC[:, :, 0:512], OG, ALU.mult, rest)

            v4 = VG.rearrange("p t (h v) -> p t h v", h=4)
            group_norm(v4, v4, GV)
            tri = CA[:, CA_TRI:CA_TRI + 128]
            gw_ready = tt(GW, GW, tri.unsqueeze(1).to_broadcast([128, 4, 128]), ALU.mult, gw_tok)
            for t in range(2):
                b, wb = bank()
                for g in range(4):
                    tok = mm(lambda e, g=g, t=t, b=b: e.matmul(
                        PS[:, b, g * 128:g * 128 + 128], GW[:, g, :], VG[:, t, g * 128:g * 128 + 128],
                        start=True, stop=True), gw_ready, *wb, mark=(g == 3))
                for g in range(4):
                    r = stt(OC[:, t, 512 + g * 128:640 + g * 128], PS[:, b, g * 128:g * 128 + 128],
                            PVT[:, PV_BS + g:PV_BS + g + 1], U[:, t, g * 128:g * 128 + 128], ALU.add, ALU.mult, tok)
                free[b] = [r]
            mt_tok = transposed(lambda k: MT[:, k, :], lambda t, k: OC[:, t, k * 128:k * 128 + 128], [P.last("V")])
            out_proj(d["l0_wout"], MT, mt_tok)

        def peer(l):
            G = AR[:, :].rearrange("p (e t) -> p e t", t=256)
            QT = ar(28672, 16, 256)
            S = ar(24576, 2, 2048)
            CD, OH, OH2 = ar(22528, 2048), ar(20480, 2048), ar(18432, 2048)
            SV, SI, SF = ar(17920, 16, 16), ar(17664, 16, 16), ar(17408, 16, 16)
            TS, TC, HI = ar(17280, 8, 16), ar(17152, 128), ar(17024, 128)
            HF, LF = ar(16896, 128), ar(16768, 128)
            TK = ar(16384, 3, 128)
            before = everything()
            xn = norm_T((PV_FFN0, PV_FFN1)[l], before)
            n = f"l{l}_"

            proj_T(d[n + "wq"], xnt, xn, 8, range(8),
                   lambda blk, ps, tok: evac(QT[:, blk:blk + 2, :], ps, tok))
            q_tok = [P.last("V"), P.last("A")]
            s, kv, kt = load(d[n + "keys"][0])
            for t in range(2):
                for j0 in range(0, 16, 4):
                    b, wb = bank()
                    for j in range(j0, j0 + 4):
                        tok = mm(lambda e, b=b, j=j, t=t: e.matmul(
                            PS[:, b, (j % 4) * 128:(j % 4) * 128 + 128], QT[:, j, t * 128:t * 128 + 128],
                            kv[:, j * 128:j * 128 + 128], start=True, stop=True), kt, *q_tok, *wb, mark=(j == j0 + 3))
                    free[b] = [act(S[:, t, j0 * 128:j0 * 128 + 512], PS[:, b, :], ACT.Copy, tok)]
            ring_free[s] = tok
            s_tok = P.last("A")

            def select(t):
                for j in range(16):
                    sj = S[:, t, j * 128:j * 128 + 128]
                    for r in range(2):
                        v8, i8 = SV[:, j, r * 8:r * 8 + 8], SI[:, j, r * 8:r * 8 + 8].bitcast(U32)
                        op("V", lambda e, v8=v8, sj=sj: e.max(v8, sj), s_tok)
                        op("V", lambda e, v8=v8, i8=i8, sj=sj: e.max_index(i8, v8, sj))
                        if r == 0:
                            op("V", lambda e, v8=v8, sj=sj: e.match_replace(sj, v8, sj, FILL))
                cp(SF, SI.bitcast(U32))
                sv = SV.rearrange("p (h q) k -> p h q k", q=2)
                sf = SF.rearrange("p (h q) k -> p h q k", q=2)
                cd = CD.rearrange("p (h a b) -> p h a b", h=8, a=16)
                for h in range(8):
                    tt(cd[:, h], sv[:, h, 0, :].unsqueeze(2).to_broadcast([128, 16, 16]),
                       sv[:, h, 1, :].unsqueeze(1).to_broadcast([128, 16, 16]), ALU.add)
                tc = TC.rearrange("p (h k) -> p h k", h=8)
                for h in range(8):
                    ch = CD[:, h * 256:h * 256 + 256]
                    for r in range(2):
                        v8, i8 = TS[:, h, r * 8:r * 8 + 8], tc[:, h, r * 8:r * 8 + 8].bitcast(U32)
                        op("V", lambda e, v8=v8, ch=ch: e.max(v8, ch))
                        op("V", lambda e, v8=v8, i8=i8, ch=ch: e.max_index(i8, v8, ch))
                        if r == 0:
                            op("V", lambda e, v8=v8, ch=ch: e.match_replace(ch, v8, ch, FILL))
                gt = TK[:, 2, :].rearrange("p (h k) -> p h k", h=8)
                tt(gt, TS, TS[:, :, 0:1].to_broadcast([128, 8, 16]), ALU.subtract, *tk_read)
                x_ = act(TK[:, 2, :], TK[:, 2, :], ACT.Exp, P.last("V"))
                op("V", lambda e: e.tensor_reduce(SM[:, 16:24], gt, AX, ALU.add), x_)
                op("V", lambda e: e.reciprocal(SM[:, 16:24], SM[:, 16:24]))
                tt(gt, gt, SM[:, 16:24].unsqueeze(2).to_broadcast([128, 8, 16]), ALU.mult)
                for which, (shift, mask) in enumerate(((4, None), (None, 15))):
                    if which == 0:
                        ts(HI.bitcast(U32), TC.bitcast(U32), 4, None, ALU.logical_shift_right)
                    else:
                        ts(HI.bitcast(U32), TC.bitcast(U32), 15, None, ALU.bitwise_and)
                    cp(HF, HI.bitcast(U32))
                    oh = OH.rearrange("p (a b) -> p a b", b=16)
                    tt(oh, HF.unsqueeze(2).to_broadcast([128, 128, 16]),
                       iota[:, 0:16].unsqueeze(1).to_broadcast([128, 128, 16]), ALU.is_equal)
                    oh4 = OH.rearrange("p (h k j) -> p h k j", h=8, k=16)
                    for h in range(8):
                        tt(oh4[:, h], oh4[:, h], sf[:, h, which, :].unsqueeze(1).to_broadcast([128, 16, 16]), ALU.mult)
                    op("V", lambda e, which=which, oh=oh: e.tensor_reduce(TK[:, which, :], oh, AX, ALU.add))
                return P.last("V")

            tk_read = []

            def select_to_slots(t):
                tok = select(t)
                b, wb = bank()
                for i in range(3):
                    tp = mm(lambda e, i=i, b=b: e.transpose(PS[:, b, i * 128:i * 128 + 128], TK[:, i, :], ident),
                            tok, *wb, mark=(i == 2))
                tk_read[:] = [tp]
                free[b] = [cp(IT[:, :, t * 128:t * 128 + 128],
                              PS[:, b, 0:384].rearrange("p (i t) -> p i t", i=3), tp)]
                return free[b][0]

            sel = []
            for c in range(64):
                s, wv, wt = load(d[n + "down"][c])
                b, wb = bank()
                for j in range(2):
                    for k in range(8):
                        tok = mm(lambda e, b=b, j=j, k=k, wv=wv: e.matmul(
                            PS[:, b, j * 256:j * 256 + 256], wv[:, (j * 8 + k) * 128:(j * 8 + k) * 128 + 128],
                            xnt(k), start=(k == 0), stop=(k == 7)), wt, *wb, *xn, mark=(j == 1 and k == 7))
                ring_free[s] = tok
                free[b] = [act(G[:, 2 * c:2 * c + 2, :], PS[:, b, :].rearrange("p (j t) -> p j t", j=2),
                               ACT.Gelu_apprx_tanh, tok, *(sel if c >= 32 else before))]
                if c in SEL_AT:
                    sel = [select_to_slots(SEL_AT.index(c))]
            down, g_tok = P.last("T"), P.last("A")

            A1, B1 = ([XNT[:, 4 * h + 2 * j:4 * h + 2 * j + 2, :].rearrange("p a (b i) -> p (a b) i", i=128)
                       for j in range(2)] for h in range(2))
            read = [None, None]
            for q in range(64):
                a1, b1 = A1[q % 2], B1[q % 2]
                for j in range(4):
                    t = 4 * q + j
                    av = ts(a1[:, j, :], iota, IT[:, 0, t:t + 1], None, ALU.is_equal, None, down, read[q % 2])
                    bv = ts(b1[:, j, :], iota, IT[:, 1, t:t + 1], IT[:, 2, t:t + 1], ALU.is_equal, ALU.mult)
                b, wb = bank()
                for j in range(4):
                    tok = mm(lambda e, j=j, a1=a1, b1=b1, b=b: e.matmul(
                        PS[:, b, j * 128:j * 128 + 128], b1[:, j, :], a1[:, j, :], start=True, stop=True),
                        bv, *wb, mark=(j == 3))
                read[q % 2] = tok
                if q:
                    fold(*held)
                held = (q, b, tok)

                def fold(q, b, tok):
                    g = G[:, :, 4 * q:4 * q + 4]
                    free[b] = [tt(g, PS[:, b, :].rearrange("p (t i) -> p i t", t=4), g, ALU.mult, tok, g_tok)]
            fold(*held)
            w_tok = P.last("V")

            acc = [bank() for _ in range(4)]
            for c in range(64):
                s, wv, wt = load(d[n + "up"][c])
                for j in range(2):
                    for t in range(2):
                        for h in range(2):
                            b, wb = acc[2 * t + h]
                            tok = mm(lambda e, b=b, j=j, t=t, h=h, c=c, wv=wv: e.matmul(
                                PS[:, b, :], G[:, 2 * c + j, t * 128:t * 128 + 128],
                                wv[:, j * 1024 + h * 512:j * 1024 + h * 512 + 512],
                                start=(c == 0 and j == 0), stop=(c == 63 and j == 1)),
                                wt, *wb, w_tok, mark=(j == 1 and t == 1 and h == 1))
                ring_free[s] = tok
            for t in range(2):
                for h in range(2):
                    b = acc[2 * t + h][0]
                    xv = X[:, t, h * 512:h * 512 + 512]
                    free[b] = [tt(xv, xv, PS[:, b, :], ALU.add, tok)]

        def seg_norm(v, tmp, ss, n, gain, *waits):
            m = v.shape[1]
            tt(tmp, v, v, ALU.mult, *waits)
            op("V", lambda e: e.tensor_reduce(ss, tmp, AX, ALU.add))
            rstd(ss, n)
            r = tt(v, v, ss.unsqueeze(2).to_broadcast([128, m, n]), ALU.mult)
            if gain is not None:
                r = tt(v, v, gain.unsqueeze(1).to_broadcast([128, m, n]), ALU.mult)
            return r

        def mixer1():
            Z = ar(0, 2, 2048)
            CQT, CKT = ar(4096, 2, 256), ar(4608, 1, 256)
            QC, KV, KC = ar(4864, 2, 768), ar(6400, 2, 1024), ar(8448, 2, 768)
            SN, CS, AN, RR = ar(9984, 2, 32), ar(10048, 2, 32), ar(10112, 2, 32), ar(10176, 2, 32)
            GN = ar(10240, 640)
            QN, QR, KN, KR, QD, KD = (ar(10880 + i * 1024, 4, 256) for i in range(6))
            PB = [ar(17024 + i * 384, 384) for i in range(3)]
            PT = [ar(18176 + i * 384, 3, 128) for i in range(2)]
            O = ar(18944, 2, 1024)
            MT = ar(20992, 8, 256)
            TMP = ar(23040, 1536)
            CB = ar(24576, CB_N)
            SS, MX, SU = SM[:, 24:32], SM[:, 32:48], SM[:, 48:80]
            before = everything()
            gn_tok = dma(GN, d["rows"][0:1, RW_MQ:RW_MQ + 640].to_broadcast([128, 640]), *before)
            cb_tok = dma(CB, d["cb"], *before)
            ps_i = AR[:, 25088:25090].bitcast(I32)
            ip_tok = dma(ps_i, d["pos"], *before)
            xn = norm_T(PV_MIX1, before)

            def use(c, ps, tok):
                return evac(Z[:, :, c * 256:c * 256 + 256], ps, tok)
            proj_nat(d["l1_win"], xnt, xn, 8, range(8), use)

            pf = AR[:, 25090:25092]
            cp(pf, ps_i, ip_tok)
            inv = CB[:, CB_INV:CB_INV + 32]
            for t in range(2):
                ts(AN[:, t, :], inv, pf[:, t:t + 1], None, ALU.mult, None, cb_tok)
            magic = 12582912.0
            ts(RR, AN, float(np.float32(1.0 / (2 * np.pi))), magic, ALU.mult, ALU.add)
            ts(RR, RR, magic, None, ALU.subtract)
            c1 = 6.28125
            c2 = float(np.float32(2 * np.pi - c1))
            c3 = float(2 * np.pi - c1 - c2)
            for cc in (c1, c2, c3):
                stt(AN, RR, -cc, AN, ALU.mult, ALU.add)
            lim = 3.1415925
            ts(SN, AN, lim, -lim, ALU.min, ALU.max)
            ts(AN, AN, float(np.pi / 2), None, ALU.add)
            ts(RR, AN, lim, -2 * float(np.pi), ALU.is_gt, ALU.mult)
            tt(AN, AN, RR, ALU.add)
            a_tok = ts(CS, AN, lim, -lim, ALU.min, ALU.max)
            act(SN, SN, ACT.Sin, a_tok)
            sc_tok = act(CS, CS, ACT.Sin)

            z_tok = [P.last("V"), P.last("A")]
            for t in range(2):
                seg_norm(Z[:, t:t + 1, 0:256], TMP[:, 0:256].unsqueeze(1), SS[:, 0:1], 256, None, *z_tok)
                r = seg_norm(Z[:, t:t + 1, 256:384], TMP[:, 0:128].unsqueeze(1), SS[:, 0:1], 128, None)
            cq = transposed(lambda k: CQT[:, k, :], lambda t, k: Z[:, t, k * 128:k * 128 + 128], [r],
                            gain=lambda k: PVT[:, PV_CQ + k:PV_CQ + k + 1], nk=2)
            ck = transposed(lambda k: CKT[:, k, :], lambda t, k: Z[:, t, 256:384], [r],
                            gain=lambda k: PVT[:, PV_CKV:PV_CKV + 1], nk=1)
            s, wv, wt = load(d["l1_uq"][0])
            for t in range(2):
                for h in range(2):
                    b, wb = bank()
                    for k in range(2):
                        tok = mm(lambda e, b=b, t=t, h=h, k=k, wv=wv: e.matmul(
                            PS[:, b, 0:384], CQT[:, k, t * 128:t * 128 + 128],
                            wv[:, k * 768 + h * 384:k * 768 + h * 384 + 384], start=(k == 0), stop=(k == 1)),
                            wt, *cq, *wb, mark=(k == 1))
                    free[b] = [evac(QC[:, t, h * 384:h * 384 + 384], PS[:, b, 0:384], tok)]
            ring_free[s] = tok
            s, wv2, wt = load(d["l1_ukv"][0])
            for t in range(2):
                for h in range(2):
                    b, wb = bank()
                    tok = mm(lambda e, b=b, t=t, h=h: e.matmul(
                        PS[:, b, :], CKT[:, 0, t * 128:t * 128 + 128], wv2[:, h * 512:h * 512 + 512],
                        start=True, stop=True), wt, *ck, *wb, mark=True)
                    free[b] = [evac(KV[:, t, h * 512:h * 512 + 512], PS[:, b, :], tok)]
            ring_free[s] = tok
            e_tok = P.last("A")
            kv4 = KV.rearrange("p t (h c) -> p t h c", h=4)
            kc4 = KC.rearrange("p t (h c) -> p t h c", h=4)
            for t in range(2):
                cp(kc4[:, t, :, 0:128], kv4[:, t, :, 0:128], e_tok)
                cp(kc4[:, t, :, 128:192], Z[:, t, 384:448].unsqueeze(1).to_broadcast([128, 4, 64]))
            for v, g in ((QC, GN[:, 0:192]), (KC, GN[:, 192:384])):
                v8 = v.rearrange("p t (h c) -> p (t h) c", c=192)
                seg_norm(v8, TMP.rearrange("p (s c) -> p s c", c=192), SS, 192, g, gn_tok)
                for t in range(2):
                    x1, x2 = (v8[:, 4 * t:4 * t + 4, a:a + 32] for a in (128, 160))
                    co, si = (w[:, t, :].unsqueeze(1).to_broadcast([128, 4, 32]) for w in (CS, SN))
                    t1, t2, t3, t4 = (TMP[:, i * 128:i * 128 + 128].rearrange("p (h i) -> p h i", h=4) for i in range(4))
                    tt(t1, x1, co, ALU.mult, sc_tok)
                    tt(t2, x2, si, ALU.mult)
                    tt(t3, x2, co, ALU.mult)
                    tt(t4, x1, si, ALU.mult)
                    tt(x1, t1, t2, ALU.subtract)
                    tt(x2, t3, t4, ALU.add)
            for t in range(2):
                for o, g in ((512, GN[:, 384:512]), (1024, GN[:, 512:640])):
                    seg_norm(Z[:, t, o:o + 512].rearrange("p (h c) -> p h c", h=4),
                             TMP[:, 0:512].rearrange("p (h c) -> p h c", h=4), SS[:, 0:4], 128, g)
            n_tok = P.last("V")
            q8 = QC.rearrange("p t (h c) -> p t h c", h=4)
            qk_tok = []
            for dst, src, w in ((QN, lambda t, k: q8[:, t, k, 0:128], 128), (KN, lambda t, k: kc4[:, t, k, 0:128], 128),
                                (QR, lambda t, k: q8[:, t, k, 128:192], 64), (KR, lambda t, k: kc4[:, t, k, 128:192], 64),
                                (QD, lambda t, k: Z[:, t, 512 + k * 128:640 + k * 128], 128),
                                (KD, lambda t, k: Z[:, t, 1024 + k * 128:1152 + k * 128], 128)):
                for kp in range(0, 4, 2):
                    b, wb = bank()
                    for j in range(2):
                        for t in range(2):
                            tok = mm(lambda e, b=b, j=j, t=t, kp=kp, src=src, w=w: e.transpose(
                                PS[0:w, b, j * 256 + t * 128:j * 256 + t * 128 + 128], src(t, kp + j), ident),
                                n_tok, *wb, mark=(j == 1 and t == 1))
                    free[b] = [evac(dst[0:w, kp:kp + 2, :], PS[0:w, b, :].rearrange("p (j t) -> p j t", j=2), tok)]
                    qk_tok += free[b]

            mask = CB[:, CB_M:CB_M + 384]

            def parts(h):
                if h < 4:
                    return [(QN[:, h], KN[:, h]), (QR[0:64, h], KR[0:64, h])], 192 ** -0.5
                return [(QD[:, h - 4], KD[:, h - 4])], 128 ** -0.5

            def values(h, t):
                if h < 4:
                    return KV[:, t, h * 256 + 128:h * 256 + 256]
                return Z[:, t, 1536 + (h - 4) * 128:1536 + (h - 4) * 128 + 128]
            hd = {}
            pt_read = [None, None]

            def scores(h):
                pp, scale = parts(h)
                b, wb = bank()
                for t in range(2):
                    o = PS[:, b, 0:128] if t == 0 else PS[:, b, 128:384]
                    for i, (q, k) in enumerate(pp):
                        tok = mm(lambda e, o=o, q=q, k=k, t=t, i=i: e.matmul(
                            o, q[:, t * 128:t * 128 + 128], k[:, 0:128 * (t + 1)], start=(i == 0),
                            stop=(i == len(pp) - 1)), *qk_tok, *wb, mark=True)
                p = PB[h % 3]
                mx, su = MX[:, 2 * h:2 * h + 2], SU[:, 2 * h:2 * h + 2]
                free[b] = [stt(p, PS[:, b, 0:384], float(scale), mask, ALU.mult, ALU.add, tok,
                               hd[h - 3]["tr"] if h >= 3 else None)]
                op("V", lambda e: e.tensor_reduce(mx[:, 0:1], p[:, 0:128], AX, ALU.max))
                op("V", lambda e: e.tensor_reduce(mx[:, 1:2], p[:, 128:384], AX, ALU.max))
                mt = ts(mx, mx, -1.0, None, ALU.mult)
                act(p[:, 0:128], p[:, 0:128], ACT.Exp, mt, bias=mx[:, 0:1], accum_out=su[:, 0:1])
                et = act(p[:, 128:384], p[:, 128:384], ACT.Exp, bias=mx[:, 1:2], accum_out=su[:, 1:2])
                rt = op("V", lambda e: e.reciprocal(su, su), et)
                hd[h] = {"p": p, "e": et, "r": rt}

            def turn_p(h):
                b, wb = bank()
                for i in range(3):
                    tok = mm(lambda e, i=i, b=b, h=h: e.transpose(PS[:, b, i * 128:i * 128 + 128],
                                                                  PB[h % 3][:, i * 128:i * 128 + 128], ident),
                             hd[h]["e"], *wb, mark=(i == 2))
                hd[h]["tr"] = tok
                free[b] = [evac(PT[h % 2], PS[:, b, 0:384].rearrange("p (i q) -> p i q", i=3), tok, pt_read[h % 2])]
                hd[h]["pt"] = free[b][0]

            def weigh(h):
                b, wb = bank()
                pt = PT[h % 2]
                mm(lambda e: e.matmul(PS[:, b, 0:128], pt[:, 0, :], values(h, 0), start=True, stop=True),
                   hd[h]["pt"], *wb)
                mm(lambda e: e.matmul(PS[:, b, 128:256], pt[:, 1, :], values(h, 0), start=True, stop=False))
                tok = mm(lambda e: e.matmul(PS[:, b, 128:256], pt[:, 2, :], values(h, 1), start=False, stop=True), mark=True)
                pt_read[h % 2] = tok
                for t in range(2):
                    free[b] = [evac(O[:, t, h * 128:h * 128 + 128], PS[:, b, t * 128:t * 128 + 128], tok, hd[h]["r"],
                                    scale=SU[:, 2 * h + t:2 * h + t + 1], eng="VA"[h % 2])]
            for i in range(10):
                if i < 8:
                    scores(i)
                if 1 <= i < 9:
                    turn_p(i - 1)
                if i >= 2:
                    weigh(i - 2)
            mt_tok = transposed(lambda k: MT[:, k, :], lambda t, k: O[:, t, k * 128:k * 128 + 128],
                                [P.last("V"), P.last("A")])
            out_proj(d["l1_wout"], MT, mt_tok)

        def rel_table():
            OHB, NG, RB, R = ar(0, 512), ar(512, 512), ar(1024, 24), ar(1152, 512)
            before = everything()
            a = dma(AR[0:32, 0:1024], d["cd"], *before)
            r = dma(AR[0:32, 1024:1048], d["rel"], *before)
            b, wb = bank()
            tok = mm(lambda e: e.matmul(PS[0:24, b, 0:511], RB[0:32, :], OHB[0:32, 0:511], start=True, stop=True),
                     a, r, *wb, mark=True)
            free[b] = [tt(R[0:24, 0:511], PS[0:24, b, 0:511], NG[0:24, 0:511], ALU.add, tok, a)]
            return dma(scr[:, 0:511], R[0:24, 0:511], free[b][0])

        def block2():
            QT, KT = ar(0, 12, 256), ar(3072, 12, 256)
            VN = ar(6144, 2, 1536)
            AI, SAG, BGT = ar(9216, 2, 512), ar(10240, 4, 256), ar(11264, 4, 256)
            GL = ar(12288, 2, 2048)
            SK = ar(16384, 24, 384)
            PG = ar(25600, 2, 1024)
            BG = ar(27648, 2048)
            SB = [ar(27648 + 768 * i, 768) for i in range(3)]
            PT = [ar(29952 + 768 * i, 768) for i in range(2)]
            ATT = ar(25600, 2, 512)
            PT4, YAT, WP = ar(26624, 4, 256), XNT[:, 0:4, :], ar(29696, 4, 128)
            BTT = XNT[:, 4:8, :]
            MG, MT, FG, YB = ar(0, 2, 1024), ar(2048, 8, 256), ar(4096, 1024), ar(5120, 2, 512)
            before = everything()
            pg_tok = dma(AR[:, 25600:27648], d["cc"], *before)
            bg_tok = dma(BG, d["rows"][0:1, RW_BG:RW_BG + 2048].to_broadcast([128, 2048]), *before)
            wp_tok = dma(WP, d["wpool"].rearrange("p (g t) -> p g t", g=4), *before)
            sk_tok = dma(SK, bass.AP(scr, 0, [[1, 128], [512, 24], [1, 384]]), *before, rel_tok[0])
            xn = norm_T(PV_MIX2, before)

            def use_nat(dst):
                return lambda c, ps, tok, dst=dst: evac(dst[0][:, :, (c - dst[1]) * 256:(c - dst[1]) * 256 + 256], ps, tok)

            def use_q(blk, ps, tok):
                free_ = []
                for j in range(2):
                    free_ = evac(QT[:, blk - 8 + j, :].rearrange("p (t q) -> p t q", t=2),
                                 ps[:, j, :].rearrange("p (t q) -> p t q", t=2)[:, :, ::-1], tok, eng="V")
                return free_

            def use_g(c, ps, tok):
                o = (c - 24) * 256
                bgb = BG[:, o:o + 256].unsqueeze(1).to_broadcast([128, 2, 256])
                g_ = tt(GL[:, :, o:o + 256], ps, bgb, ALU.add, tok, bg_tok)
                act(GL[:, :, o:o + 256], GL[:, :, o:o + 256], ACT.Sigmoid, g_)
                return g_
            w = d["w_in2"]
            proj_nat(w, xnt, xn, 8, range(0, 2), use_nat((AI, 0)))
            proj_T(w, xnt, xn, 8, range(2, 4),
                   lambda blk, ps, tok: act(SAG[:, blk - 4:blk - 2, :], ps, ACT.Silu, tok))
            proj_T(w, xnt, xn, 8, range(4, 10), use_q)
            proj_T(w, xnt, xn, 8, range(10, 16),
                   lambda blk, ps, tok: evac(KT[:, blk - 20:blk - 18, :], ps, tok))
            proj_nat(w, xnt, xn, 8, range(16, 22), use_nat((VN, 16)))
            proj_T(w, xnt, xn, 8, range(22, 24),
                   lambda blk, ps, tok: act(BGT[:, blk - 44:blk - 42, :], ps, ACT.Silu, tok))
            proj_nat(w, xnt, xn, 8, range(24, 32), use_g)
            z_tok = [P.last("V"), P.last("A")]
            xn_read = P.last("T")

            for g in range(0, 4, 2):
                b, wb = bank()
                for j in range(2):
                    for t in range(2):
                        tok = mm(lambda e, b=b, j=j, t=t, g=g: e.matmul(
                            PS[:, b, j * 256:j * 256 + 256], AI[:, t, (g + j) * 128:(g + j) * 128 + 128],
                            PG[:, t, (g + j) * 256:(g + j) * 256 + 256], start=(t == 0), stop=(t == 1)),
                            pg_tok, *z_tok, *wb, mark=(j == 1 and t == 1))
                free[b] = [evac(PT4[:, g:g + 2, :], PS[:, b, :].rearrange("p (j t) -> p j t", j=2), tok, eng="V")]
            p_tok = P.last("V")
            for g in range(0, 4, 2):
                b, wb = bank()
                for j in range(2):
                    tok = mm(lambda e, b=b, j=j, g=g: e.matmul(
                        PS[:, b, j * 256:j * 256 + 256], WP[:, g + j, :], PT4[:, g + j, :], start=True, stop=True),
                        p_tok, wp_tok, *wb, mark=(j == 1))
                for j in range(2):
                    r = stt(YAT[:, g + j, :], PS[:, b, j * 256:j * 256 + 256], PVT[:, PV_PS + g + j:PV_PS + g + j + 1],
                            SAG[:, g + j, :], ALU.mult, ALU.mult, tok, xn_read, *z_tok)
                free[b] = [r]
            ya_tok = P.last("V")
            pool_read = P.last("T")

            hd = {}
            pt_read = [None, None]
            allowed[0] = [0, 1, 2, 3]
            pair = [0]

            def two_banks():
                b = 2 * (pair[0] % 4)
                pair[0] += 1
                return b, [*free[b], *free[b + 1]]
            MX, SU = SM[:, 80:96], SM[:, 96:112]

            def scores(i):
                h, t = divmod(i, 2)
                b, wb = two_banks()
                sp = PS[:, b:b + 2, :].rearrange("p a n -> p (a n)")[:, 0:768]
                pb = (h % 2) * 64
                for g in range(3):
                    nb = g * 4 + h // 2
                    tok = mm(lambda e, g=g, nb=nb, sp=sp: e.matmul(
                        sp[:, g * 256:g * 256 + 256], QT[pb:pb + 64, nb, t * 128:t * 128 + 128],
                        KT[pb:pb + 64, nb, :], start=True, stop=True), *z_tok, *wb, mark=(g == 2))
                s_ = SB[i % 3]
                sk = SK.rearrange("p (g h) j -> p g h j", g=3)[:, :, h, 128 * (1 - t):128 * (1 - t) + 256]
                r = stt(s_.rearrange("p (g k) -> p g k", g=3), sp.rearrange("p (g k) -> p g k", g=3), 0.125, sk,
                        ALU.mult, ALU.add, tok, sk_tok, pool_read, hd[i - 3]["tr"] if i >= 3 else None)
                free[b], free[b + 1] = [r], [r]
                mx = MX[:, i:i + 1]
                op("V", lambda e: e.tensor_reduce(mx, s_, AX, ALU.max))
                mt = ts(mx, mx, -1.0, None, ALU.mult)
                et = act(s_, s_, ACT.Exp, mt, bias=mx, accum_out=SU[:, i:i + 1])
                rt = op("V", lambda e: e.reciprocal(SU[:, i:i + 1], SU[:, i:i + 1]), et)
                hd[i] = {"e": et, "r": rt}

            def turn_p(i):
                b, wb = two_banks()
                sp = PS[:, b:b + 2, :].rearrange("p a n -> p (a n)")[:, 0:768]
                for j in range(6):
                    tok = mm(lambda e, j=j, sp=sp: e.transpose(sp[:, j * 128:j * 128 + 128],
                                                               SB[i % 3][:, j * 128:j * 128 + 128], ident),
                             hd[i]["e"], *wb, mark=(j == 5))
                hd[i]["tr"] = tok
                r = evac(PT[i % 2], sp, tok, pt_read[i % 2], eng="A")
                free[b], free[b + 1] = [r], [r]
                hd[i]["pt"] = r

            def weigh(i):
                h, t = divmod(i, 2)
                b, wb = two_banks()
                for j in range(6):
                    g, kt = divmod(j, 2)
                    tok = mm(lambda e, j=j, g=g, kt=kt: e.matmul(
                        PS[:, b, 0:64], PT[i % 2][:, j * 128:j * 128 + 128],
                        VN[:, kt, g * 512 + h * 64:g * 512 + h * 64 + 64], start=(j == 0), stop=(j == 5)),
                        hd[i]["pt"], *wb, mark=(j == 5))
                pt_read[i % 2] = tok
                r = evac(ATT[:, t, h * 64:h * 64 + 64], PS[:, b, 0:64], tok, hd[i]["r"], scale=SU[:, i:i + 1], eng="V")
                free[b], free[b + 1] = [r], [r]
            for i in range(18):
                if i < 16:
                    scores(i)
                if 1 <= i < 17:
                    turn_p(i - 1)
                if i >= 2:
                    weigh(i - 2)
            allowed[0] = list(range(8))
            att = P.last("V")
            for nb in range(0, 4, 2):
                b, wb = bank()
                for j in range(2):
                    for t in range(2):
                        tok = mm(lambda e, b=b, j=j, t=t, nb=nb: e.transpose(
                            PS[:, b, j * 256 + t * 128:j * 256 + t * 128 + 128],
                            ATT[:, t, (nb + j) * 128:(nb + j) * 128 + 128], ident), att, *wb, mark=(j == 1 and t == 1))
                for j in range(2):
                    r = tt(BTT[:, nb + j, :].rearrange("p (t q) -> p t q", t=2),
                           PS[:, b, j * 256:j * 256 + 256].rearrange("p (t q) -> p t q", t=2)[:, :, ::-1],
                           BGT[:, nb + j, :].rearrange("p (t q) -> p t q", t=2), ALU.mult, tok)
                free[b] = [r]
            bt_tok = P.last("V")

            def use_a(c, t, ps, tok):
                return tt(MG[:, t, c * 512:c * 512 + 512], ps, GL[:, t, c * 512:c * 512 + 512], ALU.mult, tok, *z_tok)

            def use_b(c, t, ps, tok):
                r_ = tt(YB[:, t, :], ps, GL[:, t, 1024 + c * 512:1536 + c * 512], ALU.mult, tok)
                m_ = MG[:, t, c * 512:c * 512 + 512]
                tt(m_, m_, YB[:, t, :], ALU.add)
                return r_
            fg_tok = dma(FG, d["rows"][0:1, RW_FG:RW_FG + 1024].to_broadcast([128, 1024]), bt_tok, P.last("T"), P.last("A"))
            P.wait("V", P.last("T"))
            proj_nat(d["w_pa"], lambda k: YAT[:, k, :], [ya_tok], 4, range(2), use_a)
            proj_nat(d["w_pb"], lambda k: BTT[:, k, :], [bt_tok], 4, range(2), use_b)
            mt_tok = transposed(lambda k: MT[:, k, :], lambda t, k: MG[:, t, k * 128:k * 128 + 128], [P.last("V")])
            out_proj(d["w_out2"], MT, mt_tok)

            x_ = P.last("V")
            sq = GL
            for t in range(2):
                act(sq[:, t, 0:1024], X[:, t, :], ACT.Square, x_, accum_out=SM[:, t:t + 1])
            rstd(SM[:, 0:2], 1024, P.last("A"))
            for t in range(2):
                stt(X[:, t, :], X[:, t, :], SM[:, t:t + 1], FG, ALU.mult, ALU.mult, fg_tok)

        rel_tok = [None]

        def tail():
            rel_tok[0] = rel_table()
            block2()
        stages = [mixer0, lambda: peer(0), mixer1, lambda: peer(1), tail]
        for st in stages[:upto]:
            st()
        o_tok = dma(out.rearrange("(t p) c -> p t c", p=128), X[:, :, :], *everything())
        P.wait("S", o_tok)

        block = ctx.enter_context(nc.Block())

        @block.sync
        def _(eng):
            P.emit("S", eng)

        @block.gpsimd
        def _(eng):
            P.emit("G", eng)

        @block.scalar
        def _(eng):
            P.emit("A", eng)

        @block.tensor
        def _(eng):
            P.emit("T", eng)

        @block.vector
        def _(eng):
            P.emit("V", eng)


def _constants():
    p = np.arange(128)
    cst = np.zeros((128, C_N0), np.float32)
    cst[:, C_ID:C_ID + 128] = np.eye(128)
    cst[:, C_IOTA:C_IOTA + 128] = p[None, :]
    cst[:, C_ONE:C_ONE + 128] = 1
    ca = np.zeros((128, CA_N), np.float32)
    s, t = p[:, None], p[None, :]
    for lv in range(8):
        m = s == t if lv == 0 else (s >> lv == t >> lv) & ((s >> (lv - 1)) & 1 == 0) & ((t >> (lv - 1)) & 1 == 1)
        ca[:, CA_LV + lv * 128:CA_LV + lv * 128 + 128] = m
    ca[:, CA_TRI:CA_TRI + 128] = s <= t
    cb = np.zeros((128, CB_N), np.float32)
    tri = np.where(t <= s, 0, NBIG)
    cb[:, CB_M:CB_M + 128] = tri
    cb[:, CB_M + 256:CB_M + 384] = tri
    cb[:, CB_INV:CB_INV + 32] = (np.float32(10000.0) ** (-np.arange(32, dtype=np.float32) / np.float32(32)))[None, :]
    pool = np.zeros((256, 4, 256), np.float32)
    for g, w in enumerate((2, 4, 8, 16)):
        for q in range(256):
            lo, hi = max(q - w // 2, 0), min(q + w // 2 - 1, 255)
            pool[lo:hi + 1, g, q] = np.float32(1) / np.float32(hi - lo + 1)
            pool[q, g, q] -= 1
    cc = pool.reshape(2, 128, 4, 256).transpose(1, 0, 2, 3).reshape(128, 2048)
    cd = np.zeros((32, CD_N), np.float32)
    rel = np.arange(511) - 255
    n = np.abs(rel)
    large = 8 + (np.log(np.maximum(n, 1).astype(np.float32) / np.float32(8)) / np.float32(np.log(128.0))
                 * np.float32(8)).astype(np.int32)
    bucket = (rel > 0) * 16 + np.where(n < 8, n, np.minimum(large, 15))
    cd[bucket, CD_OH + np.arange(511)] = 1
    for g, dil in enumerate((1, 4, 16)):
        bad = (rel % dil != 0) | (n > 64 * dil)
        cd[g * 8:g * 8 + 8, CD_NG:CD_NG + 511] = np.where(bad, NBIG, 0)[None, :]
    return dict(cst=cst, ca=ca, cb=cb, cc=np.ascontiguousarray(cc), cd=cd)


def _layout(i):
    def cols(v):
        return v.reshape(-1, 128).T

    def chunks(w, n):
        k = w.shape[0] // 128
        return np.ascontiguousarray(
            w.reshape(k, 128, w.shape[1] // n, n).transpose(2, 1, 0, 3).reshape(w.shape[1] // n, 128, k * n))
    a = _constants()
    a["x"] = np.ascontiguousarray(i["x"][0])
    a["pos"] = np.ascontiguousarray(i["positions"].reshape(2, 128).T.astype(np.int32))
    lb = i["lb_logits"].reshape(3, 4, 128).transpose(2, 0, 1).reshape(128, 12)
    a["pv"] = np.ascontiguousarray(np.concatenate(
        [cols(i[n]) for n in ("l0_norm_mix", "l0_norm_ffn", "l1_norm_mix", "l1_norm_ffn")]
        + [cols(i["norm_gain_2"][0]), cols(i["l1_mla_cq_norm"]), cols(i["l1_mla_ckv_norm"]), lb,
           i["l0_gmlp_b_s"].T, cols(i["pool_scale_2"][0])], axis=1))
    a["rows"] = np.concatenate([i[n].reshape(1, -1) for n in (
        "l0_hgrn_out_norm", "l0_gmlp_v_norm", "l1_mla_q_norm", "l1_mla_k_norm", "l1_moba_q_norm", "l1_moba_k_norm",
        "b_gate_2", "final_gain_2")], axis=1)
    a["gw"] = np.ascontiguousarray(i["l0_gmlp_w_s"].transpose(2, 0, 1).reshape(128, 512))
    a["l0_win"] = chunks(i["l0_w_in"], 256)
    a["l0_wout"] = chunks(i["l0_w_out"], 256)
    w = i["l1_w_in"]
    w = np.concatenate([w[:, :448], np.zeros((1024, 64), w.dtype), w[:, 448:]], axis=1)
    a["l1_win"] = chunks(w, 256)
    a["l1_uq"] = chunks(i["l1_mla_w_uq"], 768)
    a["l1_ukv"] = chunks(i["l1_mla_w_ukv"], 1024)
    a["l1_wout"] = chunks(i["l1_w_out"], 256)
    for l in (0, 1):
        n = f"l{l}_"
        a[n + "wq"] = chunks(i[n + "peer_w_query"], 256)
        a[n + "keys"] = np.ascontiguousarray(
            i[n + "peer_sub_keys"].reshape(16, 128, 128).transpose(2, 0, 1).reshape(1, 128, 2048))
        a[n + "down"] = np.ascontiguousarray(
            i[n + "peer_expert_down"].reshape(64, 2, 128, 8, 128).transpose(0, 4, 1, 3, 2).reshape(64, 128, 2048))
        a[n + "up"] = np.ascontiguousarray(
            i[n + "peer_expert_up"].reshape(64, 2, 128, 1024).transpose(0, 2, 1, 3).reshape(64, 128, 2048))
    a["w_in2"] = chunks(i["w_in_2"][0], 256)
    a["rel"] = np.ascontiguousarray(i["rel_bias_2"])
    a["wpool"] = np.ascontiguousarray(i["w_pool_2"][0].transpose(1, 0, 2).reshape(128, 512))
    a["w_pa"] = chunks(i["w_proj_a_2"][0], 512)
    a["w_pb"] = chunks(i["w_proj_b_2"][0], 512)
    a["w_out2"] = chunks(i["w_out_2"][0], 256)
    return a


def kernel(**inputs):
    import numpy as _np
    import concourse.bacc as _bacc
    from concourse import mybir as _mybir
    from concourse.bass_utils import run_bass_kernel_spmd as _run

    nc = _bacc.Bacc("TRN2", target_bir_lowering=False, num_devices=1)
    arrays, args = {}, {}
    for name, a in _layout({k: _np.asarray(v) for k, v in inputs.items()}).items():
        arrays[f"in_{name}_dram"] = a
        args[name] = nc.dram_tensor(f"in_{name}_dram", a.shape, _mybir.dt.from_np(a.dtype), kind="ExternalInput").ap()
    out = nc.dram_tensor("out_0_dram", (256, 1024), _mybir.dt.float32, kind="ExternalOutput").ap()
    build(nc, args, out)
    r = _run(nc, [arrays], core_ids=[0])
    return r.results[0]["out_0_dram"].reshape(1, 256, 1024)
```

```python
from contextlib import ExitStack

import numpy as np

import concourse.bass as bass
from concourse import mybir

ALU = mybir.AluOpType
ACT = mybir.ActivationFunctionType
AX = mybir.AxisListType.X
F32 = mybir.dt.float32
F32R = mybir.dt.float32r
U32 = mybir.dt.uint32
I32 = mybir.dt.int32

NRAW = 4
NW = 3
AHEAD = 2
SLOT = 1024
NBIG = -1.0e30
FILL = -3.0e38
EPS = 1e-6

PV_MIX0, PV_FFN0, PV_MIX1, PV_FFN1, PV_MIX2, PV_CQ, PV_CKV, PV_LB, PV_BS, PV_PS, PV_BG, PV_N = (
    0, 8, 16, 24, 32, 40, 42, 43, 55, 59, 63, 79)
RW_HG, RW_GV, RW_MQ, RW_MK, RW_OQ, RW_OK, RW_FG, RW_N = (
    0, 512, 1024, 1216, 1408, 1536, 1664, 2688)
C_ID, C_IOTA, C_ONE, C_N0 = 0, 128, 256, 384
CA_LV, CA_TRI, CA_N = 0, 1024, 1152
CB_M, CB_INV, CB_N = 0, 384, 416
CC_PG, CC_N = 0, 2048
CD_OH, CD_NG, CD_N = 0, 512, 1024


class Program:

    def __init__(self, nc, ctx):
        self.nc, self.ctx = nc, ctx
        self.q = {k: [] for k in "VAGTS"}
        self.sem = {k: ctx.enter_context(nc.semaphore(f"done_{n}")) for k, n in
                    zip("VAGT", ("vector", "scalar", "gpsimd", "tensor"))}
        self.count = dict.fromkeys("VAGT", 0)
        self.ndma = 0

    def last(self, k):
        return (self.sem[k], self.count[k])

    def op(self, k, fn, *waits, loose=False):
        own = [self.last(k)] if self.count[k] and not loose else []
        self.count[k] += 1
        self.q[k].append((own + [w for w in waits if w], fn, self.sem[k], 1))
        return self.last(k)

    def mm(self, fn, *waits, mark=False):
        if mark:
            self.count["T"] += 1
        self.q["T"].append(([w for w in waits if w], fn, self.sem["T"] if mark else None, 1))
        return self.last("T")

    def dma(self, out, in_, *waits, sem=None, value=16, k="S"):
        if sem is None:
            sem = self.ctx.enter_context(self.nc.semaphore(f"dma{self.ndma}"))
            self.ndma += 1
        self.q[k].append(([w for w in waits if w], lambda e: e.dma_start(out, in_), sem, 16))
        return (sem, value)

    def wait(self, k, *waits):
        self.q[k].append(([w for w in waits if w], None, None, 0))

    def emit(self, k, eng):
        seen = {}
        for waits, fn, sem, inc in self.q[k]:
            for s, v in waits:
                if v and seen.get(s.name, 0) < v:
                    eng.wait_ge(s, v)
                    seen[s.name] = v
            if fn is not None:
                ins = fn(eng)
                if sem is not None:
                    ins.then_inc(sem, inc)


def build(nc, d, out, upto=9):
    ctx = ExitStack()
    with ctx:
        def sb(name, shape, dt=F32):
            return ctx.enter_context(nc.sbuf_tensor(name, shape, dt))

        P = Program(nc, ctx)
        op, mm, dma = P.op, P.mm, P.dma

        X = sb("X", [128, 2, 1024])
        XH = sb("XH", [128, 8, 256], F32R)
        XL = sb("XL", [128, 8, 256], F32R)
        raw = sb("raw", [128, NRAW, SLOT])
        WH = sb("WH", [128, NW, SLOT], F32R)
        WL = sb("WL", [128, NW, SLOT], F32R)
        GH = sb("GH", [128, 2, 512], F32R)
        GL_ = sb("GL", [128, 2, 512], F32R)
        OA = sb("OA", [128, 2, 256])
        OB = sb("OB", [128, 2, 512])
        AR = sb("arena", [128, 32768])
        CST = sb("cst", [128, C_N0])
        PVT = sb("pvt", [128, PV_N])
        IT = sb("it", [128, 3, 256])
        SM = sb("sm", [128, 128])
        PS = ctx.enter_context(nc.psum_tensor("ps", [128, 8, 512], F32))
        scr = nc.dram_tensor("scr_rel", [24, 512], F32, kind="Internal")
        ident = CST[:, C_ID:C_ID + 128]
        iota = CST[:, C_IOTA:C_IOTA + 128]
        ones = CST[:, C_ONE:C_ONE + 128]

        def ar(off, *shape):
            n = int(np.prod(shape))
            assert off + n <= 32768
            v = AR[:, off:off + n]
            if len(shape) == 2:
                v = v.rearrange("p (a b) -> p a b", b=shape[1])
            if len(shape) == 3:
                v = v.rearrange("p (a b c) -> p a b c", b=shape[1], c=shape[2])
            return v

        free = [[] for _ in range(8)]
        pools = {"main": [0, 1, 2, 3], "side": [4, 5, 6, 7]}
        turn = dict.fromkeys(pools, 0)

        def bank(pool="main"):
            b = pools[pool][turn[pool] % len(pools[pool])]
            turn[pool] += 1
            return b, free[b]

        order = ([("l0_qf", c) for c in range(8)] + [("l0_nat", c) for c in range(16)]
                 + [("l0_wout", c) for c in range(8)])

        def peer_order(l):
            return ([(f"l{l}_wq", c) for c in range(16)] + [(f"l{l}_down", c) for c in range(128)]
                    + [(f"l{l}_up", c) for c in range(128)])
        order += peer_order(0) + [("l1_win", c) for c in range(16)] + [("l1_wout", c) for c in range(8)] + peer_order(1)
        order += [("w2_a", c) for c in range(4)] + [("w2_qk", c) for c in range(24)] + [("w2_v", c) for c in range(12)]
        order += [("w2_gates", c) for c in range(24)]
        order += [("w_pa", c) for c in range(4)] + [("w_pb", c) for c in range(4)] + [("w_out2", c) for c in range(8)]
        raw_sem = [ctx.enter_context(nc.semaphore(f"raw{i}")) for i in range(NRAW)]
        raw_tok, raw_free, part_tok, part_free = {}, {}, {}, {}
        at = {"load": 0, "split": 0, "use": 0}

        def stream_load():
            i = at["load"]
            if i >= len(order) or (i >= NRAW and i - NRAW not in raw_free):
                return False
            name, c = order[i]
            raw_tok[i] = dma(raw[:, i % NRAW, :], d[name][c], raw_free.get(i - NRAW), sem=raw_sem[i % NRAW],
                             value=16 * (i // NRAW + 1))
            at["load"] += 1
            return True

        def stream_split():
            i = at["split"]
            if i >= len(order) or i not in raw_tok or (i >= NW and i - NW not in part_free):
                return False
            r, h, l = raw[:, i % NRAW, :], WH[:, i % NW, :], WL[:, i % NW, :]
            ht = act(h, r, ACT.Copy, raw_tok[i], part_free.get(i - NW), loose=True)
            raw_free[i] = part_tok[i] = tt(l, r, h, ALU.subtract, ht, loose=True)
            at["split"] += 1
            return True

        def stream_next(name, c):
            i = at["use"]
            assert order[i] == (name, c), (order[i], name, c)
            at["use"] += 1
            while at["split"] <= min(i + AHEAD, len(order) - 1):
                while stream_load():
                    pass
                if not stream_split():
                    break
            while stream_load():
                pass
            assert i in part_tok
            return WH[:, i % NW, :], WL[:, i % NW, :], part_tok[i], i

        def stream_done(i, tok):
            part_free[i] = tok

        def everything():
            return [P.last(k) for k in "VAGT"]

        parity = [0]

        def turn_engine():
            parity[0] ^= 1
            return "VA"[parity[0]]

        def evac(out_, in_, *waits, scale=None, eng=None):
            k = eng or turn_engine()
            if k == "V":
                if scale is None:
                    return op("V", lambda e: e.tensor_copy(out_, in_), *waits)
                return op("V", lambda e: e.tensor_scalar(out_, in_, scale, None, ALU.mult), *waits)
            if scale is None:
                return op("A", lambda e: e.activation(out_, in_, ACT.Copy), *waits)
            return op("A", lambda e: e.activation(out_, in_, ACT.Copy, scale=scale), *waits)

        def tt(out_, a, b, o, *waits, k="V", loose=False):
            return op(k, lambda e: e.tensor_tensor(out_, a, b, o), *waits, loose=loose)

        def ts(out_, a, s1, s2, o1, o2=None, *waits, k="V", loose=False):
            if o2 is None:
                return op(k, lambda e: e.tensor_scalar(out_, a, s1, None, o1), *waits, loose=loose)
            return op(k, lambda e: e.tensor_scalar(out_, a, s1, s2, o1, o2), *waits, loose=loose)

        def stt(out_, a, s, b, o1, o2, *waits):
            return op("V", lambda e: e.scalar_tensor_tensor(out=out_, in0=a, scalar=s, in1=b, op0=o1, op1=o2), *waits)

        def act(out_, in_, f, *waits, loose=False, **kw):
            return op("A", lambda e: e.activation(out_, in_, f, **kw), *waits, loose=loose)

        def cp(out_, in_, *waits, k="V"):
            return op(k, lambda e: e.tensor_copy(out_, in_), *waits)

        def rstd(v, n, *waits):
            ts(v, v, 1.0 / n, EPS, ALU.mult, ALU.add, *waits)
            ta = act(v, v, ACT.Sqrt, P.last("V"))
            return op("V", lambda e: e.reciprocal(v, v), ta)

        def transposed(dst, src, src_tok, gain=None, nk=8, pool="main"):
            toks = []
            for kp in range(0, nk, 2):
                b, w = bank(pool)
                n = min(2, nk - kp)
                for j in range(n):
                    for t in range(2):
                        last = j == n - 1 and t == 1
                        tok = mm(lambda e, b=b, j=j, t=t, kp=kp: e.transpose(
                            PS[:, b, j * 256 + t * 128:j * 256 + t * 128 + 128], src(t, kp + j), ident),
                            *w, *src_tok, mark=last)
                who = turn_engine()
                for j in range(n):
                    r = evac(dst(kp + j), PS[:, b, j * 256:j * 256 + 256], tok,
                             scale=gain(kp + j) if gain else None, eng=who)
                free[b] = [r]
                toks.append(r)
            return toks

        def transposed_split(src, src_tok, gain=None):
            toks = []
            for kp in range(0, 8, 2):
                b, w = bank()
                for j in range(2):
                    for t in range(2):
                        tok = mm(lambda e, b=b, j=j, t=t, kp=kp: e.transpose(
                            PS[:, b, j * 256 + t * 128:j * 256 + t * 128 + 128], src(t, kp + j), ident),
                            *w, *src_tok, mark=(j == 1 and t == 1))
                if gain is None:
                    ps = PS[:, b, :].rearrange("p (j t) -> p j t", j=2)
                    ht = act(XH[:, kp:kp + 2, :], ps, ACT.Copy, tok)
                    toks.append(tt(XL[:, kp:kp + 2, :], ps, XH[:, kp:kp + 2, :], ALU.subtract, ht))
                else:
                    for j in range(2):
                        ht = act(XH[:, kp + j, :], PS[:, b, j * 256:j * 256 + 256], ACT.Copy, tok, scale=gain(kp + j))
                    for j in range(2):
                        r = stt(XL[:, kp + j, :], PS[:, b, j * 256:j * 256 + 256], gain(kp + j), XH[:, kp + j, :],
                                ALU.mult, ALU.subtract, ht)
                    toks.append(r)
                free[b] = [toks[-1]]
            return toks

        def norm_T(gcol, arena_free, scr=30720):
            xs = ar(scr, 2, 1024)
            for t in range(2):
                act(xs[:, t, :], X[:, t, :], ACT.Square, *arena_free, accum_out=SM[:, t:t + 1])
            r = rstd(SM[:, 0:2], 1024, P.last("A"), *arena_free)
            for t in range(2):
                x_tok = ts(xs[:, t, :], X[:, t, :], SM[:, t:t + 1], None, ALU.mult, None, r)
            return transposed_split(lambda t, k: xs[:, t, k * 128:k * 128 + 128], [x_tok],
                                    gain=lambda k: PVT[:, gcol + k:gcol + k + 1])

        def three(o, a, b, first, last, *waits):
            mm(lambda e: e.matmul(o, a[0], b[0], start=first, stop=False), *waits)
            mm(lambda e: e.matmul(o, a[0], b[1], start=False, stop=False))
            return mm(lambda e: e.matmul(o, a[1], b[0], start=False, stop=last), mark=True)

        def pump(side, n=1):
            for _ in range(n if side is not None else 0):
                next(side, None)

        def drain(side):
            for _ in side:
                pass

        def proj_nat(name, k0, src_tok, nk, nblocks, use, c0=0, side=None, pace=1):
            for nb in range(nblocks):
                banks = [bank(), bank()]
                for kq in range(nk // 2):
                    hi, lo, wt, i = stream_next(name, c0 + nb * (nk // 2) + kq)
                    for t in range(2):
                        b, wb = banks[t]
                        for kk in range(2):
                            k = kq * 2 + kk
                            tok = three(PS[:, b, :], [v[:, k0 + k, t * 128:t * 128 + 128] for v in (XH, XL)],
                                        [v[:, kk * 512:kk * 512 + 512] for v in (hi, lo)],
                                        k == 0, k == nk - 1, wt, *wb, *src_tok)
                    stream_done(i, tok)
                    if kq < nk // 2 - 1:
                        pump(side, pace)
                for t in range(2):
                    b = banks[t][0]
                    free[b] = [use(nb, t, PS[:, b, :], tok)]
                pump(side, pace)

        def proj_T(name, k0, src_tok, nk, pairs, use, c0=0, side=None, pace=1):
            for nb in range(pairs):
                banks = [bank(), bank()]
                for kh in range(nk // 4):
                    hi, lo, wt, i = stream_next(name, c0 + nb * (nk // 4) + kh)
                    for j in range(2):
                        b, wb = banks[j]
                        for kk in range(4):
                            k = kh * 4 + kk
                            o = kk * 256 + j * 128
                            tok = three(PS[:, b, 0:256], [v[:, o:o + 128] for v in (hi, lo)],
                                        [v[:, k0 + k, :] for v in (XH, XL)], k == 0, k == nk - 1, wt, *wb, *src_tok)
                    stream_done(i, tok)
                    if kh < nk // 4 - 1:
                        pump(side, pace)
                for j in range(2):
                    b = banks[j][0]
                    free[b] = [use(2 * nb + j, PS[:, b, 0:256], tok)]
                pump(side, pace)

        def add_x(c, t, ps, tok):
            xv = X[:, t, c * 512:c * 512 + 512]
            return tt(xv, xv, ps, ALU.add, tok)

        def out_proj(name, tok):
            proj_nat(name, 0, tok, 8, 2, add_x)

        c_tok = dma(CST[:, :], d["cst"])
        p_tok = dma(PVT[:, :], d["pv"])
        x_tok = dma(X[:, :, :], d["x"].rearrange("(t p) c -> p t c", p=128))
        P.wait("V", c_tok, p_tok, x_tok)
        P.wait("A", c_tok, p_tok, x_tok)
        P.wait("G", c_tok, p_tok, x_tok)
        P.wait("T", c_tok)

        def mixer0():
            Q, F, K, B = ar(0, 4, 256), ar(1024, 4, 256), ar(2048, 4, 256), ar(3072, 4, 256)
            E = [ar(4096, 8, 128), ar(5120, 8, 128)]
            SC, SC2 = ar(6144, 8, 128), ar(7168, 4, 128)
            CA = ar(7680, CA_N)
            VN, OG, U, VG = ar(8832, 2, 512), ar(9856, 2, 512), ar(10880, 2, 512), ar(11904, 2, 512)
            HG, GV = ar(12928, 512), ar(13440, 512)
            GW = ar(13952, 4, 128)
            OC = ar(14464, 2, 1024)
            TMP = ar(18560, 2, 512)
            LB = ar(19584, 8, 4)
            SCR0 = 20480

            ca_tok = dma(CA, d["ca"])
            hg_tok = dma(HG, d["rows"][0:1, RW_HG:RW_HG + 512].to_broadcast([128, 512]))
            gv_tok = dma(GV, d["rows"][0:1, RW_GV:RW_GV + 512].to_broadcast([128, 512]))
            gw_tok = dma(GW, d["gw"].rearrange("p (g t) -> p g t", g=4))
            xn = norm_T(PV_MIX0, [], SCR0)

            L = PVT[:, PV_LB:PV_LB + 12].rearrange("p (r h) -> p r h", r=3)
            m = LB[:, 0, :]
            tt(m, L[:, 0, :], L[:, 1, :], ALU.max)
            tt(m, m, L[:, 2, :], ALU.max)
            tt(LB[:, 1:4, :], L, m.unsqueeze(1).to_broadcast([128, 3, 4]), ALU.subtract)
            ea = act(LB[:, 1:4, :], LB[:, 1:4, :], ACT.Exp, P.last("V"))
            tt(m, LB[:, 1, :], LB[:, 2, :], ALU.add, ea)
            tt(m, m, LB[:, 3, :], ALU.add)
            op("V", lambda e: e.reciprocal(m, m))
            lb, oml = LB[:, 4, :], LB[:, 5, :]
            tt(lb, LB[:, 1, :], m, ALU.mult)
            ts(oml, lb, -1.0, 1.0, ALU.mult, ALU.add)

            def use_qf(blk, ps, tok):
                if blk < 4:
                    return evac(Q[:, blk, :], ps, tok)
                return act(F[:, blk - 4, :], ps, ACT.Sigmoid, tok)
            proj_T("l0_qf", 0, xn, 8, 4, use_qf)
            sig = P.last("A")
            F8, B8, Q8, K8 = (v.rearrange("p h (t s) -> p (h t) s", t=2) for v in (F, B, Q, K))
            masks = CA[:, CA_LV:CA_LV + 1024].bitcast(U32)
            ready = {}

            def recurrence():
                for h in range(4):
                    ts(F[:, h, :], F[:, h, :], oml[:, h:h + 1], lb[:, h:h + 1], ALU.mult, ALU.add, sig)
                k_tok = ts(K, F, -1.0, 1.0, ALU.mult, ALU.add)
                g_tok = act(F, F, ACT.Ln, k_tok)
                yield
                op("V", lambda e: e.memset(SC, 0.0))
                for i in range(8):
                    op("V", lambda e, i=i: e.tensor_tensor_scan(B8[:, i, :], ones, F8[:, i, :], 0.0,
                                                                ALU.mult, ALU.add), g_tok)
                e_read = [None, None]

                def decays(lv):
                    if lv == 0:
                        return K8, Q8, (k_tok, sig)
                    Eb = E[lv % 2]
                    half = 1 << (lv - 1)
                    Bv, Ev, Qv, Kv = (v.rearrange("p s (b w i) -> p (s b) w i", w=2, i=half) if lv < 8 else
                                      v.rearrange("p (h w) i -> p h w i", w=2) for v in (B8, Eb, Q8, K8))
                    n = 1024 // (2 * half)
                    mid = Bv[:, :, 0, half - 1:half].to_broadcast([128, n, half])
                    if lv < 8:
                        tt(Ev[:, :, 1, :], Bv[:, :, 1, :], mid, ALU.subtract, e_read[lv % 2])
                    else:
                        cp(Ev[:, :, 1, :], Bv[:, :, 1, :], e_read[lv % 2])
                    d_ = tt(Ev[:, :, 0, :], mid, Bv[:, :, 0, :], ALU.subtract)
                    x_ = act(Eb, Eb, ACT.Exp, d_)
                    tt(Ev[:, :, 1, :], Ev[:, :, 1, :], Qv[:, :, 1, :], ALU.mult, x_)
                    e_tok = tt(Ev[:, :, 0, :], Ev[:, :, 0, :], Kv[:, :, 0, :], ALU.mult)
                    return Eb, Eb, (e_tok,)

                def level(lv, lhs, rhs, e_tok):
                    for hh in range(2 if lv < 8 else 1):
                        b, wb = bank("side")
                        for i in range(4):
                            a_, b_ = (hh * 4 + i,) * 2 if lv < 8 else (2 * i, 2 * i + 1)
                            s_tok = mm(lambda e, b=b, i=i, a_=a_, b_=b_: e.matmul(
                                PS[:, b, i * 128:i * 128 + 128], lhs[:, a_, :], rhs[:, b_, :],
                                start=True, stop=True), *e_tok, *wb, mark=(i == 3))
                        ps = PS[:, b, :].rearrange("p (i t) -> p i t", i=4)
                        if lv == 8:
                            r = cp(SC2, ps, s_tok)
                        else:
                            mk = masks[:, lv * 128:lv * 128 + 128].unsqueeze(1).to_broadcast([128, 4, 128])
                            r = op("V", lambda e, mk=mk, ps=ps, hh=hh: e.copy_predicated(
                                SC[:, hh * 4:hh * 4 + 4, :], mk, ps), s_tok, ca_tok)
                        free[b] = [r]
                    e_read[lv % 2] = s_tok
                    return r
                yield
                nxt = decays(0)
                for lv in range(9):
                    cur = nxt
                    if lv < 8:
                        nxt = decays(lv + 1)
                        yield
                    ready["sc"] = level(lv, *cur)
            side = recurrence()

            def use_rest(nb, t, ps, tok):
                return evac((VN, OG, U, VG)[nb][:, t, :], ps, tok)
            proj_nat("l0_nat", 0, xn, 8, 4, use_rest, side=side)
            drain(side)
            sc_tok = ready["sc"]
            for v, f in ((VN, ACT.Silu), (OG, ACT.Silu), (U, ACT.Gelu_apprx_tanh), (VG, ACT.Gelu_apprx_tanh)):
                rest = act(v, v, f, P.last("V"))

            for t in range(2):
                b, wb = bank()
                for h in range(4):
                    o = PS[:, b, h * 128:h * 128 + 128]
                    tok = mm(lambda e, h=h, t=t, o=o: e.matmul(
                        o, SC[:, 2 * h + t, :], VN[:, t, h * 128:h * 128 + 128], start=True, stop=(t == 0)),
                        sc_tok, rest, *wb, mark=True)
                    if t == 1:
                        tok = mm(lambda e, h=h, o=o: e.matmul(
                            o, SC2[:, h, :], VN[:, 0, h * 128:h * 128 + 128], start=False, stop=True), mark=True)
                free[b] = [cp(OC[:, t, 0:512], PS[:, b, :], tok)]
            o4 = OC[:, :, 0:512].rearrange("p t (h v) -> p t h v", h=4)
            tmp4 = TMP.rearrange("p t (h v) -> p t h v", h=4)

            def group_norm(dst, src, gain, *waits):
                ss = SM[:, 8:16].rearrange("p (t h) -> p t h", t=2)
                tt(tmp4, src, src, ALU.mult, *waits)
                op("V", lambda e: e.tensor_reduce(ss, tmp4, AX, ALU.add))
                rstd(SM[:, 8:16], 128)
                tt(dst, src, ss.unsqueeze(3).to_broadcast([128, 2, 4, 128]), ALU.mult)
                g = gain.rearrange("p (h v) -> p h v", h=4)
                for t in range(2):
                    r = tt(dst[:, t], dst[:, t], g, ALU.mult, hg_tok, gv_tok)
                return r
            group_norm(o4, o4, HG)
            tt(OC[:, :, 0:512], OC[:, :, 0:512], OG, ALU.mult, rest)

            v4 = VG.rearrange("p t (h v) -> p t h v", h=4)
            group_norm(v4, v4, GV)
            tri = CA[:, CA_TRI:CA_TRI + 128]
            gw_ready = tt(GW, GW, tri.unsqueeze(1).to_broadcast([128, 4, 128]), ALU.mult, gw_tok)
            for t in range(2):
                b, wb = bank()
                for g in range(4):
                    tok = mm(lambda e, g=g, t=t, b=b: e.matmul(
                        PS[:, b, g * 128:g * 128 + 128], GW[:, g, :], VG[:, t, g * 128:g * 128 + 128],
                        start=True, stop=True), gw_ready, *wb, mark=(g == 3))
                for g in range(4):
                    r = stt(OC[:, t, 512 + g * 128:640 + g * 128], PS[:, b, g * 128:g * 128 + 128],
                            PVT[:, PV_BS + g:PV_BS + g + 1], U[:, t, g * 128:g * 128 + 128], ALU.add, ALU.mult, tok)
                free[b] = [r]
            out_proj("l0_wout", transposed_split(lambda t, k: OC[:, t, k * 128:k * 128 + 128], [P.last("V")]))

        def peer(l):
            G = AR[:, :].rearrange("p (e t) -> p e t", t=256)
            KEYS, SMALL = ar(20480, 2048), 22528
            S = ar(24576, 2, 2048)
            QT = ar(28672, 16, 256)
            CD, OH = ar(28672, 2048), ar(30720, 2048)
            SV, SI, SF = (ar(SMALL + i * 256, 16, 16) for i in range(3))
            TS, TC, HI, HF = ar(SMALL + 768, 8, 16), ar(SMALL + 896, 128), ar(SMALL + 1024, 128), ar(SMALL + 1152, 128)
            TK = ar(SMALL + 1280, 3, 128)
            before = everything()
            keys_tok = dma(KEYS, d[f"l{l}_keys"], *before)
            xn = norm_T((PV_FFN0, PV_FFN1)[l], before)
            name = f"l{l}_"

            proj_T(name + "wq", 0, xn, 8, 8, lambda blk, ps, tok: evac(QT[:, blk, :], ps, tok))
            q_tok = [P.last("V"), P.last("A")]
            for t in range(2):
                for j0 in range(0, 16, 4):
                    b, wb = bank("side")
                    for j in range(j0, j0 + 4):
                        q_read = mm(lambda e, b=b, j=j, t=t: e.matmul(
                            PS[:, b, (j % 4) * 128:(j % 4) * 128 + 128], QT[:, j, t * 128:t * 128 + 128],
                            KEYS[:, j * 128:j * 128 + 128], start=True, stop=True), keys_tok, *q_tok, *wb,
                            mark=(j == j0 + 3))
                    free[b] = [act(S[:, t, j0 * 128:j0 * 128 + 512], PS[:, b, :], ACT.Copy, q_read)]
            s_tok = P.last("A")
            tk_read = []

            def top16(v, i, src, *waits):
                for r in range(2):
                    v8, i8 = v[:, r * 8:r * 8 + 8], i[:, r * 8:r * 8 + 8].bitcast(U32)
                    op("V", lambda e, v8=v8: e.max(v8, src), *waits)
                    op("V", lambda e, v8=v8, i8=i8: e.max_index(i8, v8, src))
                    if r == 0:
                        op("V", lambda e, v8=v8: e.match_replace(src, v8, src, FILL))

            def select(t):
                for j in range(16):
                    top16(SV[:, j, :], SI[:, j, :], S[:, t, j * 128:j * 128 + 128], s_tok)
                    yield
                cp(SF, SI.bitcast(U32))
                sv = SV.rearrange("p (h q) k -> p h q k", q=2)
                sf = SF.rearrange("p (h q) k -> p h q k", q=2)
                cd = CD.rearrange("p (h a b) -> p h a b", h=8, a=16)
                tc = TC.rearrange("p (h k) -> p h k", h=8)
                for h in range(8):
                    tt(cd[:, h], sv[:, h, 0, :].unsqueeze(2).to_broadcast([128, 16, 16]),
                       sv[:, h, 1, :].unsqueeze(1).to_broadcast([128, 16, 16]), ALU.add, q_read)
                    top16(TS[:, h, :], tc[:, h, :], CD[:, h * 256:h * 256 + 256])
                    yield
                gt = TK[:, 2, :].rearrange("p (h k) -> p h k", h=8)
                x_ = tt(gt, TS, TS[:, :, 0:1].to_broadcast([128, 8, 16]), ALU.subtract, *tk_read)
                x_ = act(TK[:, 2, :], TK[:, 2, :], ACT.Exp, x_)
                for which in range(2):
                    if which == 0:
                        ts(HI.bitcast(U32), TC.bitcast(U32), 4, None, ALU.logical_shift_right)
                    else:
                        ts(HI.bitcast(U32), TC.bitcast(U32), 15, None, ALU.bitwise_and)
                    cp(HF, HI.bitcast(U32))
                    oh = OH.rearrange("p (a b) -> p a b", b=16)
                    tt(oh, HF.unsqueeze(2).to_broadcast([128, 128, 16]),
                       iota[:, 0:16].unsqueeze(1).to_broadcast([128, 128, 16]), ALU.is_equal)
                    yield
                    oh4 = OH.rearrange("p (h k j) -> p h k j", h=8, k=16)
                    for h in range(8):
                        tt(oh4[:, h], oh4[:, h], sf[:, h, which, :].unsqueeze(1).to_broadcast([128, 16, 16]), ALU.mult)
                        if h == 3:
                            yield
                    yield
                    op("V", lambda e, which=which, oh=oh: e.tensor_reduce(TK[:, which, :], oh, AX, ALU.add))
                    yield
                op("V", lambda e: e.tensor_reduce(SM[:, 16:24], gt, AX, ALU.add), x_)
                op("V", lambda e: e.reciprocal(SM[:, 16:24], SM[:, 16:24]))
                tok = tt(gt, gt, SM[:, 16:24].unsqueeze(2).to_broadcast([128, 8, 16]), ALU.mult)
                yield
                yield
                b, wb = bank("side")
                for i in range(3):
                    tp = mm(lambda e, i=i, b=b: e.transpose(PS[:, b, i * 128:i * 128 + 128], TK[:, i, :], ident),
                            tok, *wb, mark=(i == 2))
                tk_read[:] = [tp]
                free[b] = [cp(IT[:, :, t * 128:t * 128 + 128],
                              PS[:, b, 0:384].rearrange("p (i t) -> p i t", i=3), tp)]
                yield

            slots = [None, None]

            def spread(half):
                held = []

                def fold(q, b, tok):
                    g = G[:, 64 * half:64 * half + 64, 4 * q:4 * q + 4]
                    free[b] = [tt(g, PS[:, b, 0:256].rearrange("p (t i) -> p i t", t=4), g, ALU.mult, tok, gelu_tok[half],
                                  loose=True)]
                it_tok = P.last("V")
                for q in range(64):
                    a1 = OA[:, q % 2, :].rearrange("p (t i) -> p t i", t=4)
                    b1 = OB[:, q % 2, :].rearrange("p (t i) -> p t i", t=4)
                    tt(a1, iota[:, 64 * half:64 * half + 64].unsqueeze(1).to_broadcast([128, 4, 64]),
                       IT[:, 0, 4 * q:4 * q + 4].unsqueeze(2).to_broadcast([128, 4, 64]), ALU.is_equal,
                       it_tok, slots[q % 2], loose=True)
                    for j in range(4):
                        t = 4 * q + j
                        bv = ts(b1[:, j, :], iota, IT[:, 1, t:t + 1], IT[:, 2, t:t + 1], ALU.is_equal, ALU.mult,
                                it_tok, slots[q % 2], loose=True)
                    if held:
                        q0, av0, bv0, a0, b0 = held.pop()
                        products(fold, q0, av0, bv0, a0, b0)
                    held.append((q, bv, bv, a1, b1))
                    yield
                q0, av0, bv0, a0, b0 = held.pop()
                products(fold, q0, av0, bv0, a0, b0)
                yield

            def products(fold, q, av, bv, a1, b1):
                b, wb = bank("side")
                for j in range(4):
                    tok = mm(lambda e, j=j: e.matmul(PS[:, b, j * 64:j * 64 + 64], b1[:, j, :], a1[:, j, :],
                                                     start=True, stop=True), bv, *wb, mark=(j == 3))
                slots[q % 2] = tok
                fold(q, b, tok)

            gelu_tok = [None, None]

            def downs():
                yield from select(0)
                yield from select(1)
                gelu_tok[0] = tail_tok[0] = P.last("V")
            tail_tok = [None]
            side = downs()
            low = None
            for c in range(128):
                hi, lo, wt, i = stream_next(name + "down", c)
                if c % 2 == 0:
                    b, wb = bank()
                o = PS[:, b, (c % 2) * 256:(c % 2) * 256 + 256]
                for k in range(8):
                    tok = three(o, [v[:, k * 128:k * 128 + 128] for v in (hi, lo)], [v[:, k, :] for v in (XH, XL)],
                                k == 0, k == 7, wt, *wb, *xn)
                stream_done(i, tok)
                if c % 2:
                    if c >= 80 and tail_tok[0] is None:
                        drain(side)
                    free[b] = [act(G[:, c - 1:c + 1, :], PS[:, b, :].rearrange("p (j t) -> p j t", j=2),
                                   ACT.Gelu_apprx_tanh, tok, *before, tail_tok[0])]
                    if c == 63:
                        lower_gelu = free[b][0]
                pump(side)
                if tail_tok[0] is not None and c >= 64:
                    if low is None:
                        gelu_tok[0] = lower_gelu
                        low = spread(0)
                    pump(low, 2 if c % 2 else 1)
            if low is None:
                drain(side)
                gelu_tok[0] = lower_gelu
                low = spread(0)
            drain(low)
            gelu_tok[1] = P.last("A")

            split_tok, split_free = {}, {}

            def split_g(p):
                if p < 64:
                    g = G[:, 2 * p:2 * p + 2, :].rearrange("p e t -> p (e t)")
                    ht = act(GH[:, p % 2, :], g, ACT.Copy, fold_tok[p // 32], split_free.get(p - 2))
                    split_tok[p] = tt(GL_[:, p % 2, :], g, GH[:, p % 2, :], ALU.subtract, ht)
            fold_tok = [P.last("V"), None]
            split_g(0)
            pools.update(main=[4, 5, 6, 7], side=[0, 1, 2, 3])
            acc = [bank() for _ in range(4)]
            high = spread(1)
            for c in range(128):
                hi, lo, wt, i = stream_next(name + "up", c)
                p, j = divmod(c, 2)
                if j == 0:
                    if c == 62:
                        drain(high)
                        fold_tok[1] = P.last("V")
                    split_g(p + 1)
                for t in range(2):
                    for h in range(2):
                        b, wb = acc[2 * t + h]
                        tok = three(PS[:, b, :], [v[:, p % 2, j * 256 + t * 128:j * 256 + t * 128 + 128] for v in (GH, GL_)],
                                    [v[:, h * 512:h * 512 + 512] for v in (hi, lo)], c == 0, c == 127,
                                    wt, *wb, split_tok[p])
                stream_done(i, tok)
                split_free[p] = tok
                pump(high, 1 if c % 8 else 2)
            for t in range(2):
                for h in range(2):
                    b = acc[2 * t + h][0]
                    xv = X[:, t, h * 512:h * 512 + 512]
                    free[b] = [tt(xv, xv, PS[:, b, :], ALU.add, tok)]
            pools.update(main=[0, 1, 2, 3], side=[4, 5, 6, 7])

        def seg_norm(v, tmp, ss, n, gain, *waits):
            m = v.shape[1]
            tt(tmp, v, v, ALU.mult, *waits)
            op("V", lambda e: e.tensor_reduce(ss, tmp, AX, ALU.add))
            rstd(ss, n)
            r = tt(v, v, ss.unsqueeze(2).to_broadcast([128, m, n]), ALU.mult)
            if gain is not None:
                r = tt(v, v, gain.unsqueeze(1).to_broadcast([128, m, n]), ALU.mult)
            return r

        def mixer1():
            Z = ar(0, 2, 2048)
            CQT, CKT = ar(4096, 2, 256), ar(4608, 1, 256)
            QC, KV, KC = ar(4864, 2, 768), ar(6400, 2, 1024), ar(8448, 2, 768)
            SN, CS, AN, RR = ar(9984, 2, 32), ar(10048, 2, 32), ar(10112, 2, 32), ar(10176, 2, 32)
            GN = ar(10240, 640)
            QN, QR, KN, KR, QD, KD = (ar(10880 + i * 1024, 4, 256) for i in range(6))
            PB = [ar(17024 + i * 384, 384) for i in range(3)]
            PT = [ar(18176 + i * 384, 3, 128) for i in range(2)]
            O = ar(18944, 2, 1024)
            TMP = ar(23040, 1536)
            CB = ar(24576, CB_N)
            UQ, UKV = ar(25600, 2, 768), ar(27136, 1024)
            SS, MX, SU = SM[:, 24:32], SM[:, 32:48], SM[:, 48:80]
            before = everything()
            gn_tok = dma(GN, d["rows"][0:1, RW_MQ:RW_MQ + 640].to_broadcast([128, 640]), *before)
            cb_tok = dma(CB, d["cb"], *before)
            ps_i = AR[:, 25088:25090].bitcast(I32)
            ip_tok = dma(ps_i, d["pos"], *before)
            uq_tok = dma(UQ, d["l1_uq"].rearrange("p (k n) -> p k n", k=2), *before)
            ukv_tok = dma(UKV, d["l1_ukv"], *before)
            xn = norm_T(PV_MIX1, before)
            rel_table(before)

            pf = AR[:, 25090:25092]
            cp(pf, ps_i, ip_tok)
            inv = CB[:, CB_INV:CB_INV + 32]
            for t in range(2):
                ts(AN[:, t, :], inv, pf[:, t:t + 1], None, ALU.mult, None, cb_tok)
            magic = 12582912.0
            ts(RR, AN, float(np.float32(1.0 / (2 * np.pi))), magic, ALU.mult, ALU.add)
            ts(RR, RR, magic, None, ALU.subtract)
            c1 = 6.28125
            c2 = float(np.float32(2 * np.pi - c1))
            c3 = float(2 * np.pi - c1 - c2)
            for cc in (c1, c2, c3):
                stt(AN, RR, -cc, AN, ALU.mult, ALU.add)
            lim = 3.1415925
            ts(SN, AN, lim, -lim, ALU.min, ALU.max)
            ts(AN, AN, float(np.pi / 2), None, ALU.add)
            ts(RR, AN, lim, -2 * float(np.pi), ALU.is_gt, ALU.mult)
            tt(AN, AN, RR, ALU.add)
            a_tok = ts(CS, AN, lim, -lim, ALU.min, ALU.max)
            act(SN, SN, ACT.Sin, a_tok)
            sc_tok = act(CS, CS, ACT.Sin)

            def use(nb, t, ps, tok):
                return evac(Z[:, t, nb * 512:nb * 512 + 512], ps, tok)
            proj_nat("l1_win", 0, xn, 8, 1, use)
            qk_tok, n_tok = [], []

            def heads_T(dst, src, w, tok):
                for kp in range(0, 4, 2):
                    b, wb = bank("side")
                    for j in range(2):
                        for t in range(2):
                            tp = mm(lambda e, b=b, j=j, t=t, kp=kp: e.transpose(
                                PS[0:w, b, j * 256 + t * 128:j * 256 + t * 128 + 128], src(t, kp + j), ident),
                                tok, *wb, mark=(j == 1 and t == 1))
                    free[b] = [evac(dst[0:w, kp:kp + 2, :], PS[0:w, b, :].rearrange("p (j t) -> p j t", j=2), tp)]
                    qk_tok.append(free[b][0])

            def low_rank():
                z_tok = [P.last("V"), P.last("A")]
                for t in range(2):
                    seg_norm(Z[:, t:t + 1, 0:256], TMP[:, 0:256].unsqueeze(1), SS[:, 0:1], 256, None, *z_tok)
                    r = seg_norm(Z[:, t:t + 1, 256:384], TMP[:, 0:128].unsqueeze(1), SS[:, 0:1], 128, None)
                yield
                cq = transposed(lambda k: CQT[:, k, :], lambda t, k: Z[:, t, k * 128:k * 128 + 128], [r],
                                gain=lambda k: PVT[:, PV_CQ + k:PV_CQ + k + 1], nk=2, pool="side")
                ck = transposed(lambda k: CKT[:, k, :], lambda t, k: Z[:, t, 256:384], [r],
                                gain=lambda k: PVT[:, PV_CKV:PV_CKV + 1], nk=1, pool="side")
                yield
                for t in range(2):
                    for h in range(2):
                        b, wb = bank("side")
                        for k in range(2):
                            tok = mm(lambda e, b=b, t=t, h=h, k=k: e.matmul(
                                PS[:, b, 0:384], CQT[:, k, t * 128:t * 128 + 128],
                                UQ[:, k, h * 384:h * 384 + 384], start=(k == 0), stop=(k == 1)),
                                uq_tok, *cq, *wb, mark=(k == 1))
                        free[b] = [evac(QC[:, t, h * 384:h * 384 + 384], PS[:, b, 0:384], tok)]
                    for h in range(2):
                        b, wb = bank("side")
                        tok = mm(lambda e, b=b, t=t, h=h: e.matmul(
                            PS[:, b, :], CKT[:, 0, t * 128:t * 128 + 128], UKV[:, h * 512:h * 512 + 512],
                            start=True, stop=True), ukv_tok, *ck, *wb, mark=True)
                        free[b] = [evac(KV[:, t, h * 512:h * 512 + 512], PS[:, b, :], tok)]
                e_tok = P.last("A")
                yield
                for t in range(2):
                    cp(kc4[:, t, :, 0:128], kv4[:, t, :, 0:128], e_tok)
                    cp(kc4[:, t, :, 128:192], Z[:, t, 384:448].unsqueeze(1).to_broadcast([128, 4, 64]))
                for v, g in ((QC, GN[:, 0:192]), (KC, GN[:, 192:384])):
                    v8 = v.rearrange("p t (h c) -> p (t h) c", c=192)
                    seg_norm(v8, TMP.rearrange("p (s c) -> p s c", c=192), SS, 192, g, gn_tok)
                    yield
                    for t in range(2):
                        x1, x2 = (v8[:, 4 * t:4 * t + 4, a:a + 32] for a in (128, 160))
                        co, si = (w[:, t, :].unsqueeze(1).to_broadcast([128, 4, 32]) for w in (CS, SN))
                        t1, t2, t3, t4 = (TMP[:, i * 128:i * 128 + 128].rearrange("p (h i) -> p h i", h=4)
                                          for i in range(4))
                        tt(t1, x1, co, ALU.mult, sc_tok)
                        tt(t2, x2, si, ALU.mult)
                        tt(t3, x2, co, ALU.mult)
                        tt(t4, x1, si, ALU.mult)
                        tt(x1, t1, t2, ALU.subtract)
                        r = tt(x2, t3, t4, ALU.add)
                    yield
                heads_T(QN, lambda t, k: q8[:, t, k, 0:128], 128, r)
                heads_T(KN, lambda t, k: kc4[:, t, k, 0:128], 128, r)
                yield
                heads_T(QR, lambda t, k: q8[:, t, k, 128:192], 64, r)
                heads_T(KR, lambda t, k: kc4[:, t, k, 128:192], 64, r)
                yield
            kv4 = KV.rearrange("p t (h c) -> p t h c", h=4)
            kc4 = KC.rearrange("p t (h c) -> p t h c", h=4)
            q8 = QC.rearrange("p t (h c) -> p t h c", h=4)
            side = low_rank()

            def use2(nb, t, ps, tok):
                return use(nb + 1, t, ps, tok)
            proj_nat("l1_win", 0, xn, 8, 3, use2, c0=4, side=side)
            drain(side)
            z2_tok = P.last("A")
            for t in range(2):
                for o, g in ((512, GN[:, 384:512]), (1024, GN[:, 512:640])):
                    r = seg_norm(Z[:, t, o:o + 512].rearrange("p (h c) -> p h c", h=4),
                                 TMP[:, 0:512].rearrange("p (h c) -> p h c", h=4), SS[:, 0:4], 128, g, z2_tok)
            heads_T(QD, lambda t, k: Z[:, t, 512 + k * 128:640 + k * 128], 128, r)
            heads_T(KD, lambda t, k: Z[:, t, 1024 + k * 128:1152 + k * 128], 128, r)

            mask = CB[:, CB_M:CB_M + 384]

            def parts(h):
                if h < 4:
                    return [(QN[:, h], KN[:, h]), (QR[0:64, h], KR[0:64, h])], 192 ** -0.5
                return [(QD[:, h - 4], KD[:, h - 4])], 128 ** -0.5

            def values(h, t):
                if h < 4:
                    return KV[:, t, h * 256 + 128:h * 256 + 256]
                return Z[:, t, 1536 + (h - 4) * 128:1536 + (h - 4) * 128 + 128]
            hd = {}
            pt_read = [None, None]

            def scores(h):
                pp, scale = parts(h)
                b, wb = bank("side")
                for t in range(2):
                    o = PS[:, b, 0:128] if t == 0 else PS[:, b, 128:384]
                    for i, (q, k) in enumerate(pp):
                        tok = mm(lambda e, o=o, q=q, k=k, t=t, i=i: e.matmul(
                            o, q[:, t * 128:t * 128 + 128], k[:, 0:128 * (t + 1)], start=(i == 0),
                            stop=(i == len(pp) - 1)), *qk_tok, *wb, mark=True)
                p = PB[h % 3]
                mx, su = MX[:, 2 * h:2 * h + 2], SU[:, 2 * h:2 * h + 2]
                free[b] = [stt(p, PS[:, b, 0:384], float(scale), mask, ALU.mult, ALU.add, tok,
                               hd[h - 3]["tr"] if h >= 3 else None)]
                op("V", lambda e: e.tensor_reduce(mx[:, 0:1], p[:, 0:128], AX, ALU.max))
                op("V", lambda e: e.tensor_reduce(mx[:, 1:2], p[:, 128:384], AX, ALU.max))
                mt = ts(mx, mx, -1.0, None, ALU.mult)
                act(p[:, 0:128], p[:, 0:128], ACT.Exp, mt, bias=mx[:, 0:1], accum_out=su[:, 0:1])
                et = act(p[:, 128:384], p[:, 128:384], ACT.Exp, bias=mx[:, 1:2], accum_out=su[:, 1:2])
                rt = op("V", lambda e: e.reciprocal(su, su), et)
                hd[h] = {"p": p, "e": et, "r": rt}

            def turn_p(h):
                b, wb = bank("side")
                for i in range(3):
                    tok = mm(lambda e, i=i, b=b, h=h: e.transpose(PS[:, b, i * 128:i * 128 + 128],
                                                                  PB[h % 3][:, i * 128:i * 128 + 128], ident),
                             hd[h]["e"], *wb, mark=(i == 2))
                hd[h]["tr"] = tok
                free[b] = [evac(PT[h % 2], PS[:, b, 0:384].rearrange("p (i q) -> p i q", i=3), tok, pt_read[h % 2])]
                hd[h]["pt"] = free[b][0]

            def weigh(h):
                b, wb = bank("side")
                pt = PT[h % 2]
                mm(lambda e: e.matmul(PS[:, b, 0:128], pt[:, 0, :], values(h, 0), start=True, stop=True),
                   hd[h]["pt"], *wb)
                mm(lambda e: e.matmul(PS[:, b, 128:256], pt[:, 1, :], values(h, 0), start=True, stop=False))
                tok = mm(lambda e: e.matmul(PS[:, b, 128:256], pt[:, 2, :], values(h, 1), start=False, stop=True), mark=True)
                pt_read[h % 2] = tok
                for t in range(2):
                    free[b] = [evac(O[:, t, h * 128:h * 128 + 128], PS[:, b, t * 128:t * 128 + 128], tok, hd[h]["r"],
                                    scale=SU[:, 2 * h + t:2 * h + t + 1], eng="VA"[h % 2])]
            for i in range(10):
                if i < 8:
                    scores(i)
                if 1 <= i < 9:
                    turn_p(i - 1)
                if i >= 2:
                    weigh(i - 2)
            out_proj("l1_wout", transposed_split(lambda t, k: O[:, t, k * 128:k * 128 + 128],
                                                 [P.last("V"), P.last("A")]))

        def rel_table(before):
            OHB, NG, RB, R = ar(28160, 512), ar(28672, 512), ar(29184, 24), ar(29312, 512)
            a = dma(AR[0:32, 28160:29184], d["cd"], *before)
            r = dma(AR[0:32, 29184:29208], d["rel"], *before)
            b, wb = bank("side")
            tok = mm(lambda e: e.matmul(PS[0:24, b, 0:511], RB[0:32, :], OHB[0:32, 0:511], start=True, stop=True),
                     a, r, *wb, mark=True)
            free[b] = [tt(R[0:24, 0:511], PS[0:24, b, 0:511], NG[0:24, 0:511], ALU.add, tok, a)]
            rel_tok[0] = dma(scr[:, 0:511], R[0:24, 0:511], free[b][0])

        def block2():
            QT, KT = ar(0, 12, 256), ar(3072, 12, 256)
            VN = ar(6144, 2, 1536)
            AI, SAG, BGT = ar(9216, 2, 512), ar(10240, 4, 256), ar(11264, 4, 256)
            GT = ar(12288, 16, 256)
            SK = ar(16384, 24, 384)
            PG = ar(25600, 2, 1024)
            SB = [ar(27648 + 768 * i, 768) for i in range(3)]
            PT = [ar(29952 + 768 * i, 768) for i in range(2)]
            WP = ar(31488, 4, 128)
            PT4 = ar(27648, 4, 256)
            MIX = ar(9216, 4, 256)
            ATT = ar(25600, 2, 512)
            MG, YB, FG, SQ = ar(0, 8, 256), ar(2048, 2, 256), ar(3072, 1024), ar(4096, 2, 1024)
            before = everything()
            pg_tok = dma(AR[:, 25600:27648], d["cc"], *before)
            wp_tok = dma(WP, d["wpool"].rearrange("p (g t) -> p g t", g=4), *before)
            sk_tok = dma(SK, bass.AP(scr, 0, [[1, 128], [512, 24], [1, 384]]), *before, rel_tok[0])
            xn = norm_T(PV_MIX2, before, 0)

            proj_nat("w2_a", 0, xn, 8, 1, lambda nb, t, ps, tok: evac(AI[:, t, :], ps, tok))

            def pooling():
                a_tok = [P.last("V"), P.last("A")]
                for g in range(0, 4, 2):
                    b, wb = bank("side")
                    for j in range(2):
                        for t in range(2):
                            tok = mm(lambda e, b=b, j=j, t=t, g=g: e.matmul(
                                PS[:, b, j * 256:j * 256 + 256], AI[:, t, (g + j) * 128:(g + j) * 128 + 128],
                                PG[:, t, (g + j) * 256:(g + j) * 256 + 256], start=(t == 0), stop=(t == 1)),
                                pg_tok, *a_tok, *wb, mark=(j == 1 and t == 1))
                    free[b] = [evac(PT4[:, g:g + 2, :], PS[:, b, :].rearrange("p (j t) -> p j t", j=2), tok, eng="V")]
                yield
                yield
                p_tok = P.last("V")
                for g in range(0, 4, 2):
                    b, wb = bank("side")
                    for j in range(2):
                        tok = mm(lambda e, b=b, j=j, g=g: e.matmul(
                            PS[:, b, j * 256:j * 256 + 256], WP[:, g + j, :], PT4[:, g + j, :], start=True, stop=True),
                            p_tok, wp_tok, *wb, mark=(j == 1))
                    free[b] = [evac(MIX[:, g:g + 2, :], PS[:, b, :].rearrange("p (j t) -> p j t", j=2), tok, eng="V")]
                pool_read[0] = P.last("T")
                yield
            pool_read = [None]
            side = pooling()

            def use_qk(blk, ps, tok):
                if blk < 12:
                    return evac(QT[:, blk, :].rearrange("p (t q) -> p t q", t=2),
                                ps.rearrange("p (t q) -> p t q", t=2)[:, :, ::-1], tok, eng="V")
                return evac(KT[:, blk - 12, :], ps, tok, eng="A")
            proj_T("w2_qk", 0, xn, 8, 12, use_qk, side=side)
            drain(side)
            proj_nat("w2_v", 0, xn, 8, 3, lambda nb, t, ps, tok: evac(VN[:, t, nb * 512:nb * 512 + 512], ps, tok))
            z_tok = [P.last("V"), P.last("A")]

            hd = {}
            pt_read = [None, None]
            pair = [0]

            def two_banks():
                b = 4 + 2 * (pair[0] % 2)
                pair[0] += 1
                return b, [*free[b], *free[b + 1]]
            MX, SU = SM[:, 80:96], SM[:, 96:112]

            def scores(i):
                h, t = divmod(i, 2)
                b, wb = two_banks()
                sp = PS[:, b:b + 2, :].rearrange("p a n -> p (a n)")[:, 0:768]
                pb = (h % 2) * 64
                for g in range(3):
                    nb = g * 4 + h // 2
                    tok = mm(lambda e, g=g, nb=nb, sp=sp: e.matmul(
                        sp[:, g * 256:g * 256 + 256], QT[pb:pb + 64, nb, t * 128:t * 128 + 128],
                        KT[pb:pb + 64, nb, :], start=True, stop=True), *z_tok, *wb, mark=(g == 2))
                s_ = SB[i % 3]
                sk = SK.rearrange("p (g h) j -> p g h j", g=3)[:, :, h, 128 * (1 - t):128 * (1 - t) + 256]
                r = stt(s_.rearrange("p (g k) -> p g k", g=3), sp.rearrange("p (g k) -> p g k", g=3), 0.125, sk,
                        ALU.mult, ALU.add, tok, sk_tok, pool_read[0], hd[i - 3]["tr"] if i >= 3 else None)
                free[b], free[b + 1] = [r], [r]
                mx = MX[:, i:i + 1]
                mt = op("V", lambda e: e.tensor_reduce(mx, s_, AX, ALU.max, negate=True))
                et = act(s_, s_, ACT.Exp, mt, bias=mx, accum_out=SU[:, i:i + 1])
                hd[i] = {"e": et}

            def turn_p(i):
                b, wb = two_banks()
                sp = PS[:, b:b + 2, :].rearrange("p a n -> p (a n)")[:, 0:768]
                for j in range(6):
                    tok = mm(lambda e, j=j, sp=sp: e.transpose(sp[:, j * 128:j * 128 + 128],
                                                               SB[i % 3][:, j * 128:j * 128 + 128], ident),
                             hd[i]["e"], *wb, mark=(j == 5))
                hd[i]["tr"] = tok
                r = evac(PT[i % 2], sp, tok, pt_read[i % 2], eng="A")
                free[b], free[b + 1] = [r], [r]
                hd[i]["pt"] = r
                hd[i]["r"] = op("V", lambda e: e.reciprocal(SU[:, i:i + 1], SU[:, i:i + 1]), hd[i]["e"])

            def weigh(i):
                h, t = divmod(i, 2)
                b, wb = two_banks()
                for j in range(6):
                    g, kt = divmod(j, 2)
                    tok = mm(lambda e, j=j, g=g, kt=kt: e.matmul(
                        PS[:, b, 0:64], PT[i % 2][:, j * 128:j * 128 + 128],
                        VN[:, kt, g * 512 + h * 64:g * 512 + h * 64 + 64], start=(j == 0), stop=(j == 5)),
                        hd[i]["pt"], *wb, mark=(j == 5))
                pt_read[i % 2] = tok
                r = evac(ATT[:, t, h * 64:h * 64 + 64], PS[:, b, 0:64], tok, hd[i]["r"], scale=SU[:, i:i + 1], eng="V")
                free[b], free[b + 1] = [r], [r]

            def attention():
                for i in range(18):
                    if i >= 2:
                        weigh(i - 2)
                    if 1 <= i < 17:
                        turn_p(i - 1)
                    if i < 16:
                        scores(i)
                    yield

            def use_gates(blk, ps, tok):
                if blk < 8:
                    return evac((SAG if blk < 4 else BGT)[:, blk % 4, :], ps, tok)
                bg = PVT[:, PV_BG + blk - 8:PV_BG + blk - 7]
                if turn_engine() == "V":
                    return ts(GT[:, blk - 8, :], ps, bg, None, ALU.add, None, tok)
                return act(GT[:, blk - 8, :], ps, ACT.Identity, tok, bias=bg)
            side = attention()
            proj_T("w2_gates", 0, xn, 8, 12, use_gates, side=side)
            drain(side)
            g_tok = P.last("V")
            act(SAG, SAG, ACT.Silu, g_tok)
            sb_tok = act(BGT, BGT, ACT.Silu)
            gt_tok = act(GT, GT, ACT.Sigmoid)
            xn_read = P.last("T")

            def parts(k, v, tok, *waits):
                ht = act(XH[:, k:k + 2, :], v, ACT.Copy, tok, *waits)
                return tt(XL[:, k:k + 2, :], v, XH[:, k:k + 2, :], ALU.subtract, ht)
            for g in range(4):
                r = stt(MIX[:, g, :], MIX[:, g, :], PVT[:, PV_PS + g:PV_PS + g + 1], SAG[:, g, :], ALU.mult, ALU.mult, sb_tok)
            ya_tok = [parts(k, MIX[:, k:k + 2, :], r, xn_read) for k in (0, 2)]
            att = P.last("V")
            bt_tok = []
            for nb in range(0, 4, 2):
                b, wb = bank()
                for j in range(2):
                    for t in range(2):
                        tok = mm(lambda e, b=b, j=j, t=t, nb=nb: e.transpose(
                            PS[:, b, j * 256 + t * 128:j * 256 + t * 128 + 128],
                            ATT[:, t, (nb + j) * 128:(nb + j) * 128 + 128], ident), att, *wb, mark=(j == 1 and t == 1))
                v = BGT[:, nb:nb + 2, :]
                r = tt(v.rearrange("p j (t q) -> p (j t) q", t=2),
                       PS[:, b, :].rearrange("p (j q) -> p j q", j=4)[:, :, ::-1],
                       v.rearrange("p j (t q) -> p (j t) q", t=2), ALU.mult, tok, sb_tok)
                free[b] = [r]
                bt_tok.append(parts(4 + nb, v, r, xn_read))

            fg_tok = dma(FG, d["rows"][0:1, RW_FG:RW_FG + 1024].to_broadcast([128, 1024]), *everything())
            mg_free = P.last("T")

            def use_a(blk, ps, tok):
                return tt(MG[:, blk, :], ps, GT[:, blk, :], ALU.mult, tok, gt_tok, mg_free)

            def use_b(blk, ps, tok):
                r_ = tt(YB[:, blk % 2, :], ps, GT[:, 8 + blk, :], ALU.mult, tok, mg_free)
                tt(MG[:, blk, :], MG[:, blk, :], YB[:, blk % 2, :], ALU.add)
                return r_
            proj_T("w_pa", 0, ya_tok, 4, 4, use_a)
            proj_T("w_pb", 4, bt_tok, 4, 4, use_b)
            m_tok, b_read = P.last("V"), P.last("T")
            out_proj("w_out2", [parts(k, MG[:, k:k + 2, :], m_tok, b_read) for k in (0, 2, 4, 6)])

            x_ = P.last("V")
            for t in range(2):
                act(SQ[:, t, :], X[:, t, :], ACT.Square, x_, accum_out=SM[:, t:t + 1])
            rstd(SM[:, 0:2], 1024, P.last("A"))
            for t in range(2):
                stt(X[:, t, :], X[:, t, :], SM[:, t:t + 1], FG, ALU.mult, ALU.mult, fg_tok)

        rel_tok = [None]
        stages = [mixer0, lambda: peer(0), mixer1, lambda: peer(1), block2]
        for st in stages[:upto]:
            st()
        o_tok = dma(out.rearrange("(t p) c -> p t c", p=128), X[:, :, :], *everything())
        P.wait("S", o_tok)

        block = ctx.enter_context(nc.Block())

        @block.sync
        def _(eng):
            P.emit("S", eng)

        @block.gpsimd
        def _(eng):
            P.emit("G", eng)

        @block.scalar
        def _(eng):
            P.emit("A", eng)

        @block.tensor
        def _(eng):
            P.emit("T", eng)

        @block.vector
        def _(eng):
            P.emit("V", eng)


def _constants():
    p = np.arange(128)
    cst = np.zeros((128, C_N0), np.float32)
    cst[:, C_ID:C_ID + 128] = np.eye(128)
    cst[:, C_IOTA:C_IOTA + 128] = p[None, :]
    cst[:, C_ONE:C_ONE + 128] = 1
    ca = np.zeros((128, CA_N), np.float32)
    s, t = p[:, None], p[None, :]
    for lv in range(8):
        m = s == t if lv == 0 else (s >> lv == t >> lv) & ((s >> (lv - 1)) & 1 == 0) & ((t >> (lv - 1)) & 1 == 1)
        ca[:, CA_LV + lv * 128:CA_LV + lv * 128 + 128] = m
    ca[:, CA_TRI:CA_TRI + 128] = s <= t
    cb = np.zeros((128, CB_N), np.float32)
    tri = np.where(t <= s, 0, NBIG)
    cb[:, CB_M:CB_M + 128] = tri
    cb[:, CB_M + 256:CB_M + 384] = tri
    cb[:, CB_INV:CB_INV + 32] = (np.float32(10000.0) ** (-np.arange(32, dtype=np.float32) / np.float32(32)))[None, :]
    pool = np.zeros((256, 4, 256), np.float32)
    for g, w in enumerate((2, 4, 8, 16)):
        for q in range(256):
            lo, hi = max(q - w // 2, 0), min(q + w // 2 - 1, 255)
            pool[lo:hi + 1, g, q] = np.float32(1) / np.float32(hi - lo + 1)
            pool[q, g, q] -= 1
    cc = pool.reshape(2, 128, 4, 256).transpose(1, 0, 2, 3).reshape(128, 2048)
    cd = np.zeros((32, CD_N), np.float32)
    rel = np.arange(511) - 255
    n = np.abs(rel)
    large = 8 + (np.log(np.maximum(n, 1).astype(np.float32) / np.float32(8)) / np.float32(np.log(128.0))
                 * np.float32(8)).astype(np.int32)
    bucket = (rel > 0) * 16 + np.where(n < 8, n, np.minimum(large, 15))
    cd[bucket, CD_OH + np.arange(511)] = 1
    for g, dil in enumerate((1, 4, 16)):
        bad = (rel % dil != 0) | (n > 64 * dil)
        cd[g * 8:g * 8 + 8, CD_NG:CD_NG + 511] = np.where(bad, NBIG, 0)[None, :]
    return dict(cst=cst, ca=ca, cb=cb, cc=np.ascontiguousarray(cc), cd=cd)


def _layout(i):
    def cols(v):
        return v.reshape(-1, 128).T

    def chunks(w, k, n):
        r, c = w.shape[0] // (128 * k), w.shape[1] // n
        return np.ascontiguousarray(
            w.reshape(r, k, 128, c, n).transpose(3, 0, 2, 1, 4).reshape(c * r, 128, k * n))
    a = _constants()
    a["x"] = np.ascontiguousarray(i["x"][0])
    a["pos"] = np.ascontiguousarray(i["positions"].reshape(2, 128).T.astype(np.int32))
    lb = i["lb_logits"].reshape(3, 4, 128).transpose(2, 0, 1).reshape(128, 12)
    a["pv"] = np.ascontiguousarray(np.concatenate(
        [cols(i[n]) for n in ("l0_norm_mix", "l0_norm_ffn", "l1_norm_mix", "l1_norm_ffn")]
        + [cols(i["norm_gain_2"][0]), cols(i["l1_mla_cq_norm"]), cols(i["l1_mla_ckv_norm"]), lb,
           i["l0_gmlp_b_s"].T, cols(i["pool_scale_2"][0]), cols(i["b_gate_2"][0].reshape(-1))], axis=1))
    a["rows"] = np.concatenate([i[n].reshape(1, -1) for n in (
        "l0_hgrn_out_norm", "l0_gmlp_v_norm", "l1_mla_q_norm", "l1_mla_k_norm", "l1_moba_q_norm", "l1_moba_k_norm",
        "final_gain_2")], axis=1)
    a["gw"] = np.ascontiguousarray(i["l0_gmlp_w_s"].transpose(2, 0, 1).reshape(128, 512))
    nat, trn = (2, 512), (4, 256)
    w = i["l0_w_in"]
    a["l0_qf"] = chunks(w[:, :1024], *trn)
    a["l0_nat"] = chunks(w[:, 1024:], *nat)
    a["l0_wout"] = chunks(i["l0_w_out"], *nat)
    w = i["l1_w_in"]
    a["l1_win"] = chunks(np.concatenate([w[:, :448], np.zeros((1024, 64), w.dtype), w[:, 448:]], axis=1), *nat)
    a["l1_uq"] = np.ascontiguousarray(i["l1_mla_w_uq"].reshape(2, 128, 768).transpose(1, 0, 2).reshape(128, 1536))
    a["l1_ukv"] = np.ascontiguousarray(i["l1_mla_w_ukv"])
    a["l1_wout"] = chunks(i["l1_w_out"], *nat)
    for l in (0, 1):
        n = f"l{l}_"
        a[n + "wq"] = chunks(i[n + "peer_w_query"], *trn)
        a[n + "keys"] = np.ascontiguousarray(
            i[n + "peer_sub_keys"].reshape(16, 128, 128).transpose(2, 0, 1).reshape(128, 2048))
        a[n + "down"] = np.ascontiguousarray(
            i[n + "peer_expert_down"].reshape(128, 128, 8, 128).transpose(0, 3, 2, 1).reshape(128, 128, 1024))
        a[n + "up"] = np.ascontiguousarray(i[n + "peer_expert_up"].reshape(128, 128, 1024))
    w = i["w_in_2"][0]
    a["w2_a"] = chunks(w[:, :512], *nat)
    a["w2_qk"] = chunks(w[:, 1024:4096], *trn)
    a["w2_v"] = chunks(w[:, 4096:5632], *nat)
    a["w2_gates"] = chunks(np.concatenate([w[:, 512:1024], w[:, 5632:]], axis=1), *trn)
    a["rel"] = np.ascontiguousarray(i["rel_bias_2"])
    a["wpool"] = np.ascontiguousarray(i["w_pool_2"][0].transpose(1, 0, 2).reshape(128, 512))
    a["w_pa"] = chunks(i["w_proj_a_2"][0], *trn)
    a["w_pb"] = chunks(i["w_proj_b_2"][0], *trn)
    a["w_out2"] = chunks(i["w_out_2"][0], *nat)
    return a


def kernel(**inputs):
    import numpy as _np
    import concourse.bacc as _bacc
    from concourse import mybir as _mybir
    from concourse.bass_utils import run_bass_kernel_spmd as _run

    nc = _bacc.Bacc("TRN2", target_bir_lowering=False, num_devices=1, dynamic_dma_scratch_size=1024)
    arrays, args = {}, {}
    for name, a in _layout({k: _np.asarray(v) for k, v in inputs.items()}).items():
        arrays[f"in_{name}_dram"] = a
        args[name] = nc.dram_tensor(f"in_{name}_dram", a.shape, _mybir.dt.from_np(a.dtype), kind="ExternalInput").ap()
    out = nc.dram_tensor("out_0_dram", (256, 1024), _mybir.dt.float32, kind="ExternalOutput").ap()
    build(nc, args, out)
    r = _run(nc, [arrays], core_ids=[0])
    return r.results[0]["out_0_dram"].reshape(1, 256, 1024)
```

```python
from contextlib import ExitStack

import numpy as np

import concourse.bass as bass
from concourse import mybir

ALU = mybir.AluOpType
ACT = mybir.ActivationFunctionType
AX = mybir.AxisListType.X
F32 = mybir.dt.float32
F32R = mybir.dt.float32r
BF16 = mybir.dt.bfloat16
U32 = mybir.dt.uint32
I32 = mybir.dt.int32

NRAW = 4
NW = 4
AHEAD = 3
SLOT = 1024
NBIG = -1.0e30
FILL = -3.0e38
EPS = 1e-6

PV_MIX0, PV_FFN0, PV_MIX1, PV_FFN1, PV_MIX2, PV_CQ, PV_CKV, PV_LB, PV_BS, PV_PS, PV_BG, PV_N = (
    0, 8, 16, 24, 32, 40, 42, 43, 55, 59, 63, 79)
RW_HG, RW_GV, RW_MQ, RW_MK, RW_OQ, RW_OK, RW_FG, RW_N = (
    0, 512, 1024, 1216, 1408, 1536, 1664, 2688)
C_ID, C_IOTA, C_ONE, C_N0 = 0, 128, 256, 257
CA_LV, CA_TRI, CA_N = 0, 1024, 1152
CB_M, CB_INV, CB_N = 0, 384, 416
CC_PG, CC_N = 0, 2048
CD_OH, CD_NG, CD_N = 0, 512, 1024


class Program:

    def __init__(self, nc, ctx):
        self.nc, self.ctx = nc, ctx
        self.q = {k: [] for k in "VAGTS"}
        self.sem = {k: ctx.enter_context(nc.semaphore(f"done_{n}")) for k, n in
                    zip("VAGT", ("vector", "scalar", "gpsimd", "tensor"))}
        self.count = dict.fromkeys("VAGT", 0)
        self.ndma = 0

    def last(self, k):
        return (self.sem[k], self.count[k])

    def op(self, k, fn, *waits, loose=False):
        own = [self.last(k)] if self.count[k] and not loose else []
        self.count[k] += 1
        self.q[k].append((own + [w for w in waits if w], fn, self.sem[k], 1))
        return self.last(k)

    def mm(self, fn, *waits, mark=False):
        if mark:
            self.count["T"] += 1
        self.q["T"].append(([w for w in waits if w], fn, self.sem["T"] if mark else None, 1))
        return self.last("T")

    def dma(self, out, in_, *waits, sem=None, value=16, k="S"):
        if sem is None:
            sem = self.ctx.enter_context(self.nc.semaphore(f"dma{self.ndma}"))
            self.ndma += 1
        self.q[k].append(([w for w in waits if w], lambda e: e.dma_start(out, in_), sem, 16))
        return (sem, value)

    def wait(self, k, *waits):
        self.q[k].append(([w for w in waits if w], None, None, 0))

    def emit(self, k, eng):
        seen = {}
        for waits, fn, sem, inc in self.q[k]:
            for s, v in waits:
                if v and seen.get(s.name, 0) < v:
                    eng.wait_ge(s, v)
                    seen[s.name] = v
            if fn is not None:
                ins = fn(eng)
                if sem is not None:
                    ins.then_inc(sem, inc)


def build(nc, d, out, upto=9):
    ctx = ExitStack()
    with ctx:
        def sb(name, shape, dt=F32):
            return ctx.enter_context(nc.sbuf_tensor(name, shape, dt))

        P = Program(nc, ctx)
        op, mm, dma = P.op, P.mm, P.dma

        X = sb("X", [128, 2, 1024])
        XH = sb("XH", [128, 8, 256], F32R)
        XL = sb("XL", [128, 8, 256], F32R)
        raw = sb("raw", [128, NRAW, SLOT])
        WH = sb("WH", [128, NW, SLOT], F32R)
        WL = sb("WL", [128, NW, SLOT], F32R)
        GH = sb("GH", [128, 512], F32R)
        GL_ = sb("GL", [128, 512], F32R)
        OA = sb("OA", [128, 3, 3, 4, 128], BF16)
        OB = sb("OB", [128, 3, 4, 128], BF16)
        GP = sb("GP", [128, 3, 256], BF16)
        AR = sb("arena", [128, 32768])
        CST = sb("cst", [128, C_N0])
        PVT = sb("pvt", [128, PV_N])
        TRIG = sb("trig", [128, 2, 2, 32])
        IT = sb("it", [128, 3, 256])
        SM = sb("sm", [128, 128])
        PS = ctx.enter_context(nc.psum_tensor("ps", [128, 8, 512], F32))
        scr = nc.dram_tensor("scr_rel", [24, 512], F32, kind="Internal")
        ident = CST[:, C_ID:C_ID + 128]
        iota = CST[:, C_IOTA:C_IOTA + 128]
        ones = CST[:, C_ONE:C_ONE + 1].to_broadcast([128, 128])

        def ar(off, *shape):
            n = int(np.prod(shape))
            assert off + n <= 32768
            v = AR[:, off:off + n]
            if len(shape) == 2:
                v = v.rearrange("p (a b) -> p a b", b=shape[1])
            if len(shape) == 3:
                v = v.rearrange("p (a b c) -> p a b c", b=shape[1], c=shape[2])
            return v

        free = [[] for _ in range(8)]
        pools = {"main": [0, 1, 2, 3], "side": [4, 5, 6, 7]}
        turn = dict.fromkeys(pools, 0)

        def bank(pool="main"):
            b = pools[pool][turn[pool] % len(pools[pool])]
            turn[pool] += 1
            return b, free[b]

        order = ([("l0_qf", c) for c in range(8)] + [("l0_nat", c) for c in range(16)]
                 + [("l0_wout", nb * 4 + kp) for kp in (2, 3, 0, 1) for nb in range(2)])

        def peer_order(l):
            return ([(f"l{l}_wq", c) for c in range(16)] + [(f"l{l}_down", c) for c in range(128)]
                    + [(f"l{l}_up", c) for c in range(128)])
        order += peer_order(0) + [("l1_win", c) for c in range(16)] + [("l1_wout", nb * 4 + kp) for kp in range(4) for nb in range(2)] + peer_order(1)
        order += [("w2_a", c) for c in range(4)] + [("w2_qk", c) for c in range(24)] + [("w2_v", c) for c in range(12)]
        order += [("w2_gates", c) for c in range(24)]
        order += [("w_pa", c) for c in range(4)] + [("w_pb", c) for c in range(4)] + [("w_out2", nb * 4 + kp) for kp in range(4) for nb in range(2)]
        raw_sem = [ctx.enter_context(nc.semaphore(f"raw{i}")) for i in range(NRAW)]
        raw_tok, raw_free, part_tok, part_free = {}, {}, {}, {}
        high_tok = {}
        at = {"load": 0, "high": 0, "low": 0, "use": 0}

        def stream_load():
            i = at["load"]
            if i >= len(order) or (i >= NRAW and i - NRAW not in raw_free):
                return False
            name, c = order[i]
            raw_tok[i] = dma(raw[:, i % NRAW, :], d[name][c], raw_free.get(i - NRAW), sem=raw_sem[i % NRAW],
                             value=16 * (i // NRAW + 1))
            at["load"] += 1
            return True

        def stream_high():
            i = at["high"]
            if i >= len(order) or i not in raw_tok or (i >= NW and i - NW not in part_free):
                return False
            high_tok[i] = act(WH[:, i % NW, :], raw[:, i % NRAW, :], ACT.Copy,
                              raw_tok[i], part_free.get(i - NW), loose=True)
            at["high"] += 1
            return True

        def stream_low():
            i = at["low"]
            name, c = order[i]
            beside = name[3:] == "down" and c < 64 and c % 3 or name in ("l1_win", "w2_a", "w2_qk", "w2_v", "w2_gates", "w_pa", "w_pb") and c % 2
            k = "G" if beside else "V"
            raw_free[i] = part_tok[i] = tt(WL[:, i % NW, :], raw[:, i % NRAW, :], WH[:, i % NW, :], ALU.subtract,
                                           high_tok[i], loose=True, k=k)
            at["low"] += 1

        def stream_ahead(n=0):
            while stream_load():
                pass
            for _ in range(n):
                stream_high()
                stream_low()

        def stream_next(name, c):
            i = at["use"]
            assert order[i] == (name, c), (order[i], name, c)
            at["use"] += 1
            while at["low"] < at["high"]:
                stream_low()
            while at["high"] <= min(i + AHEAD, len(order) - 1):
                while stream_load():
                    pass
                if not stream_high():
                    break
                if at["high"] <= i + 2:
                    stream_low()
            while stream_load():
                pass
            return WH[:, i % NW, :], WL[:, i % NW, :], part_tok[i], i

        def stream_done(i, tok):
            part_free[i] = tok

        def everything():
            return [P.last(k) for k in "VAGT"]

        parity = [0]

        def turn_engine():
            parity[0] ^= 1
            return "VA"[parity[0]]

        def evac(out_, in_, *waits, scale=None, eng=None):
            k = eng or turn_engine()
            if k == "V":
                if scale is None:
                    return op("V", lambda e: e.tensor_copy(out_, in_), *waits)
                return op("V", lambda e: e.tensor_scalar(out_, in_, scale, None, ALU.mult), *waits)
            if scale is None:
                return op("A", lambda e: e.activation(out_, in_, ACT.Copy), *waits)
            return op("A", lambda e: e.activation(out_, in_, ACT.Copy, scale=scale), *waits)

        def tt(out_, a, b, o, *waits, k="V", loose=False):
            return op(k, lambda e: e.tensor_tensor(out_, a, b, o), *waits, loose=loose)

        def ts(out_, a, s1, s2, o1, o2=None, *waits, k="V", loose=False):
            if o2 is None:
                return op(k, lambda e: e.tensor_scalar(out_, a, s1, None, o1), *waits, loose=loose)
            return op(k, lambda e: e.tensor_scalar(out_, a, s1, s2, o1, o2), *waits, loose=loose)

        def stt(out_, a, s, b, o1, o2, *waits):
            return op("V", lambda e: e.scalar_tensor_tensor(out=out_, in0=a, scalar=s, in1=b, op0=o1, op1=o2), *waits)

        def act(out_, in_, f, *waits, loose=False, **kw):
            return op("A", lambda e: e.activation(out_, in_, f, **kw), *waits, loose=loose)

        def cp(out_, in_, *waits, k="V"):
            return op(k, lambda e: e.tensor_copy(out_, in_), *waits)

        def table(f):
            act(SM[:, 126:127], SM[:, 125:126], f)

        def rstd(v, n, *waits):
            ta = act(v, v, ACT.Sqrt, *waits, P.last("V"), scale=1.0 / n, bias=SM[:, 127:128])
            return op("V", lambda e: e.reciprocal(v, v), ta)

        def transposed(dst, src, src_tok, gain=None, nk=8, pool="main"):
            toks = []
            for kp in range(0, nk, 2):
                b, w = bank(pool)
                n = min(2, nk - kp)
                for j in range(n):
                    for t in range(2):
                        last = j == n - 1 and t == 1
                        tok = mm(lambda e, b=b, j=j, t=t, kp=kp: e.transpose(
                            PS[:, b, j * 256 + t * 128:j * 256 + t * 128 + 128], src(t, kp + j), ident),
                            *w, *src_tok, mark=last)
                who = turn_engine()
                for j in range(n):
                    r = evac(dst(kp + j), PS[:, b, j * 256:j * 256 + 256], tok,
                             scale=gain(kp + j) if gain else None, eng=who)
                free[b] = [r]
                toks.append(r)
            return toks

        def transposed_split(src, src_tok, gain=None, pairs=range(4), pool="main", by_tile=False):
            toks, t_tok = [None] * 4, {}
            banks = {kp: bank(pool) for kp in pairs}
            for t in range(2):
                for kp, (b, w) in banks.items():
                    for j in range(2):
                        t_tok[kp] = mm(lambda e, b=b, j=j, t=t, kp=kp: e.transpose(
                            PS[:, b, j * 256 + t * 128:j * 256 + t * 128 + 128], src(t, 2 * kp + j), ident),
                            *w, *(src_tok[t:t + 1] if by_tile else src_tok), mark=(j == 1 and t == 1))
            for kp, (b, w) in banks.items():
                tok = t_tok[kp]
                x2 = XH[:, 2 * kp:2 * kp + 2, :]
                if gain is None:
                    ps = PS[:, b, :].rearrange("p (j t) -> p j t", j=2)
                    ht = act(x2, ps, ACT.Copy, tok, loose=True)
                    toks[kp] = tt(XL[:, 2 * kp:2 * kp + 2, :], ps, x2, ALU.subtract, ht, loose=True)
                else:
                    for j in range(2):
                        k = 2 * kp + j
                        ht = act(XH[:, k, :], PS[:, b, j * 256:j * 256 + 256], ACT.Copy, tok, scale=gain(k), loose=True)
                    for j in range(2):
                        k = 2 * kp + j
                        toks[kp] = op("V", lambda e, b=b, j=j, k=k: e.scalar_tensor_tensor(
                            out=XL[:, k, :], in0=PS[:, b, j * 256:j * 256 + 256], scalar=gain(k), in1=XH[:, k, :],
                            op0=ALU.mult, op1=ALU.subtract), ht, loose=True)
                free[b] = [toks[kp]]
            return toks

        arena_read = []
        x_tok = {}

        def norm_X(xs, arena_free):
            for t in range(2):
                for h in range(2):
                    xv = X[:, t, h * 512:h * 512 + 512]
                    sq = act(xs[:, t, h * 512:h * 512 + 512], xv, ACT.Square, x_tok[t, h], *arena_free,
                             accum_out=SM[:, 2 * t + h:2 * t + h + 1])
                v = SM[:, 4 + t:5 + t]
                tt(v, SM[:, 2 * t:2 * t + 1], SM[:, 2 * t + 1:2 * t + 2], ALU.add, sq)
                yield t, rstd(v, 1024)

        def norm_T(gcol, arena_free, scr=30720):
            xs = ar(scr, 2, 1024)
            n_tok = [ts(xs[:, t, :], X[:, t, :], SM[:, 4 + t:5 + t], None, ALU.mult, None, r, *arena_free, loose=True)
                     for t, r in norm_X(xs, arena_free)]
            if not at["high"]:
                stream_ahead(2)
                P.wait("A", p_tok)
            return transposed_split(lambda t, k: xs[:, t, k * 128:k * 128 + 128], n_tok, by_tile=True,
                                    gain=lambda k: PVT[:, gcol + k:gcol + k + 1])

        def three(o, a, b, first, last, *waits):
            mm(lambda e: e.matmul(o, a[0], b[0], start=first, stop=False), *waits)
            mm(lambda e: e.matmul(o, a[0], b[1], start=False, stop=False))
            return mm(lambda e: e.matmul(o, a[1], b[0], start=False, stop=last), mark=True)

        def pump(side, n=1):
            for _ in range(n if side is not None else 0):
                next(side, None)

        def drain(side):
            for _ in side:
                pass

        def proj_nat(name, k0, src_tok, nk, nblocks, use, c0=0, side=None, pace=1):
            for nb in range(nblocks):
                banks = [bank(), bank()]
                for kq in range(nk // 2):
                    hi, lo, wt, i = stream_next(name, c0 + nb * (nk // 2) + kq)
                    for t in range(2):
                        b, wb = banks[t]
                        for kk in range(2):
                            k = kq * 2 + kk
                            tok = three(PS[:, b, :], [v[:, k0 + k, t * 128:t * 128 + 128] for v in (XH, XL)],
                                        [v[:, kk * 512:kk * 512 + 512] for v in (hi, lo)],
                                        k == 0, k == nk - 1, wt, *wb, src_tok[(k0 + k) // 2])
                    stream_done(i, tok)
                    if kq < nk // 2 - 1:
                        pump(side, pace)
                for t in range(2):
                    b = banks[t][0]
                    free[b] = [use(nb, t, PS[:, b, :], tok)]
                pump(side, pace)

        def proj_T(name, k0, src_tok, nk, pairs, use, c0=0, side=None, pace=1):
            for nb in range(pairs):
                banks = [bank(), bank()]
                for kh in range(nk // 4):
                    hi, lo, wt, i = stream_next(name, c0 + nb * (nk // 4) + kh)
                    for j in range(2):
                        b, wb = banks[j]
                        for kk in range(4):
                            k = kh * 4 + kk
                            o = kk * 256 + j * 128
                            tok = three(PS[:, b, 0:256], [v[:, o:o + 128] for v in (hi, lo)],
                                        [v[:, k0 + k, :] for v in (XH, XL)], k == 0, k == nk - 1, wt, *wb, src_tok[(k0 + k) // 2])
                    stream_done(i, tok)
                    if kh < nk // 4 - 1:
                        pump(side, pace)
                for j in range(2):
                    b = banks[j][0]
                    free[b] = [use(2 * nb + j, PS[:, b, 0:256], tok)]
                pump(side, pace)

        def out_proj(name, pairs, tok, side=None):
            if name not in sums:
                sums[name] = [bank() for _ in range(4)], []
            banks, done = sums[name]
            for kp in pairs:
                for nb in range(2):
                    hi, lo, wt, i = stream_next(name, nb * 4 + kp)
                    for t in range(2):
                        b, wb = banks[2 * nb + t]
                        for kk in range(2):
                            k = 2 * kp + kk
                            last = three(PS[:, b, :], [v[:, k, t * 128:t * 128 + 128] for v in (XH, XL)],
                                         [v[:, kk * 512:kk * 512 + 512] for v in (hi, lo)],
                                         not done and kk == 0, len(done) == 3 and kk == 1, wt, *wb, tok[kp])
                        if len(done) == 3:
                            xv = X[:, t, nb * 512:nb * 512 + 512]
                            free[b] = [tt(xv, xv, PS[:, b, :], ALU.add, last, loose=True)]
                            x_tok[t, nb] = free[b][0]
                    stream_done(i, last)
                    pump(side)
                done.append(kp)
        sums = {}

        for t in range(2):
            xd = dma(X[:, t, :], d["x"][t * 128:t * 128 + 128, :])
            x_tok[t, 0] = x_tok[t, 1] = xd
            if t == 0:
                c_tok = dma(CST[:, :], d["cst"])
        p_tok = dma(PVT[:, :], d["pv"])
        stream_ahead()
        op("V", lambda e: e.memset(SM[:, 125:126], 1.0))
        eps_tok = op("V", lambda e: e.memset(SM[:, 127:128], EPS))
        P.wait("A", eps_tok)
        table(ACT.Sqrt)
        P.wait("V", c_tok, p_tok)
        P.wait("G", c_tok, p_tok)
        P.wait("T", c_tok)

        trig_tok = [None]

        def angles():
            CB, AN, RR = ar(30000, CB_N), ar(30500, 2, 32), ar(30564, 2, 32)
            ps_i, pf = AR[:, 30628:30630].bitcast(I32), AR[:, 30630:30632]
            SN, CS = TRIG[:, 0], TRIG[:, 1]
            cb_tok = dma(CB, d["cb"])
            ip_tok = dma(ps_i, d["pos"])
            yield
            cp(pf, ps_i, ip_tok)
            inv = CB[:, CB_INV:CB_INV + 32]
            for t in range(2):
                ts(AN[:, t, :], inv, pf[:, t:t + 1], None, ALU.mult, None, cb_tok)
            magic = 12582912.0
            ts(RR, AN, float(np.float32(1.0 / (2 * np.pi))), magic, ALU.mult, ALU.add)
            yield
            ts(RR, RR, magic, None, ALU.subtract)
            c1 = 6.28125
            c2 = float(np.float32(2 * np.pi - c1))
            c3 = float(2 * np.pi - c1 - c2)
            for cc in (c1, c2, c3):
                stt(AN, RR, -cc, AN, ALU.mult, ALU.add)
            yield
            lim = 3.1415925
            ts(SN, AN, lim, -lim, ALU.min, ALU.max)
            ts(AN, AN, float(np.pi / 2), None, ALU.add)
            ts(RR, AN, lim, -2 * float(np.pi), ALU.is_gt, ALU.mult)
            yield
            tt(AN, AN, RR, ALU.add)
            a_tok = ts(CS, AN, lim, -lim, ALU.min, ALU.max)
            yield
            yield
            act(SN, SN, ACT.Sin, a_tok)
            trig_tok[0] = act(CS, CS, ACT.Sin)
            yield

        def mixer0():
            F, Q, K, B = ar(0, 4, 256), ar(1024, 4, 256), ar(2048, 4, 256), ar(3072, 4, 256)
            E = [ar(24576 + 1024 * i, 8, 128) for i in range(3)]
            SC, SC2 = ar(6144, 8, 128), ar(7168, 4, 128)
            CA = ar(7680, CA_N)
            VN, OG, VG, U = (ar(8832 + 1024 * i, 2, 512) for i in range(4))
            HG, GV = ar(12928, 512), ar(13440, 512)
            GW = ar(13952, 4, 128)
            OC = ar(14464, 2, 1024)
            TMP = ar(18560, 2, 512)
            LB = ar(19584, 8, 4)

            ca_tok = dma(CA, d["ca"])
            gw_tok = dma(GW, d["gw"].rearrange("p (g t) -> p g t", g=4))
            hg_tok = dma(HG, d["rows"][0:1, RW_HG:RW_HG + 512].to_broadcast([128, 512]))
            gv_tok = dma(GV, d["rows"][0:1, RW_GV:RW_GV + 512].to_broadcast([128, 512]))
            xn = norm_T(PV_MIX0, [], 20480)

            L = PVT[:, PV_LB:PV_LB + 12].rearrange("p (r h) -> p r h", r=3)
            m = LB[:, 0, :]
            tt(m, L[:, 0, :], L[:, 1, :], ALU.max)
            tt(m, m, L[:, 2, :], ALU.max)
            tt(LB[:, 1:4, :], L, m.unsqueeze(1).to_broadcast([128, 3, 4]), ALU.subtract)
            ea = act(LB[:, 1:4, :], LB[:, 1:4, :], ACT.Exp, P.last("V"))
            lb, oml = LB[:, 4, :], LB[:, 5, :]

            def lower_bound():
                tt(m, LB[:, 1, :], LB[:, 2, :], ALU.add, ea)
                tt(m, m, LB[:, 3, :], ALU.add)
                op("V", lambda e: e.reciprocal(m, m))
                tt(lb, LB[:, 1, :], m, ALU.mult)
                ts(oml, lb, -1.0, 1.0, ALU.mult, ALU.add)

            def use_f(blk, ps, tok):
                return act(F[:, blk, :], ps, ACT.Sigmoid, tok)

            def use_q(blk, ps, tok):
                return evac(Q[:, blk, :], ps, tok)
            proj_T("l0_qf", 0, xn, 8, 2, use_f)
            lower_bound()
            sig = P.last("A")
            F8, B8, Q8, K8 = (v.rearrange("p h (t s) -> p (h t) s", t=2) for v in (F, B, Q, K))
            masks = CA[:, CA_LV:CA_LV + 1024].bitcast(U32)
            ready = {}

            def halves(v, lv):
                return v.rearrange("p s (b w i) -> p s b w i", w=2, i=1 << (lv - 1))

            def recurrence():
                for h in range(4):
                    f_tok = ts(F[:, h, :], F[:, h, :], oml[:, h:h + 1], lb[:, h:h + 1], ALU.mult, ALU.add, sig)
                k_tok = ts(K, F, -1.0, 1.0, ALU.mult, ALU.add)
                g_tok = act(F, F, ACT.Ln, k_tok)
                op("V", lambda e: e.memset(SC, 0.0))
                yield
                for i in range(8):
                    op("V", lambda e, i=i: e.tensor_tensor_scan(B8[:, i, :], ones, F8[:, i, :], 0.0,
                                                                ALU.mult, ALU.add), g_tok, loose=i > 0)
                b_tok = P.last("V")
                e_read = [None] * 3

                def decays(lv):
                    Eb = E[lv % 3]
                    half = 1 << (lv - 1)
                    Bv, Ev, Qv, Kv = (v.rearrange("p s (b w i) -> p (s b) w i", w=2, i=half) if lv < 8 else
                                      v.rearrange("p (h w) i -> p h w i", w=2) for v in (B8, Eb, Q8, K8))
                    n = 1024 // (2 * half)
                    mid = Bv[:, :, 0, half - 1:half].to_broadcast([128, n, half])
                    if lv < 8:
                        tt(Ev[:, :, 1, :], Bv[:, :, 1, :], mid, ALU.subtract, e_read[lv % 3], b_tok, loose=True)
                    else:
                        cp(Ev[:, :, 1, :], Bv[:, :, 1, :], e_read[lv % 3], b_tok)
                    d_ = tt(Ev[:, :, 0, :], mid, Bv[:, :, 0, :], ALU.subtract, e_read[lv % 3], b_tok, loose=True)
                    x_ = act(Eb, Eb, ACT.Exp, d_)
                    tt(Ev[:, :, 1, :], Ev[:, :, 1, :], Qv[:, :, 1, :], ALU.mult, x_, *ready["q"], k="G", loose=True)
                    e_tok = tt(Ev[:, :, 0, :], Ev[:, :, 0, :], Kv[:, :, 0, :], ALU.mult, x_, k_tok, k="G", loose=True)
                    return Eb, (e_tok,)

                def level(lv, lhs, e_tok):
                    b, wb = bank("side")
                    for i in range(8 if lv < 8 else 4):
                        if lv < 8:
                            rhs = halves(lhs, lv)[:, i, :, 1, :]
                            o, a_ = PS[:, b, i * 64:i * 64 + 64].rearrange("p (b i) -> p b i", i=1 << (lv - 1)), i
                        else:
                            rhs, o, a_ = lhs[:, 2 * i + 1, :], PS[:, b, i * 128:i * 128 + 128], 2 * i
                        s_tok = mm(lambda e, o=o, a_=a_, rhs=rhs: e.matmul(o, lhs[:, a_, :], rhs, start=True, stop=True),
                                   *e_tok, *wb, mark=(i == (7 if lv < 8 else 3)))
                    if lv == 8:
                        r = cp(SC2, PS[:, b, :].rearrange("p (i t) -> p i t", i=4), s_tok)
                    else:
                        ps = PS[:, b, :].rearrange("p (s b i) -> p s b i", s=8, i=1 << (lv - 1))
                        mk = masks[:, lv * 128:lv * 128 + 128].rearrange("p (b w i) -> p b w i", w=2, i=1 << (lv - 1))
                        mk = mk[:, :, 1, :].unsqueeze(1).to_broadcast([128, 8, 64 >> (lv - 1), 1 << (lv - 1)])
                        r = op("V", lambda e: e.copy_predicated(halves(SC, lv)[:, :, :, 1, :], mk, ps), s_tok, ca_tok)
                    free[b] = [r]
                    e_read[lv % 3] = s_tok
                    return r

                def diagonal():
                    for hh in range(2):
                        b, wb = bank("side")
                        for i in range(4):
                            s_tok = mm(lambda e, b=b, i=i, hh=hh: e.matmul(
                                PS[:, b, i * 128:i * 128 + 128], K8[:, hh * 4 + i, :], Q8[:, hh * 4 + i, :],
                                start=True, stop=True), k_tok, *ready["q"], *wb, mark=(i == 3))
                        mk = masks[:, 0:128].unsqueeze(1).to_broadcast([128, 4, 128])
                        free[b] = [op("V", lambda e, b=b, hh=hh: e.copy_predicated(
                            SC[:, hh * 4:hh * 4 + 4, :], mk, PS[:, b, :].rearrange("p (i t) -> p i t", i=4)),
                            s_tok, ca_tok)]
                while "q" not in ready:
                    yield
                nxt = [decays(1)]
                yield
                nxt.append(decays(2))
                yield
                diagonal()
                for lv in range(1, 9):
                    ready["sc"] = level(lv, *nxt.pop(0))
                    if lv + 2 < 9:
                        nxt.append(decays(lv + 2))
                    yield
                ready["rec"] = True

            def group_norm(v, sq, gain, *waits):
                ss = SM[:, 8:16]
                q_ = tt(sq, v, v, ALU.mult, *waits, k="G")
                yield
                r_ = op("V", lambda e: e.tensor_reduce(ss, sq, AX, ALU.add), q_)
                yield
                r_ = rstd(ss, 128, r_)
                tt(v, v, ss.unsqueeze(2).to_broadcast([128, 8, 128]), ALU.mult, r_, k="G")
                yield
                tt(v.rearrange("p (t h) c -> p t (h c)", t=2), v.rearrange("p (t h) c -> p t (h c)", t=2),
                   gain.unsqueeze(1).to_broadcast([128, 2, 512]), ALU.mult, k="G")

            def gating():
                tri = CA[:, CA_TRI:CA_TRI + 128]
                gw_ready = tt(GW, GW, tri.unsqueeze(1).to_broadcast([128, 4, 128]), ALU.mult, gw_tok, ca_tok, k="G")
                while 0 not in ready:
                    yield
                uv_tok = act(VG, VG, ACT.Gelu_apprx_tanh, *ready[0])
                yield
                yield from group_norm(VG.rearrange("p t (h c) -> p (t h) c", h=4),
                                      TMP.rearrange("p t (h c) -> p (t h) c", h=4), GV, uv_tok, gv_tok)
                vg_tok = P.last("G")
                yield
                yield
                while 1 not in ready:
                    yield
                uv_tok = act(U, U, ACT.Gelu_apprx_tanh, *ready[1])
                yield
                for t in range(2):
                    b, wb = bank("side")
                    for g in range(4):
                        tok = mm(lambda e, g=g, t=t, b=b: e.matmul(
                            PS[:, b, g * 128:g * 128 + 128], GW[:, g, :], VG[:, t, g * 128:g * 128 + 128],
                            start=True, stop=True), gw_ready, vg_tok, *wb, mark=(g == 3))
                    for g in range(4):
                        r = op("V", lambda e, b=b, g=g, t=t: e.scalar_tensor_tensor(
                            out=OC[:, t, 512 + g * 128:640 + g * 128], in0=PS[:, b, g * 128:g * 128 + 128],
                            scalar=PVT[:, PV_BS + g:PV_BS + g + 1], in1=U[:, t, g * 128:g * 128 + 128],
                            op0=ALU.add, op1=ALU.mult), tok, uv_tok, loose=True)
                    free[b] = [r]
                    ready["gate"] = r
                    yield
            o_bank, ss = [None, None], SM[:, 8:16]

            def heads():
                yield from gating()
                while 2 not in ready or "rec" not in ready:
                    yield
                vn_tok = act(VN, VN, ACT.Silu, *ready[2])
                yield
                yield
                for t in range(2):
                    b, wb = bank("side")
                    o_bank[t] = b
                    for h in range(4):
                        o = PS[:, b, h * 128:h * 128 + 128]
                        tok = mm(lambda e, h=h, t=t, o=o: e.matmul(
                            o, SC[:, 2 * h + t, :], VN[:, t, h * 128:h * 128 + 128], start=True, stop=(t == 0)),
                            ready["sc"], vn_tok, *wb, mark=True)
                        if t == 1:
                            tok = mm(lambda e, h=h, o=o: e.matmul(
                                o, SC2[:, h, :], VN[:, 0, h * 128:h * 128 + 128], start=False, stop=True), mark=True)
                    for h in range(4):
                        q_ = act(TMP[:, t, h * 128:h * 128 + 128], PS[:, b, h * 128:h * 128 + 128], ACT.Square, tok,
                                 accum_out=ss[:, 4 * t + h:4 * t + h + 1])
                    yield
                ready["squares"] = q_
            gens = recurrence(), heads(), angles(), rel_table([])

            def both():
                while True:
                    if [next(g, 0) for g in gens] == [0] * 4:
                        return
                    yield
            side = both()
            proj_T("l0_qf", 0, xn, 8, 2, use_q, c0=4, side=side)
            ready["q"] = [P.last("V"), P.last("A")]

            def use_rest(nb, t, ps, tok):
                r = evac((VG, U, VN, OG)[nb][:, t, :], ps, tok)
                if t == 1:
                    ready[nb] = [P.last("V"), P.last("A")]
                return r
            proj_nat("l0_nat", 0, xn, 8, 2, use_rest, side=side)
            proj_nat("l0_nat", 0, xn, 8, 2, lambda nb, t, ps, tok: use_rest(nb + 2, t, ps, tok), c0=8, side=side)
            drain(side)
            low = transposed_split(lambda t, k: OC[:, t, k * 128:k * 128 + 128], [ready["gate"]], pairs=(2, 3))

            def gated():
                n_tok = rstd(ss, 128, ready["squares"])
                yield
                og_tok = act(OG, OG, ACT.Silu, *ready[3])
                yield
                og_tok = tt(OG, OG, HG.unsqueeze(1).to_broadcast([128, 2, 512]), ALU.mult, og_tok, hg_tok)
                for t in range(2):
                    for h in range(4):
                        ready["o"] = op("V", lambda e, h=h, t=t: e.scalar_tensor_tensor(
                            out=OC[:, t, h * 128:h * 128 + 128], in0=PS[:, o_bank[t], h * 128:h * 128 + 128],
                            scalar=ss[:, 4 * t + h:4 * t + h + 1], in1=OG[:, t, h * 128:h * 128 + 128],
                            op0=ALU.mult, op1=ALU.mult), n_tok, og_tok, loose=True)
                    free[o_bank[t]] = [ready["o"]]
                yield
            side = gated()
            out_proj("l0_wout", (2, 3), low, side=side)
            drain(side)
            o_tok = ready["o"]
            high = transposed_split(lambda t, k: OC[:, t, k * 128:k * 128 + 128], [o_tok], pairs=(0, 1), pool="side")
            arena_read[:] = [P.last("V"), P.last("A"), P.last("G")]
            table(ACT.Sqrt)
            out_proj("l0_wout", (0, 1), high)

        def peer(l):
            G = AR[:, :].rearrange("p (e t) -> p e t", t=256)
            KEYS, SMALL = ar(20480, 2048), 22528
            S = ar(24576, 2, 2048)
            QT = ar(28672, 16, 256)
            CD, OH = ar(28672, 2048), ar(30720, 2048)
            SV, SI, SF = (ar(SMALL + i * 256, 16, 16) for i in range(3))
            TS, TC, HI, HF = ar(SMALL + 768, 8, 16), ar(SMALL + 896, 128), ar(SMALL + 1024, 128), ar(SMALL + 1152, 128)
            TK, HF2 = ar(SMALL + 1280, 3, 128), ar(SMALL + 1664, 128)
            before = everything()
            keys_tok = dma(KEYS, d[f"l{l}_keys"], *before)
            xn = norm_T((PV_FFN0, PV_FFN1)[l], arena_read)
            name = f"l{l}_"

            proj_T(name + "wq", 0, xn, 8, 8, lambda blk, ps, tok: evac(QT[:, blk, :], ps, tok))
            q_tok = [P.last("V"), P.last("A")]
            for t in range(2):
                for j0 in range(0, 16, 4):
                    b, wb = bank("side")
                    for j in range(j0, j0 + 4):
                        q_read = mm(lambda e, b=b, j=j, t=t: e.matmul(
                            PS[:, b, (j % 4) * 128:(j % 4) * 128 + 128], QT[:, j, t * 128:t * 128 + 128],
                            KEYS[:, j * 128:j * 128 + 128], start=True, stop=True), keys_tok, *q_tok, *wb,
                            mark=(j == j0 + 3))
                    free[b] = [act(S[:, t, j0 * 128:j0 * 128 + 512], PS[:, b, :], ACT.Copy, q_read)]
            s_tok = P.last("A")
            tk_read, by = [], [None, None]

            def top16(lists, *waits):
                for r in range(2):
                    vi = [(v[:, r * 8:r * 8 + 8], i[:, r * 8:r * 8 + 8].bitcast(U32), src) for v, i, src in lists]
                    toks = [op("V", lambda e, v8=v8, src=src: e.max(v8, src), *waits, loose=r == 0)
                            for v8, _, src in vi]
                    yield
                    for (v8, i8, src), tok in zip(vi, toks):
                        op("V", lambda e, v8=v8, i8=i8, src=src: e.max_index(i8, v8, src), tok, loose=True)
                    if r == 0:
                        yield
                        for (v8, i8, src), tok in zip(vi, toks):
                            last = op("V", lambda e, v8=v8, src=src: e.match_replace(src, v8, src, FILL), tok, loose=True)
                        waits = (last,)
                    yield

            def select(t):
                begin = P.last("V")
                for j in range(0, 16, 4):
                    yield from top16([(SV[:, i, :], SI[:, i, :], S[:, t, i * 128:i * 128 + 128])
                                      for i in range(j, j + 4)], s_tok, begin)
                cp(SF, SI.bitcast(U32))
                sv = SV.rearrange("p (h q) k -> p h q k", q=2)
                sf = SF.rearrange("p (h q) k -> p h q k", q=2)
                cd = CD.rearrange("p (h a b) -> p h a b", h=8, a=16)
                tc = TC.rearrange("p (h k) -> p h k", h=8)
                s_done = P.last("V")
                for h0 in range(0, 8, 4):
                    for h in range(h0, h0 + 4):
                        tt(cd[:, h], sv[:, h, 0, :].unsqueeze(2).to_broadcast([128, 16, 16]),
                           sv[:, h, 1, :].unsqueeze(1).to_broadcast([128, 16, 16]), ALU.add, q_read, s_done, loose=True)
                    yield
                    yield from top16([(TS[:, h, :], tc[:, h, :], CD[:, h * 256:h * 256 + 256])
                                      for h in range(h0, h0 + 4)], P.last("V"))
                gt = TK[:, 2, :].rearrange("p (h k) -> p h k", h=8)
                x_ = tt(gt, TS, TS[:, :, 0:1].to_broadcast([128, 8, 16]), ALU.subtract, *tk_read)
                for which, (hf, oh) in enumerate(((HF, OH), (HF2, CD))):
                    if which == 0:
                        ts(HI.bitcast(U32), TC.bitcast(U32), 4, None, ALU.logical_shift_right)
                    else:
                        ts(HI.bitcast(U32), TC.bitcast(U32), 15, None, ALU.bitwise_and)
                    cp(hf, HI.bitcast(U32))
                    yield
                    oh_tok = tt(oh.rearrange("p (a b) -> p a b", b=16), hf.unsqueeze(2).to_broadcast([128, 128, 16]),
                                iota[:, 0:16].unsqueeze(1).to_broadcast([128, 128, 16]), ALU.is_equal)
                    oh4 = oh.rearrange("p (h k j) -> p h k j", h=8, k=16)
                    for h in range(0, 8, 2):
                        v = oh4[:, h:h + 2]
                        by[which] = tt(v, v, sf[:, h:h + 2, which, :].unsqueeze(2).to_broadcast([128, 2, 16, 16]),
                                       ALU.mult, oh_tok, k="G", loose=True)
                        yield
                for which, oh in enumerate((OH, CD)):
                    yield
                    yield
                    op("V", lambda e, which=which, oh=oh: e.tensor_reduce(
                        TK[:, which, :], oh.rearrange("p (a b) -> p a b", b=16), AX, ALU.add), by[which], *tk_read)
                yield
                x_ = act(TK[:, 2, :], TK[:, 2, :], ACT.Exp, x_)
                yield
                yield
                yield
                op("V", lambda e: e.tensor_reduce(SM[:, 16:24], gt, AX, ALU.add), x_)
                op("V", lambda e: e.reciprocal(SM[:, 16:24], SM[:, 16:24]))
                tok = tt(gt, gt, SM[:, 16:24].unsqueeze(2).to_broadcast([128, 8, 16]), ALU.mult)
                for _ in range(2):
                    yield
                b, wb = bank("side")
                for i in range(3):
                    tp = mm(lambda e, i=i, b=b: e.transpose(PS[:, b, i * 128:i * 128 + 128], TK[:, i, :], ident),
                            tok, *wb, mark=(i == 2))
                tk_read[:] = [tp]
                free[b] = [cp(IT[:, :, t * 128:t * 128 + 128],
                              PS[:, b, 0:384].rearrange("p (i t) -> p i t", i=3), tp)]
                gate = IT[:, 2, t * 128:t * 128 + 128]
                for k in range(3):
                    part = GP[:, k, t * 128:t * 128 + 128]
                    cp(part, gate)
                    if k < 2:
                        tt(gate, gate, part, ALU.subtract)
                cp(gate, GP[:, 0, t * 128:t * 128 + 128])
                yield

            at_g = {"chunks": 0, "tokens": 0}

            def spread():
                a_tok, p_tok, t_tok = {}, {}, {}
                it_tok = P.last("V")

                def spread_of(i, q):
                    return IT[:, i, 4 * q:4 * q + 4].unsqueeze(2).to_broadcast([128, 4, 128])

                def fold(q):
                    b, tok = t_tok[q]
                    n, ps = at_g["chunks"], PS[:, b, :].rearrange("p (t i) -> p i t", t=4)
                    g = G[:, :, 4 * q:4 * q + 4]
                    r = tt(g[:, 0:n], ps[:, 0:n], g[:, 0:n], ALU.mult, tok, at_g["tok"], loose=True)
                    if n < 128:
                        r = act(g[:, n:128], ps[:, n:128], ACT.Copy, r)
                    free[b] = [r]
                    at_g["tokens"], at_g["gates"] = 4 * q + 4, r

                def products(q):
                    b, wb = bank("side")
                    for j in range(4):
                        for k in range(3):
                            tok = mm(lambda e, j=j, k=k: e.matmul(
                                PS[:, b, j * 128:j * 128 + 128], OB[:, q % 3, j, :], OA[:, q % 3, k, j, :],
                                start=(k == 0), stop=(k == 2)), *p_tok[q], *wb, mark=(j == 3 and k == 2))
                    t_tok[q] = b, tok

                def gates(q):
                    o1 = OA[:, q % 3, 2]
                    for j in range(4):
                        x_ = act(OA[:, q % 3, 0, j], o1[:, j], ACT.Copy, a_tok[q], scale=IT[:, 2, 4 * q + j:4 * q + j + 1],
                                 loose=True)
                    for k in (1, 2):
                        y_ = tt(OA[:, q % 3, k], o1, GP[:, k, 4 * q:4 * q + 4].unsqueeze(2).to_broadcast([128, 4, 128]),
                                ALU.mult, a_tok[q], x_ if k == 2 else None, k="G", loose=k == 1)
                    p_tok[q] = x_, y_
                for s_ in range(67):
                    if s_ >= 3:
                        fold(s_ - 3)
                    if 2 <= s_ < 66:
                        products(s_ - 2)
                    if 1 <= s_ < 65:
                        gates(s_ - 1)
                    if s_ < 64:
                        before_ = t_tok[s_ - 3][1] if s_ >= 3 else None
                        for o, i in ((OA[:, s_ % 3, 2], 0), (OB[:, s_ % 3], 1)):
                            a_tok[s_] = tt(o, iota.unsqueeze(1).to_broadcast([128, 4, 128]), spread_of(i, s_), ALU.is_equal,
                                           it_tok, before_, loose=True)
                    yield

            def activate(c, b, tok):
                ps, g, n = PS[:, b, :].rearrange("p (j t) -> p j t", j=2), G[:, c - 1:c + 1, :], at_g["tokens"]
                if n < 256:
                    r = act(g[:, :, n:256], ps[:, :, n:256], ACT.Gelu_apprx_tanh, tok, *before, tail_tok[0])
                    free[b] = [r]
                if n:
                    x_ = act(ps[:, :, 0:n], ps[:, :, 0:n], ACT.Gelu_apprx_tanh, tok)
                    to_gate.append((b, ps[:, :, 0:n], g[:, :, 0:n], x_, at_g["gates"]))
                at_g["chunks"], at_g["tok"] = c + 1, P.last("A")
            to_gate = []

            def gate():
                if to_gate:
                    b, ps, g, x_, w_ = to_gate.pop()
                    free[b] = [tt(g, ps, g, ALU.mult, x_, w_, loose=True)]

            down_tok, fold_tok = [None], []
            split_tok, split_free = {}, {}

            def parts_g(p):
                if p % 3 == 0:
                    return GH[:, :], GL_[:, :]
                return [v[:, 2 * (p % 3):2 * (p % 3) + 2, :].rearrange("p e t -> p (e t)") for v in (XH, XL)]

            def split_g(p):
                if p < 64:
                    g = G[:, 2 * p:2 * p + 2, :].rearrange("p e t -> p (e t)")
                    gh, gl = parts_g(p)
                    ht = act(gh, g, ACT.Copy, *fold_tok, split_free.get(p - 3, down_tok[0] if p else None))
                    split_tok[p] = tt(gl, g, gh, ALU.subtract, ht)
            tail_tok = [None]

            def side_work():
                yield from select(0)
                yield from select(1)
                tail_tok[0] = P.last("V")
                yield from spread()
            side = side_work()
            for c in range(128):
                hi, lo, wt, i = stream_next(name + "down", c)
                if c % 2 == 0:
                    b, wb = bank()
                o = PS[:, b, (c % 2) * 256:(c % 2) * 256 + 256]
                for k in range(8):
                    tok = three(o, [v[:, k * 128:k * 128 + 128] for v in (hi, lo)], [v[:, k, :] for v in (XH, XL)],
                                k == 0, k == 7, wt, *wb, xn[k // 2])
                stream_done(i, tok)
                if c % 2 == 0:
                    gate()
                pump(side, 1 if tail_tok[0] else 1 + (c % 5 > 0))
                if c == 127:
                    drain(side)
                    fold_tok[:] = [P.last("V"), P.last("A")]
                    split_g(0)
                if c % 2:
                    while c >= 80 and tail_tok[0] is None:
                        pump(side)
                    activate(c, b, tok)
            gate()
            fold_tok[:] = [P.last("V"), P.last("A")]

            down_tok[0] = tok
            pools.update(main=[4, 5, 6, 7], side=[0, 1, 2, 3])
            acc = [bank() for _ in range(4)]
            acc_tok = [None] * 4
            for c in range(128):
                hi, lo, wt, i = stream_next(name + "up", c)
                p, j = divmod(c, 2)
                if c == 124:
                    table(ACT.Sqrt)
                if j == 0:
                    split_g(p + 1)
                for t in range(2):
                    for h in range(2):
                        b, wb = acc[2 * t + h]
                        tok = acc_tok[2 * t + h] = three(PS[:, b, :], [v[:, j * 256 + t * 128:j * 256 + t * 128 + 128] for v in parts_g(p)],
                                    [v[:, h * 512:h * 512 + 512] for v in (hi, lo)], c == 0, c == 127,
                                    wt, *wb, split_tok[p])
                stream_done(i, tok)
                split_free[p] = tok
            for t in range(2):
                for h in range(2):
                    b = acc[2 * t + h][0]
                    xv = X[:, t, h * 512:h * 512 + 512]
                    x_tok[t, h] = tt(xv, xv, PS[:, b, :], ALU.add, acc_tok[2 * t + h], loose=True)
                    free[b] = [x_tok[t, h]]
            arena_read[:] = [split_tok[63]]
            pools.update(main=[0, 1, 2, 3], side=[4, 5, 6, 7])

        def mixer1():
            Z = ar(0, 2, 2048)
            CQT, CKT = ar(4096, 2, 256), ar(4608, 1, 256)
            QC, KV, KC = ar(4864, 2, 768), ar(6400, 2, 1024), ar(8448, 2, 768)
            GN = ar(10240, 640)
            QN, QR, KN, KR, QD, KD = (ar(10880 + i * 1024, 4, 256) for i in range(6))
            PB = [ar(17024 + i * 384, 384) for i in range(3)]
            PT = [ar(18176 + i * 384, 3, 128) for i in range(2)]
            O = ar(18944, 2, 1024)
            SQ = ar(23040, 512)
            ROT = [ar(23552 + 512 * i, 4, 4, 32) for i in range(2)]
            CB = ar(24576, CB_N)
            UQ, UKV = ar(25600, 2, 768), ar(27136, 1024)
            MX, SU = SM[:, 32:48], SM[:, 48:64]
            before = arena_read
            gn_tok = dma(GN, d["rows"][0:1, RW_MQ:RW_MQ + 640].to_broadcast([128, 640]), *before)
            cb_tok = dma(CB, d["cb"], *before)
            uq_tok = dma(UQ, d["l1_uq"].rearrange("p (k n) -> p k n", k=2), *before)
            ukv_tok = dma(UKV, d["l1_ukv"], *before)
            xn = norm_T(PV_MIX1, before)
            kv4 = KV.rearrange("p t (h c) -> p t h c", h=4)
            kc4 = KC.rearrange("p t (h c) -> p t h c", h=4)
            q8 = QC.rearrange("p t (h c) -> p t h c", h=4)
            ready, qk_tok = {}, {}

            def squares(ss, segs, *waits):
                for i, v in enumerate(segs):
                    r_ = act(SQ[:, 0:v.shape[-1]], v, ACT.Square, *waits, accum_out=ss[:, i:i + 1])
                return r_

            def scaled(outs, segs, ss, gain, r_, *waits):
                for i, (o, v) in enumerate(zip(outs, segs)):
                    r = op("V", lambda e, o=o, v=v, i=i: e.scalar_tensor_tensor(
                        out=o, in0=v, scalar=ss[:, i:i + 1], in1=gain, op0=ALU.mult, op1=ALU.mult), r_, *waits, loose=True)
                return r

            def heads_T(name, dst, src, w, tok):
                for kp in range(0, 4, 2):
                    b, wb = bank("side")
                    for j in range(2):
                        for t in range(2):
                            tp = mm(lambda e, b=b, j=j, t=t, kp=kp: e.transpose(
                                PS[0:w, b, j * 256 + t * 128:j * 256 + t * 128 + 128], src(t, kp + j), ident),
                                tok, *wb, mark=(j == 1 and t == 1))
                    free[b] = [evac(dst[0:w, kp:kp + 2, :], PS[0:w, b, :].rearrange("p (j t) -> p j t", j=2), tp)]
                    qk_tok.setdefault(name, []).append(free[b][0])

            def rotate(v, t, r, buf, k):
                x1, x2 = v[:, :, 0:32], v[:, :, 32:64]
                co, si = (TRIG[:, i, t, :].unsqueeze(1).to_broadcast([128, 4, 32]) for i in (1, 0))
                t1, t2, t3, t4 = (buf[:, i] for i in range(4))
                tt(t1, x1, co, ALU.mult, trig_tok[0], r, k=k)
                for o, a_, b_ in ((t2, x2, si), (t3, x2, co), (t4, x1, si)):
                    r = tt(o, a_, b_, ALU.mult, trig_tok[0], r, k=k, loose=True)
                tt(x1, t1, t2, ALU.subtract, r, k=k)
                return tt(x2, t3, t4, ALU.add, r, k=k)

            def low_rank():
                z_tok = [P.last("V"), P.last("A")]
                ssc, sso = SM[:, 24:28], SM[:, 28:30]
                segs = [Z[:, t, a:b] for a, b in ((0, 256), (256, 384)) for t in range(2)]
                for i, v in enumerate(segs):
                    r_ = act(SQ[:, 0:v.shape[-1]], v, ACT.Square, *z_tok, accum_out=ssc[:, i:i + 1])
                for t in range(2):
                    pe = act(SQ[:, 0:64], Z[:, t, 384:448], ACT.Square, *z_tok, accum_out=sso[:, t:t + 1])
                rstd(ssc[:, 0:2], 256, r_)
                r_ = rstd(ssc[:, 2:4], 128, r_)
                for i, v in enumerate(segs):
                    r = ts(v, v, ssc[:, i:i + 1], None, ALU.mult, None, r_, loose=True)
                yield
                cq = transposed(lambda k: CQT[:, k, :], lambda t, k: Z[:, t, k * 128:k * 128 + 128], [r],
                                gain=lambda k: PVT[:, PV_CQ + k:PV_CQ + k + 1], nk=2, pool="side")
                ck = transposed(lambda k: CKT[:, k, :], lambda t, k: Z[:, t, 256:384], [r],
                                gain=lambda k: PVT[:, PV_CKV:PV_CKV + 1], nk=1, pool="side")
                yield
                done = [None, None]
                for t in range(2):
                    for h in range(2):
                        b, wb = bank("side")
                        for k in range(2):
                            tok = mm(lambda e, b=b, t=t, h=h, k=k: e.matmul(
                                PS[:, b, 0:384], CQT[:, k, t * 128:t * 128 + 128],
                                UQ[:, k, h * 384:h * 384 + 384], start=(k == 0), stop=(k == 1)),
                                uq_tok, *cq, *wb, mark=(k == 1))
                        free[b] = [evac(QC[:, t, h * 384:h * 384 + 384], PS[:, b, 0:384], tok)]
                    for h in range(2):
                        b, wb = bank("side")
                        tok = mm(lambda e, b=b, t=t, h=h: e.matmul(
                            PS[:, b, :], CKT[:, 0, t * 128:t * 128 + 128], UKV[:, h * 512:h * 512 + 512],
                            start=True, stop=True), ukv_tok, *ck, *wb, mark=True)
                        free[b] = [evac(KV[:, t, h * 512:h * 512 + 512], PS[:, b, :], tok)]
                    done[t] = [P.last("V"), P.last("A")]
                    yield
                rot = {}
                for t in range(2):
                    sq, sk = SM[:, 64 + 8 * t:68 + 8 * t], SM[:, 68 + 8 * t:72 + 8 * t]
                    squares(sk, [kv4[:, t, h, 0:128] for h in range(4)], *done[t])
                    r_ = squares(sq, [q8[:, t, h, :] for h in range(4)], *done[t])
                    r_ = ts(sk, sk, sso[:, t:t + 1], None, ALU.add, None, r_)
                    r_ = rstd(SM[:, 64 + 8 * t:72 + 8 * t], 192, r_)
                    yield
                    k_ = scaled([kc4[:, t, h, 128:192] for h in range(4)], [Z[:, t, 384:448]] * 4, sk, GN[:, 320:384], r_, gn_tok)
                    rot[1, t] = rotate(kc4[:, t, :, 128:192], t, k_, ROT[1], "G")
                    q_ = scaled([q8[:, t, h, :] for h in range(4)], [q8[:, t, h, :] for h in range(4)], sq, GN[:, 0:192], r_, gn_tok)
                    yield
                    k_ = scaled([kc4[:, t, h, 0:128] for h in range(4)], [kv4[:, t, h, 0:128] for h in range(4)], sk,
                                GN[:, 192:320], r_, gn_tok)
                    rot[0, t] = rotate(q8[:, t, :, 128:192], t, q_, ROT[0], "V")
                    yield
                heads_T("mla", QN, lambda t, k: q8[:, t, k, 0:128], 128, k_)
                heads_T("mla", KN, lambda t, k: kc4[:, t, k, 0:128], 128, k_)
                yield
                heads_T("mla", QR, lambda t, k: q8[:, t, k, 128:192], 64, rot[0, 1])
                heads_T("mla", KR, lambda t, k: kc4[:, t, k, 128:192], 64, rot[1, 1])
                yield

            def moba():
                for n, (o, g, dst) in enumerate(((512, GN[:, 384:512], QD), (1024, GN[:, 512:640], KD))):
                    while n + 1 not in ready:
                        yield
                    for t in range(2):
                        segs = [Z[:, t, o + h * 128:o + h * 128 + 128] for h in range(4)]
                        ss = SM[:, 80 + 8 * n + 4 * t:84 + 8 * n + 4 * t]
                        r_ = rstd(ss, 128, squares(ss, segs, *ready[n + 1]))
                        yield
                        r = scaled(segs, segs, ss, g, r_, gn_tok)
                        yield
                    heads_T("moba", dst, lambda t, k, o=o: Z[:, t, o + k * 128:o + 128 + k * 128], 128, r)
                    yield

            def use(nb, t, ps, tok):
                r = evac(Z[:, t, nb * 512:nb * 512 + 512], ps, tok)
                if t == 1:
                    ready[nb] = [P.last("V"), P.last("A")]
                return r
            proj_nat("l1_win", 0, xn, 8, 1, use)
            low, mob = low_rank(), moba()

            def both():
                while next(low, 0) != 0:
                    yield
                    next(mob, 0)
            side = both()
            proj_nat("l1_win", 0, xn, 8, 3, lambda nb, t, ps, tok: use(nb + 1, t, ps, tok), c0=4, side=side)
            drain(side)

            mask = CB[:, CB_M:CB_M + 384]

            def parts(h):
                if h < 4:
                    return [(QN[:, h], KN[:, h]), (QR[0:64, h], KR[0:64, h])], 192 ** -0.5
                return [(QD[:, h - 4], KD[:, h - 4])], 128 ** -0.5

            def values(h, t):
                if h < 4:
                    return KV[:, t, h * 256 + 128:h * 256 + 256]
                return Z[:, t, 1536 + (h - 4) * 128:1536 + (h - 4) * 128 + 128]
            hd = {}
            pt_read = [None, None]

            def scores(h):
                pp, scale = parts(h)
                b, wb = bank("side")
                for t in range(2):
                    o = PS[:, b, 0:128] if t == 0 else PS[:, b, 128:384]
                    for i, (q, k) in enumerate(pp):
                        tok = mm(lambda e, o=o, q=q, k=k, t=t, i=i: e.matmul(
                            o, q[:, t * 128:t * 128 + 128], k[:, 0:128 * (t + 1)], start=(i == 0),
                            stop=(i == len(pp) - 1)), *qk_tok["mla" if h < 4 else "moba"], *wb, mark=True)
                p = PB[h % 3]
                mx, su = MX[:, 2 * h:2 * h + 2], SU[:, 2 * h:2 * h + 2]
                free[b] = [stt(p, PS[:, b, 0:384], float(scale), mask, ALU.mult, ALU.add, tok, cb_tok,
                               hd[h - 3]["tr"] if h >= 3 else None)]
                op("V", lambda e: e.tensor_reduce(mx[:, 0:1], p[:, 0:128], AX, ALU.max, negate=True))
                mt = op("V", lambda e: e.tensor_reduce(mx[:, 1:2], p[:, 128:384], AX, ALU.max, negate=True), loose=True)
                act(p[:, 0:128], p[:, 0:128], ACT.Exp, mt, bias=mx[:, 0:1], accum_out=su[:, 0:1])
                et = act(p[:, 128:384], p[:, 128:384], ACT.Exp, mt, bias=mx[:, 1:2], accum_out=su[:, 1:2], loose=True)
                hd[h] = {"p": p, "e": et}

            def turn_p(h):
                b, wb = bank("side")
                for i in range(3):
                    tok = mm(lambda e, i=i, b=b, h=h: e.transpose(PS[:, b, i * 128:i * 128 + 128],
                                                                  PB[h % 3][:, i * 128:i * 128 + 128], ident),
                             hd[h]["e"], *wb, mark=(i == 2))
                hd[h]["tr"] = tok
                free[b] = [evac(PT[h % 2], PS[:, b, 0:384].rearrange("p (i q) -> p i q", i=3), tok, pt_read[h % 2])]
                hd[h]["pt"] = free[b][0]

            def weigh(h):
                b, wb = bank("side")
                pt, su = PT[h % 2], SU[:, 2 * h:2 * h + 2]
                rt = op("V", lambda e: e.reciprocal(su, su), hd[h]["e"])
                mm(lambda e: e.matmul(PS[:, b, 0:128], pt[:, 0, :], values(h, 0), start=True, stop=True),
                   hd[h]["pt"], *wb)
                mm(lambda e: e.matmul(PS[:, b, 128:256], pt[:, 1, :], values(h, 0), start=True, stop=False))
                tok = mm(lambda e: e.matmul(PS[:, b, 128:256], pt[:, 2, :], values(h, 1), start=False, stop=True), mark=True)
                pt_read[h % 2] = tok
                for t in range(2):
                    free[b] = [evac(O[:, t, h * 128:h * 128 + 128], PS[:, b, t * 128:t * 128 + 128], tok, rt,
                                    scale=SU[:, 2 * h + t:2 * h + t + 1], eng="VA"[h % 2])]

            def attention():
                for i in range(10):
                    if i < 8:
                        scores(i)
                    if 1 <= i < 9:
                        turn_p(i - 1)
                    if i >= 2:
                        weigh(i - 2)
                    if i == 5:
                        ready["o"] = [P.last("V"), P.last("A")]
                    yield
            side = attention()
            table(ACT.Exp)
            for i in range(4):
                pump(side)
                pump(mob, 2)
            drain(mob)
            pump(side, 2)
            part = transposed_split(lambda t, k: O[:, t, k * 128:k * 128 + 128], ready["o"], pairs=(0, 1), pool="side")
            out_proj("l1_wout", (0, 1), part, side=side)
            drain(side)
            part = transposed_split(lambda t, k: O[:, t, k * 128:k * 128 + 128], [P.last("V"), P.last("A")],
                                    pairs=(2, 3), pool="side")
            arena_read[:] = [P.last("V"), P.last("A"), P.last("G")]
            table(ACT.Sqrt)
            out_proj("l1_wout", (2, 3), part)

        def rel_table(before):
            OHB, NG, RB, R = ar(28160, 512), ar(28672, 512), ar(29184, 24), ar(29312, 512)
            a = dma(AR[0:32, 28160:29184], d["cd"], *before)
            r = dma(AR[0:32, 29184:29208], d["rel"], *before)
            for _ in range(8):
                yield
            b, wb = bank("side")
            tok = mm(lambda e: e.matmul(PS[0:24, b, 0:511], RB[0:32, :], OHB[0:32, 0:511], start=True, stop=True),
                     a, r, *wb, mark=True)
            free[b] = [tt(R[0:24, 0:511], PS[0:24, b, 0:511], NG[0:24, 0:511], ALU.add, tok, a)]
            rel_tok[0] = dma(scr[:, 0:511], R[0:24, 0:511], free[b][0])

        def block2():
            QT, KT = ar(0, 12, 256), ar(3072, 12, 256)
            VN = ar(6144, 2, 1536)
            AI, SAG, BGT = ar(9216, 2, 512), ar(10240, 4, 256), ar(11264, 4, 256)
            GT = ar(12288, 16, 256)
            SK = ar(16384, 24, 384)
            PG = ar(25600, 2, 1024)
            SB = [ar(27648 + 768 * i, 768) for i in range(3)]
            PT = [ar(29952 + 768 * i, 768) for i in range(2)]
            WP = ar(31488, 4, 128)
            PT4 = ar(27648, 4, 256)
            MIX = ar(9216, 4, 256)
            ATT = ar(25600, 2, 512)
            MG, YB, FG, SQ = ar(0, 8, 256), ar(2048, 2, 256), ar(3072, 1024), ar(4096, 2, 1024)
            before = everything()
            pg_tok = dma(AR[:, 25600:27648], d["cc"], *before)
            wp_tok = dma(WP, d["wpool"].rearrange("p (g t) -> p g t", g=4), *before)
            sk_tok = dma(SK, bass.AP(scr, 0, [[1, 128], [512, 24], [1, 384]]), *before, rel_tok[0])
            xn = norm_T(PV_MIX2, arena_read, 0)

            proj_nat("w2_a", 0, xn, 8, 1, lambda nb, t, ps, tok: evac(AI[:, t, :], ps, tok))

            def pooling():
                a_tok = [P.last("V"), P.last("A")]
                for g in range(0, 4, 2):
                    b, wb = bank("side")
                    for j in range(2):
                        for t in range(2):
                            tok = mm(lambda e, b=b, j=j, t=t, g=g: e.matmul(
                                PS[:, b, j * 256:j * 256 + 256], AI[:, t, (g + j) * 128:(g + j) * 128 + 128],
                                PG[:, t, (g + j) * 256:(g + j) * 256 + 256], start=(t == 0), stop=(t == 1)),
                                pg_tok, *a_tok, *wb, mark=(j == 1 and t == 1))
                    free[b] = [evac(PT4[:, g:g + 2, :], PS[:, b, :].rearrange("p (j t) -> p j t", j=2), tok, eng="V")]
                yield
                yield
                p_tok = P.last("V")
                for g in range(0, 4, 2):
                    b, wb = bank("side")
                    for j in range(2):
                        tok = mm(lambda e, b=b, j=j, g=g: e.matmul(
                            PS[:, b, j * 256:j * 256 + 256], WP[:, g + j, :], PT4[:, g + j, :], start=True, stop=True),
                            p_tok, wp_tok, *wb, mark=(j == 1))
                    free[b] = [evac(MIX[:, g:g + 2, :], PS[:, b, :].rearrange("p (j t) -> p j t", j=2), tok, eng="V")]
                pool_read[0] = P.last("T")
                yield
            pool_read = [None]
            side = pooling()

            def use_qk(blk, ps, tok):
                if blk < 12:
                    return evac(QT[:, blk, :].rearrange("p (t q) -> p t q", t=2),
                                ps.rearrange("p (t q) -> p t q", t=2)[:, :, ::-1], tok, eng="V")
                return evac(KT[:, blk - 12, :], ps, tok, eng="A")
            proj_T("w2_qk", 0, xn, 8, 12, use_qk, side=side)
            drain(side)
            z_tok = [P.last("V"), P.last("A")]
            v_tok = []

            def use_v(nb, t, ps, tok):
                return evac(VN[:, t, nb * 512:nb * 512 + 512], ps, tok)
            proj_nat("w2_v", 0, xn, 8, 2, use_v)

            hd = {}
            pt_read = [None, None]
            pair = [0]

            def two_banks():
                b = 4 + 2 * (pair[0] % 2)
                pair[0] += 1
                return b, [*free[b], *free[b + 1]]
            MX, SU = SM[:, 80:96], SM[:, 96:112]

            def scores(i):
                h, t = divmod(i, 2)
                b, wb = two_banks()
                sp = PS[:, b:b + 2, :].rearrange("p a n -> p (a n)")[:, 0:768]
                pb = (h % 2) * 64
                for g in range(3):
                    nb = g * 4 + h // 2
                    tok = mm(lambda e, g=g, nb=nb, sp=sp: e.matmul(
                        sp[:, g * 256:g * 256 + 256], QT[pb:pb + 64, nb, t * 128:t * 128 + 128],
                        KT[pb:pb + 64, nb, :], start=True, stop=True), *z_tok, *wb, mark=(g == 2))
                s_ = SB[i % 3]
                sk = SK.rearrange("p (g h) j -> p g h j", g=3)[:, :, h, 128 * (1 - t):128 * (1 - t) + 256]
                r = stt(s_.rearrange("p (g k) -> p g k", g=3), sp.rearrange("p (g k) -> p g k", g=3), 0.125, sk,
                        ALU.mult, ALU.add, tok, sk_tok, pool_read[0], hd[i - 3]["tr"] if i >= 3 else None)
                free[b], free[b + 1] = [r], [r]
                mx = MX[:, i:i + 1]
                mt = op("V", lambda e: e.tensor_reduce(mx, s_, AX, ALU.max, negate=True))
                et = act(s_, s_, ACT.Exp, mt, bias=mx, accum_out=SU[:, i:i + 1])
                hd[i] = {"e": et}

            def turn_p(i):
                b, wb = two_banks()
                sp = PS[:, b:b + 2, :].rearrange("p a n -> p (a n)")[:, 0:768]
                for j in range(6):
                    tok = mm(lambda e, j=j, sp=sp: e.transpose(sp[:, j * 128:j * 128 + 128],
                                                               SB[i % 3][:, j * 128:j * 128 + 128], ident),
                             hd[i]["e"], *wb, mark=(j == 5))
                hd[i]["tr"] = tok
                r = evac(PT[i % 2], sp, tok, pt_read[i % 2], eng="A")
                free[b], free[b + 1] = [r], [r]
                hd[i]["pt"] = r
                hd[i]["r"] = op("V", lambda e: e.reciprocal(SU[:, i:i + 1], SU[:, i:i + 1]), hd[i]["e"])

            def weigh(i):
                h, t = divmod(i, 2)
                b, wb = two_banks()
                for j in range(6):
                    g, kt = divmod(j, 2)
                    tok = mm(lambda e, j=j, g=g, kt=kt: e.matmul(
                        PS[:, b, 0:64], PT[i % 2][:, j * 128:j * 128 + 128],
                        VN[:, kt, g * 512 + h * 64:g * 512 + h * 64 + 64], start=(j == 0), stop=(j == 5)),
                        hd[i]["pt"], *wb, *v_tok, mark=(j == 5))
                pt_read[i % 2] = tok
                r = evac(ATT[:, t, h * 64:h * 64 + 64], PS[:, b, 0:64], tok, hd[i]["r"], scale=SU[:, i:i + 1], eng="V")
                free[b], free[b + 1] = [r], [r]

            def attention():
                for i in range(18):
                    if i >= 2:
                        weigh(i - 2)
                    if 1 <= i < 17:
                        turn_p(i - 1)
                    if i < 16:
                        scores(i)
                    yield

            def att_T():
                ready["exp"] = True
                n = len(raw)
                sb_tok = act(AR[:, 10240:12288], AR[:, 10240:12288], ACT.Silu, *raw[7])
                for g in range(4):
                    ready["mix"] = stt(MIX[:, g, :], MIX[:, g, :], PVT[:, PV_PS + g:PV_PS + g + 1], SAG[:, g, :],
                                       ALU.mult, ALU.mult, sb_tok)
                yield
                att = P.last("V")
                for nb in range(0, 4, 2):
                    b, wb = bank("side")
                    for j in range(2):
                        for t in range(2):
                            tok = mm(lambda e, b=b, j=j, t=t, nb=nb: e.transpose(
                                PS[:, b, j * 256 + t * 128:j * 256 + t * 128 + 128],
                                ATT[:, t, (nb + j) * 128:(nb + j) * 128 + 128], ident), att, *wb,
                                mark=(j == 1 and t == 1))
                    v = BGT[:, nb:nb + 2, :].rearrange("p j (t q) -> p (j t) q", t=2)
                    ready[nb] = tt(v, PS[:, b, :].rearrange("p (j q) -> p j q", j=4)[:, :, ::-1], v, ALU.mult, tok, sb_tok)
                    free[b] = [ready[nb]]
                yield
                for j in range(8, n):
                    ready["gt"] = act(GT[:, j - 8, :], GT[:, j - 8, :], ACT.Sigmoid, *raw[j])
                    if j % 2:
                        yield
            raw, ready = [], {}

            def use_gates(blk, ps, tok):
                if "exp" in ready and blk >= len(raw):
                    ready["gt"] = act(GT[:, blk - 8, :], ps, ACT.Sigmoid, tok, bias=PVT[:, PV_BG + blk - 8:PV_BG + blk - 7])
                    return ready["gt"]
                if blk < 8:
                    r = evac((SAG if blk < 4 else BGT)[:, blk % 4, :], ps, tok)
                else:
                    bg = PVT[:, PV_BG + blk - 8:PV_BG + blk - 7]
                    r = (ts(GT[:, blk - 8, :], ps, bg, None, ALU.add, None, tok) if turn_engine() == "V" else
                         act(GT[:, blk - 8, :], ps, ACT.Identity, tok, bias=bg))
                raw.append((P.last("V"), P.last("A")))
                return r

            def chain():
                yield from attention()
                yield from att_T()
            side = chain()
            proj_nat("w2_v", 0, xn, 8, 1, lambda nb, t, ps, tok: use_v(2, t, ps, tok), c0=8,
                     side=(next(side) for _ in range(2)))
            v_tok[:] = [P.last("V"), P.last("A")]
            proj_T("w2_gates", 0, xn, 8, 12, use_gates, side=side)
            drain(side)
            gt_tok = ready["gt"]
            xn_read = P.last("T")

            def parts(k, v, *waits):
                ht = act(XH[:, k:k + 2, :], v, ACT.Copy, *waits)
                return tt(XL[:, k:k + 2, :], v, XH[:, k:k + 2, :], ALU.subtract, ht, loose=True)
            ya_tok = [parts(k, MIX[:, k:k + 2, :], ready["mix"], xn_read) for k in (0, 2)]
            bt_tok = [None, None] + [parts(4 + nb, BGT[:, nb:nb + 2, :], ready[nb], xn_read) for nb in (0, 2)]

            fg_tok = dma(FG, d["rows"][0:1, RW_FG:RW_FG + 1024].to_broadcast([128, 1024]), *everything())
            mg_free, mg_tok = P.last("T"), {}

            def use_a(blk, ps, tok):
                return tt(MG[:, blk, :], ps, GT[:, blk, :], ALU.mult, tok, gt_tok, mg_free)

            def use_b(blk, ps, tok):
                r_ = tt(YB[:, blk % 2, :], ps, GT[:, 8 + blk, :], ALU.mult, tok, mg_free)
                mg_tok[blk] = tt(MG[:, blk, :], MG[:, blk, :], YB[:, blk % 2, :], ALU.add)
                if blk in (1, 3):
                    o_tok[blk // 2] = parts(blk - 1, MG[:, blk - 1:blk + 1, :], mg_tok[blk], a_read)
                return r_
            proj_T("w_pa", 0, ya_tok, 4, 4, use_a)
            a_read, o_tok = P.last("T"), [None] * 4
            proj_T("w_pb", 4, bt_tok, 4, 4, use_b)
            b_read = P.last("T")
            for k in (4, 6):
                o_tok[k // 2] = parts(k, MG[:, k:k + 2, :], mg_tok[k + 1], b_read)
            m_tok = P.last("V")
            table(ACT.Sqrt)
            out_proj("w_out2", range(4), o_tok)

            o_tok = []
            for t, r in norm_X(SQ, [m_tok]):
                y = stt(X[:, t, :], X[:, t, :], SM[:, 4 + t:5 + t], FG, ALU.mult, ALU.mult, fg_tok, r)
                o_tok.append(dma(out[t * 128:t * 128 + 128, :], X[:, t, :], y))
            P.wait("S", *o_tok)

        rel_tok = [None]
        stages = [mixer0, lambda: peer(0), mixer1, lambda: peer(1), block2]
        for st in stages[:upto]:
            st()
        if upto < 5:
            P.wait("S", dma(out.rearrange("(t p) c -> p t c", p=128), X[:, :, :], *everything()), rel_tok[0])

        block = ctx.enter_context(nc.Block())

        @block.sync
        def _(eng):
            P.emit("S", eng)

        @block.gpsimd
        def _(eng):
            P.emit("G", eng)

        @block.scalar
        def _(eng):
            P.emit("A", eng)

        @block.tensor
        def _(eng):
            P.emit("T", eng)

        @block.vector
        def _(eng):
            P.emit("V", eng)


def _constants():
    p = np.arange(128)
    cst = np.zeros((128, C_N0), np.float32)
    cst[:, C_ID:C_ID + 128] = np.eye(128)
    cst[:, C_IOTA:C_IOTA + 128] = p[None, :]
    cst[:, C_ONE] = 1
    ca = np.zeros((128, CA_N), np.float32)
    s, t = p[:, None], p[None, :]
    for lv in range(8):
        m = s == t if lv == 0 else (s >> lv == t >> lv) & ((s >> (lv - 1)) & 1 == 0) & ((t >> (lv - 1)) & 1 == 1)
        ca[:, CA_LV + lv * 128:CA_LV + lv * 128 + 128] = m
    ca[:, CA_TRI:CA_TRI + 128] = s <= t
    cb = np.zeros((128, CB_N), np.float32)
    tri = np.where(t <= s, 0, NBIG)
    cb[:, CB_M:CB_M + 128] = tri
    cb[:, CB_M + 256:CB_M + 384] = tri
    cb[:, CB_INV:CB_INV + 32] = (np.float32(10000.0) ** (-np.arange(32, dtype=np.float32) / np.float32(32)))[None, :]
    pool = np.zeros((256, 4, 256), np.float32)
    for g, w in enumerate((2, 4, 8, 16)):
        for q in range(256):
            lo, hi = max(q - w // 2, 0), min(q + w // 2 - 1, 255)
            pool[lo:hi + 1, g, q] = np.float32(1) / np.float32(hi - lo + 1)
            pool[q, g, q] -= 1
    cc = pool.reshape(2, 128, 4, 256).transpose(1, 0, 2, 3).reshape(128, 2048)
    cd = np.zeros((32, CD_N), np.float32)
    rel = np.arange(511) - 255
    n = np.abs(rel)
    large = 8 + (np.log(np.maximum(n, 1).astype(np.float32) / np.float32(8)) / np.float32(np.log(128.0))
                 * np.float32(8)).astype(np.int32)
    bucket = (rel > 0) * 16 + np.where(n < 8, n, np.minimum(large, 15))
    cd[bucket, CD_OH + np.arange(511)] = 1
    for g, dil in enumerate((1, 4, 16)):
        bad = (rel % dil != 0) | (n > 64 * dil)
        cd[g * 8:g * 8 + 8, CD_NG:CD_NG + 511] = np.where(bad, NBIG, 0)[None, :]
    return dict(cst=cst, ca=ca, cb=cb, cc=np.ascontiguousarray(cc), cd=cd)


def _layout(i):
    def cols(v):
        return v.reshape(-1, 128).T

    def chunks(w, k, n):
        r, c = w.shape[0] // (128 * k), w.shape[1] // n
        return np.ascontiguousarray(
            w.reshape(r, k, 128, c, n).transpose(3, 0, 2, 1, 4).reshape(c * r, 128, k * n))
    a = _constants()
    a["x"] = np.ascontiguousarray(i["x"][0])
    a["pos"] = np.ascontiguousarray(i["positions"].reshape(2, 128).T.astype(np.int32))
    lb = i["lb_logits"].reshape(3, 4, 128).transpose(2, 0, 1).reshape(128, 12)
    a["pv"] = np.ascontiguousarray(np.concatenate(
        [cols(i[n]) for n in ("l0_norm_mix", "l0_norm_ffn", "l1_norm_mix", "l1_norm_ffn")]
        + [cols(i["norm_gain_2"][0]), cols(i["l1_mla_cq_norm"]), cols(i["l1_mla_ckv_norm"]), lb,
           i["l0_gmlp_b_s"].T, cols(i["pool_scale_2"][0]), cols(i["b_gate_2"][0].reshape(-1))], axis=1))
    a["rows"] = np.concatenate([i[n].reshape(1, -1) for n in (
        "l0_hgrn_out_norm", "l0_gmlp_v_norm", "l1_mla_q_norm", "l1_mla_k_norm", "l1_moba_q_norm", "l1_moba_k_norm",
        "final_gain_2")], axis=1)
    a["gw"] = np.ascontiguousarray(i["l0_gmlp_w_s"].transpose(2, 0, 1).reshape(128, 512))
    nat, trn = (2, 512), (4, 256)
    w = i["l0_w_in"]
    a["l0_qf"] = chunks(np.concatenate([w[:, 512:1024], w[:, :512]], axis=1), *trn)
    a["l0_nat"] = chunks(np.concatenate([w[:, 2560:], w[:, 2048:2560], w[:, 1024:2048]], axis=1), *nat)
    a["l0_wout"] = chunks(i["l0_w_out"], *nat)
    w = i["l1_w_in"]
    a["l1_win"] = chunks(np.concatenate([w[:, :448], np.zeros((1024, 64), w.dtype), w[:, 448:]], axis=1), *nat)
    a["l1_uq"] = np.ascontiguousarray(i["l1_mla_w_uq"].reshape(2, 128, 768).transpose(1, 0, 2).reshape(128, 1536))
    a["l1_ukv"] = np.ascontiguousarray(i["l1_mla_w_ukv"])
    a["l1_wout"] = chunks(i["l1_w_out"], *nat)
    for l in (0, 1):
        n = f"l{l}_"
        a[n + "wq"] = chunks(i[n + "peer_w_query"], *trn)
        a[n + "keys"] = np.ascontiguousarray(
            i[n + "peer_sub_keys"].reshape(16, 128, 128).transpose(2, 0, 1).reshape(128, 2048))
        a[n + "down"] = np.ascontiguousarray(
            i[n + "peer_expert_down"].reshape(128, 128, 8, 128).transpose(0, 3, 2, 1).reshape(128, 128, 1024))
        a[n + "up"] = np.ascontiguousarray(i[n + "peer_expert_up"].reshape(128, 128, 1024))
    w = i["w_in_2"][0]
    a["w2_a"] = chunks(w[:, :512], *nat)
    a["w2_qk"] = chunks(w[:, 1024:4096], *trn)
    a["w2_v"] = chunks(w[:, 4096:5632], *nat)
    a["w2_gates"] = chunks(np.concatenate([w[:, 512:1024], w[:, 5632:]], axis=1), *trn)
    a["rel"] = np.ascontiguousarray(i["rel_bias_2"])
    a["wpool"] = np.ascontiguousarray(i["w_pool_2"][0].transpose(1, 0, 2).reshape(128, 512))
    a["w_pa"] = chunks(i["w_proj_a_2"][0], *trn)
    a["w_pb"] = chunks(i["w_proj_b_2"][0], *trn)
    a["w_out2"] = chunks(i["w_out_2"][0], *nat)
    return a


def kernel(**inputs):
    import numpy as _np
    import concourse.bacc as _bacc
    from concourse import mybir as _mybir
    from concourse.bass_utils import run_bass_kernel_spmd as _run

    nc = _bacc.Bacc("TRN2", target_bir_lowering=False, num_devices=1, dynamic_dma_scratch_size=1024)
    arrays, args = {}, {}
    for name, a in _layout({k: _np.asarray(v) for k, v in inputs.items()}).items():
        arrays[f"in_{name}_dram"] = a
        args[name] = nc.dram_tensor(f"in_{name}_dram", a.shape, _mybir.dt.from_np(a.dtype), kind="ExternalInput").ap()
    out = nc.dram_tensor("out_0_dram", (256, 1024), _mybir.dt.float32, kind="ExternalOutput").ap()
    build(nc, args, out)
    r = _run(nc, [arrays], core_ids=[0])
    return r.results[0]["out_0_dram"].reshape(1, 256, 1024)
```
